# Optimizing a Trainium2 kernel written in Bass

```python
import jax, jax.numpy as jnp
from jax import lax
import numpy as np
import jax
import jax.numpy as jnp
import math

D_MODEL = 1024
BATCH = 1
SEQ = 256
DEPTH = 1

GRID_W = 64
CTX_LEN = 256

HEAD_DIM = 64
N_HEADS = 16
N_KV_HEADS = 4
GROUP = N_HEADS // N_KV_HEADS
ATTN_W = N_HEADS * HEAD_DIM
KV_W = N_KV_HEADS * HEAD_DIM
WINDOW = 128
ATTN_BLOCK = 128
ATTN_SCALE = HEAD_DIM ** -0.5
ROPE_BASE = 10000.0
ROPE_PAIRS = HEAD_DIM // 4

POOL_WINDOWS = (2, 4, 8, 16)
N_POOL_GROUPS = len(POOL_WINDOWS)
POOL_W = D_MODEL
POOL_GROUP_W = POOL_W // N_POOL_GROUPS

IN_W = ATTN_W + 2 * KV_W + POOL_W + 2 * D_MODEL
SPLIT_POINTS = (ATTN_W, ATTN_W + KV_W, ATTN_W + 2 * KV_W,
                ATTN_W + 2 * KV_W + POOL_W, ATTN_W + 2 * KV_W + POOL_W + D_MODEL)

N_EXPERTS = 32
TOP_K = 4
D_FF = D_MODEL
SWIGLU_ALPHA = 1.702
SWIGLU_LIMIT = 7.0
EXPERT_BLOCK = 128

NORM_EPS = 1e-5
NEG_INF = -1e30


def rmsnorm(x, g):
    xf = x.astype(jnp.float32)
    y = xf * lax.rsqrt(jnp.mean(xf * xf, axis=-1, keepdims=True) + NORM_EPS)
    return (y * g.astype(jnp.float32)).astype(x.dtype)

def modulate(h, shift, scale):
    return h * (1 + scale) + shift

def apply_axial_rope(t, cos, sin):
    B, L, H, _ = t.shape
    tr = t.reshape(B, L, H, 2, 2, ROPE_PAIRS)
    t1, t2 = tr[..., 0, :], tr[..., 1, :]
    cs = cos[None, :, None].astype(t.dtype)
    sn = sin[None, :, None].astype(t.dtype)
    out = jnp.stack([t1 * cs - t2 * sn, t2 * cs + t1 * sn], axis=-2)
    return out.reshape(t.shape)

def windowed_attention(q, k, v, k_ctx, v_ctx, sink):
    B, L = q.shape[:2]
    Lc = k_ctx.shape[1]
    nblk = L // ATTN_BLOCK
    qb = q.reshape(B, nblk, ATTN_BLOCK, N_KV_HEADS, GROUP, HEAD_DIM).transpose(1, 0, 2, 3, 4, 5)
    pad = ((0, 0), (ATTN_BLOCK, ATTN_BLOCK), (0, 0), (0, 0))

    def band(t):
        tp = jnp.pad(t, pad).reshape(B, nblk + 2, ATTN_BLOCK, N_KV_HEADS, HEAD_DIM)
        tb = jnp.concatenate([tp[:, :-2], tp[:, 1:-1], tp[:, 2:]], axis=2)
        return tb.transpose(1, 0, 2, 3, 4)

    k_band, v_band = band(k), band(v)
    sink_l = sink.reshape(N_KV_HEADS, GROUP).astype(jnp.float32)
    q_off = jnp.arange(ATTN_BLOCK, dtype=jnp.int32)
    k_off = jnp.arange(3 * ATTN_BLOCK, dtype=jnp.int32) - ATTN_BLOCK
    n_loc = 3 * ATTN_BLOCK

    def one_block(args):
        qn, kn, vn, n = args
        s_loc = jnp.einsum('bqhgd,bshd->bhgqs', qn, kn).astype(jnp.float32) * ATTN_SCALE
        s_ctx = jnp.einsum('bqhgd,bchd->bhgqc', qn, k_ctx).astype(jnp.float32) * ATTN_SCALE
        qpos = n * ATTN_BLOCK + q_off
        kpos = n * ATTN_BLOCK + k_off
        valid = ((jnp.abs(qpos[:, None] - kpos[None, :]) <= WINDOW)
                 & (kpos[None, :] >= 0) & (kpos[None, :] < L))
        s_loc = jnp.where(valid, s_loc, NEG_INF)
        sink_b = jnp.broadcast_to(sink_l[None, :, :, None, None], s_loc.shape[:-1] + (1,))
        probs = jax.nn.softmax(jnp.concatenate([s_loc, s_ctx, sink_b], axis=-1), axis=-1)
        p_loc = probs[..., :n_loc].astype(vn.dtype)
        p_ctx = probs[..., n_loc:n_loc + Lc].astype(v_ctx.dtype)
        return (jnp.einsum('bhgqs,bshd->bqhgd', p_loc, vn)
                + jnp.einsum('bhgqc,bchd->bqhgd', p_ctx, v_ctx))

    out = lax.map(one_block, (qb, k_band, v_band, jnp.arange(nblk, dtype=jnp.int32)))
    return out.transpose(1, 0, 2, 3, 4, 5).reshape(B, L, ATTN_W)

def context_attention(q, k, v, sink):
    B, Lc = q.shape[:2]
    qg = q.reshape(B, Lc, N_KV_HEADS, GROUP, HEAD_DIM)
    s = jnp.einsum('bqhgd,bchd->bhgqc', qg, k).astype(jnp.float32) * ATTN_SCALE
    sink_b = jnp.broadcast_to(
        sink.reshape(N_KV_HEADS, GROUP).astype(jnp.float32)[None, :, :, None, None],
        s.shape[:-1] + (1,))
    p = jax.nn.softmax(jnp.concatenate([s, sink_b], axis=-1), axis=-1)[..., :Lc].astype(v.dtype)
    return jnp.einsum('bhgqc,bchd->bqhgd', p, v).reshape(B, Lc, ATTN_W)

def multiscale_pool(u, w_pool, pool_scale):
    B, L, _ = u.shape
    ug = u.reshape(B, L, N_POOL_GROUPS, POOL_GROUP_W).astype(jnp.float32)
    cs = jnp.concatenate([jnp.zeros_like(ug[:, :1]), jnp.cumsum(ug, axis=1)], axis=1)
    half = jnp.array([w // 2 for w in POOL_WINDOWS], dtype=jnp.int32)
    t = jnp.arange(L, dtype=jnp.int32)[:, None]
    lo = jnp.clip(t - half[None, :], 0, L)
    hi = jnp.clip(t + half[None, :], 0, L)
    g = jnp.arange(N_POOL_GROUPS, dtype=jnp.int32)[None, :]
    window_sum = cs[:, hi, g] - cs[:, lo, g]
    mean = window_sum / (hi - lo).astype(jnp.float32)[None, :, :, None]
    diff = (mean - ug).astype(u.dtype)
    mixed = jnp.einsum('blgc,gcd->blgd', diff, w_pool)
    return mixed.reshape(B, L, POOL_W) * pool_scale

def merge_branches(attn_o, pool_o, g_attn, g_pool, w_attn_br, w_pool_br, w_out):
    merged = (jax.nn.sigmoid(g_attn) * (attn_o @ w_attn_br)
              + jax.nn.sigmoid(g_pool) * (pool_o @ w_pool_br))
    return merged @ w_out

def clamped_swiglu(gu):
    gate = jnp.minimum(gu[..., :D_FF], SWIGLU_LIMIT)
    lin = jnp.clip(gu[..., D_FF:], -SWIGLU_LIMIT, SWIGLU_LIMIT)
    return gate * jax.nn.sigmoid(SWIGLU_ALPHA * gate) * (lin + 1)

def moe_ffn(h, w_router, b_router, w_gu, b_gu, w_down, b_down):
    N, D = h.shape
    logits = (h @ w_router + b_router).astype(jnp.float32)
    top_val, top_idx = lax.top_k(logits, TOP_K)
    gate_w = jax.nn.softmax(top_val, axis=-1).astype(h.dtype)
    NK = N * TOP_K
    flat_e = top_idx.reshape(-1)
    order = jnp.argsort(flat_e)
    sorted_e = flat_e[order]
    tok_sorted = (order // TOP_K).astype(jnp.int32)
    counts = jnp.zeros((N_EXPERTS,), jnp.int32).at[flat_e].add(1)
    padded = (counts + EXPERT_BLOCK - 1) // EXPERT_BLOCK * EXPERT_BLOCK
    start = jnp.cumsum(counts) - counts
    pend = jnp.cumsum(padded)
    pstart = pend - padded
    dest = pstart[sorted_e] + (jnp.arange(NK, dtype=jnp.int32) - start[sorted_e])
    num_blocks = -(-NK // EXPERT_BLOCK) + N_EXPERTS
    P = num_blocks * EXPERT_BLOCK
    tok_buf = jnp.full((P,), N, jnp.int32).at[dest].set(tok_sorted)
    h_pad = jnp.concatenate([h, jnp.zeros((1, D), h.dtype)], axis=0)
    x_blocks = h_pad[tok_buf].reshape(num_blocks, EXPERT_BLOCK, D)
    block_start = jnp.arange(num_blocks, dtype=jnp.int32) * EXPERT_BLOCK
    block_e = jnp.minimum(jnp.searchsorted(pend, block_start, side='right'), N_EXPERTS - 1)

    def expert_block(args):
        xb, e = args
        gu = xb @ w_gu[e] + b_gu[e]
        return clamped_swiglu(gu) @ w_down[e] + b_down[e]

    y_buf = lax.map(expert_block, (x_blocks, block_e)).reshape(P, D)
    y_sorted = y_buf[dest] * gate_w.reshape(-1)[order][:, None]
    return jax.ops.segment_sum(y_sorted, tok_sorted, num_segments=N)

def hybrid_layer(x, ctx, rope_cos, rope_sin, c, c_ctx, w_ada, b_ada, norm1_g, norm2_g,
                 w_in, b_in, attn_sink, w_pool, pool_scale, w_attn_br, w_pool_br, w_out,
                 w_router, b_router, w_gu, b_gu, w_down, b_down, update_ctx):
    B, L, D = x.shape
    Lc = ctx.shape[1]
    mod_x = (jax.nn.silu(c) @ w_ada + b_ada)[:, None, :]
    mod_c = jax.nn.silu(c_ctx) @ w_ada + b_ada
    sh1x, sc1x, g1x, sh2x, sc2x, g2x = jnp.split(mod_x, 6, axis=-1)
    sh1c, sc1c, g1c, sh2c, sc2c, g2c = jnp.split(mod_c, 6, axis=-1)

    hx = modulate(rmsnorm(x, norm1_g), sh1x, sc1x)
    hc = modulate(rmsnorm(ctx, norm1_g), sh1c, sc1c)
    qx, kx, vx, ux, gax, gpx = jnp.split(hx @ w_in + b_in, SPLIT_POINTS, axis=-1)
    kv_sl = slice(ATTN_W, ATTN_W + 2 * KV_W)
    kc, vc = jnp.split(hc @ w_in[:, kv_sl] + b_in[kv_sl], 2, axis=-1)
    kc = kc.reshape(B, Lc, N_KV_HEADS, HEAD_DIM)
    vc = vc.reshape(B, Lc, N_KV_HEADS, HEAD_DIM)
    qx = apply_axial_rope(qx.reshape(B, L, N_HEADS, HEAD_DIM), rope_cos, rope_sin)
    kx = apply_axial_rope(kx.reshape(B, L, N_KV_HEADS, HEAD_DIM), rope_cos, rope_sin)
    vx = vx.reshape(B, L, N_KV_HEADS, HEAD_DIM)
    attn_x = windowed_attention(qx, kx, vx, kc, vc, attn_sink)
    pool_x = multiscale_pool(ux, w_pool, pool_scale)
    x = x + g1x * merge_branches(attn_x, pool_x, gax, gpx, w_attn_br, w_pool_br, w_out)
    if update_ctx:
        qc, _, _, uc, gac, gpc = jnp.split(hc @ w_in + b_in, SPLIT_POINTS, axis=-1)
        attn_c = context_attention(qc.reshape(B, Lc, N_HEADS, HEAD_DIM), kc, vc, attn_sink)
        pool_c = multiscale_pool(uc, w_pool, pool_scale)
        ctx = ctx + g1c * merge_branches(attn_c, pool_c, gac, gpc, w_attn_br, w_pool_br, w_out)

    h2x = modulate(rmsnorm(x, norm2_g), sh2x, sc2x).reshape(B * L, D)
    if update_ctx:
        h2c = modulate(rmsnorm(ctx, norm2_g), sh2c, sc2c).reshape(B * Lc, D)
        y = moe_ffn(jnp.concatenate([h2x, h2c], axis=0),
                    w_router, b_router, w_gu, b_gu, w_down, b_down)
        x = x + g2x * y[:B * L].reshape(B, L, D)
        ctx = ctx + g2c * y[B * L:].reshape(B, Lc, D)
    else:
        y = moe_ffn(h2x, w_router, b_router, w_gu, b_gu, w_down, b_down)
        x = x + g2x * y.reshape(B, L, D)
    return x, ctx

def first_inputs(seed: int = 0) -> dict:
    key = jax.random.key(seed)
    ks = jax.random.split(key, 24)

    def nrm(k, shape, scale):
        return jax.random.normal(k, shape, jnp.float32) * scale

    D = D_MODEL
    return {
        'x': nrm(ks[0], (BATCH, SEQ, D), 1.0),
        'c': nrm(ks[1], (BATCH, D), 1.0),
        'ctx': nrm(ks[2], (BATCH, CTX_LEN, D), 1.0),
        'c_ctx': nrm(ks[3], (D,), 1.0),
        'w_ada': nrm(ks[4], (DEPTH, D, 6 * D), 0.5 * D ** -0.5),
        'b_ada': nrm(ks[5], (DEPTH, 6 * D), 0.02),
        'norm1_g': 1.0 + nrm(ks[6], (DEPTH, D), 0.02),
        'norm2_g': 1.0 + nrm(ks[7], (DEPTH, D), 0.02),
        'w_in': nrm(ks[8], (DEPTH, D, IN_W), D ** -0.5),
        'b_in': nrm(ks[9], (DEPTH, IN_W), 0.02),
        'attn_sink': nrm(ks[10], (DEPTH, N_HEADS), 0.5),
        'w_pool': nrm(ks[11], (DEPTH, N_POOL_GROUPS, POOL_GROUP_W, POOL_GROUP_W), POOL_GROUP_W ** -0.5),
        'pool_scale': 1.0 + nrm(ks[12], (DEPTH, POOL_W), 0.02),
        'w_attn_br': nrm(ks[13], (DEPTH, ATTN_W, D), ATTN_W ** -0.5),
        'w_pool_br': nrm(ks[14], (DEPTH, POOL_W, D), POOL_W ** -0.5),
        'w_out': nrm(ks[15], (DEPTH, D, D), D ** -0.5),
        'w_router': nrm(ks[16], (DEPTH, D, N_EXPERTS), D ** -0.5),
        'b_router': nrm(ks[17], (DEPTH, N_EXPERTS), 0.01),
        'w_gu': nrm(ks[18], (DEPTH, N_EXPERTS, D, 2 * D_FF), D ** -0.5),
        'b_gu': nrm(ks[19], (DEPTH, N_EXPERTS, 2 * D_FF), 0.02),
        'w_down': nrm(ks[20], (DEPTH, N_EXPERTS, D_FF, D), D_FF ** -0.5),
        'b_down': nrm(ks[21], (DEPTH, N_EXPERTS, D), 0.02),
        'final_g': 1.0 + nrm(ks[22], (D,), 0.02),
    }

def first_block(x, c, ctx, c_ctx, w_ada, b_ada, norm1_g, norm2_g, w_in, b_in, attn_sink,
              w_pool, pool_scale, w_attn_br, w_pool_br, w_out, w_router, b_router,
              w_gu, b_gu, w_down, b_down, final_g):
    L = x.shape[1]
    ROWS = L // GRID_W
    row = jnp.broadcast_to(jnp.arange(ROWS, dtype=jnp.float32)[:, None], (ROWS, GRID_W)).reshape(-1)
    col = jnp.broadcast_to(jnp.arange(GRID_W, dtype=jnp.float32)[None, :], (ROWS, GRID_W)).reshape(-1)
    inv_freq = ROPE_BASE ** (-jnp.arange(ROPE_PAIRS, dtype=jnp.float32) / ROPE_PAIRS)
    ang = jnp.stack([row[:, None] * inv_freq, col[:, None] * inv_freq], axis=1)
    rope_cos, rope_sin = jnp.cos(ang), jnp.sin(ang)
    for i in range(DEPTH):
        x, ctx = hybrid_layer(
            x, ctx, rope_cos, rope_sin, c, c_ctx, w_ada[i], b_ada[i], norm1_g[i], norm2_g[i],
            w_in[i], b_in[i], attn_sink[i], w_pool[i], pool_scale[i], w_attn_br[i],
            w_pool_br[i], w_out[i], w_router[i], b_router[i], w_gu[i], b_gu[i],
            w_down[i], b_down[i], update_ctx=(i + 1 < DEPTH))
    return rmsnorm(x, final_g)


EPS = 1e-6
ROPE_THETA = 10000.0

NSA_HEADS = 8
NSA_KV_GROUPS = 2
NSA_GROUP = NSA_HEADS // NSA_KV_GROUPS
NSA_WIDTH = NSA_HEADS * HEAD_DIM
KV_WIDTH = NSA_KV_GROUPS * HEAD_DIM
CMP_BLOCK = 32
CMP_STRIDE = 16
CMP_HIDDEN = 128
SEL_BLOCK = 64
SEL_TOPK = 16
WINDOW_2 = 512
Q_CHUNK = 32
FORCE_BONUS = 1000.0

HGRN_HEADS = 4
HGRN_EXPAND = 128
HGRN_HEAD_V = 128
HGRN_WIDTH = HGRN_HEADS * HGRN_EXPAND
HGRN_V_WIDTH = HGRN_HEADS * HGRN_HEAD_V
HGRN_CHUNK = 32

PEER_HEADS = 8
PEER_NKEYS = 128
PEER_NEXPERTS = PEER_NKEYS * PEER_NKEYS
PEER_QDIM = 256
PEER_TOPK = 16
PEER_TOK_CHUNK = 128

IN_SPLITS = (NSA_WIDTH, KV_WIDTH, KV_WIDTH, KV_WIDTH, KV_WIDTH, KV_WIDTH, KV_WIDTH, 3 * NSA_HEADS, HGRN_WIDTH, HGRN_WIDTH, HGRN_V_WIDTH, HGRN_V_WIDTH, 2 * D_MODEL)
IN_COLS = NSA_WIDTH + 6 * KV_WIDTH + 3 * NSA_HEADS + 2 * HGRN_WIDTH + 2 * HGRN_V_WIDTH + 2 * D_MODEL


def _rmsnorm(x, g):
    xf = x.astype(jnp.float32)
    y = xf * lax.rsqrt(jnp.mean(xf * xf, axis=-1, keepdims=True) + EPS)
    return (y * g.astype(jnp.float32)).astype(x.dtype)

def _masked_softmax(s, mask):
    s = jnp.where(mask, s.astype(jnp.float32), -jnp.inf)
    m = jnp.max(s, axis=-1, keepdims=True)
    m = jnp.where(jnp.isfinite(m), m, 0.0)
    p = jnp.exp(s - m)
    return p / jnp.maximum(jnp.sum(p, axis=-1, keepdims=True), 1e-30)

def _rope(x, pos):
    half = HEAD_DIM // 2
    inv = ROPE_THETA ** (-jnp.arange(half, dtype=jnp.float32) / half)
    ang = pos.astype(jnp.float32)[:, None] * inv[None, :]
    cos = jnp.cos(ang)[None, :, None, :]
    sin = jnp.sin(ang)[None, :, None, :]
    xf = x.astype(jnp.float32)
    x1, x2 = xf[..., :half], xf[..., half:]
    return jnp.concatenate([x1 * cos - x2 * sin, x2 * cos + x1 * sin], axis=-1).astype(x.dtype)

def _selection_map(n_cmp, n_sel):
    r_sel = SEL_BLOCK // CMP_STRIDE
    r_cmp = CMP_BLOCK // CMP_STRIDE
    i = np.arange(n_cmp)[:, None]
    j = np.arange(n_sel)[None, :]
    d = i - r_sel * j
    cnt = np.minimum(d, r_sel - 1) - np.maximum(d - r_cmp + 1, 0) + 1
    return np.clip(cnt, 0, None).astype(np.float32)

def _compress(k, pos_emb, w1, w2):
    B, T = k.shape[0], k.shape[1]
    r = CMP_BLOCK // CMP_STRIDE
    pieces = k.reshape(B, T // CMP_STRIDE, CMP_STRIDE, NSA_KV_GROUPS, HEAD_DIM)
    n_cmp = T // CMP_STRIDE - r + 1
    blocks = jnp.concatenate([pieces[:, j:j + n_cmp] for j in range(r)], axis=2)
    blocks = blocks + pos_emb[None, None, :, None, :]
    flat = blocks.transpose(0, 1, 3, 2, 4).reshape(B, n_cmp, NSA_KV_GROUPS, CMP_BLOCK * HEAD_DIM)
    return jax.nn.gelu(flat @ w1) @ w2

def _nsa(q, k_c, v_c, k_s, v_s, k_w, v_w, gate_logits, cmp_pos_k, cmp_pos_v, w_ck1, w_ck2, w_cv1, w_cv2):
    B, T = q.shape[0], q.shape[1]
    G, R, dh = NSA_KV_GROUPS, NSA_GROUP, HEAD_DIM
    scale = HEAD_DIM ** -0.5
    kc = _compress(k_c, cmp_pos_k, w_ck1, w_ck2)
    vc = _compress(v_c, cmp_pos_v, w_cv1, w_cv2)
    n_cmp = kc.shape[1]
    cmp_end = jnp.arange(n_cmp) * CMP_STRIDE + CMP_BLOCK - 1
    n_sel = T // SEL_BLOCK
    top_n = min(SEL_TOPK, n_sel)
    sel_map = jnp.asarray(_selection_map(n_cmp, n_sel))
    ks_blocks = k_s.reshape(B, n_sel, SEL_BLOCK, G, dh).transpose(0, 3, 1, 2, 4)
    vs_blocks = v_s.reshape(B, n_sel, SEL_BLOCK, G, dh).transpose(0, 3, 1, 2, 4)
    kw_pad = jnp.pad(k_w, ((0, 0), (WINDOW_2, 0), (0, 0), (0, 0)))
    vw_pad = jnp.pad(v_w, ((0, 0), (WINDOW_2, 0), (0, 0), (0, 0)))
    n_chunks = T // Q_CHUNK
    q_chunks = q.reshape(B, n_chunks, Q_CHUNK, G, R, dh).transpose(1, 0, 2, 3, 4, 5)
    g_chunks = gate_logits.reshape(B, n_chunks, Q_CHUNK, G, R, 3).transpose(1, 0, 2, 3, 4, 5)
    b_ix = jnp.arange(B)[:, None, None, None]
    g_ix = jnp.arange(G)[None, None, :, None]
    blk_ids = jnp.arange(n_sel)
    in_blk = jnp.arange(SEL_BLOCK)
    win_off = jnp.arange(WINDOW_2 + Q_CHUNK)

    def chunk_fn(args):
        ci, qg, gl = args
        start = ci * Q_CHUNK
        t = start + jnp.arange(Q_CHUNK)
        s_c = jnp.einsum('bqgrd,bngd->bqgrn', qg, kc) * scale
        m_c = (cmp_end[None, :] <= t[:, None])[None, :, None, None, :]
        p_c = _masked_softmax(s_c, m_c)
        o_c = jnp.einsum('bqgrn,bngd->bqgrd', p_c.astype(vc.dtype), vc)
        imp = jnp.einsum('bqgrn,nj->bqgj', p_c, sel_map)
        cur = t // SEL_BLOCK
        forced = (blk_ids[None, :] == 0) | (blk_ids[None, :] == cur[:, None]) | (blk_ids[None, :] == cur[:, None] - 1)
        causal_blk = blk_ids[None, :] * SEL_BLOCK <= t[:, None]
        imp = jnp.where(forced[None, :, None, :], imp + FORCE_BONUS, imp)
        imp = jnp.where(causal_blk[None, :, None, :], imp, -1.0)
        _, idx = lax.top_k(imp, top_n)
        kg = ks_blocks[b_ix, g_ix, idx]
        vg = vs_blocks[b_ix, g_ix, idx]
        s_s = jnp.einsum('bqgrd,bqgnld->bqgrnl', qg, kg) * scale
        kpos = idx[..., None] * SEL_BLOCK + in_blk
        m_s = (kpos <= t[None, :, None, None, None]).reshape(B, Q_CHUNK, G, 1, top_n * SEL_BLOCK)
        p_s = _masked_softmax(s_s.reshape(B, Q_CHUNK, G, R, top_n * SEL_BLOCK), m_s)
        p_s = p_s.reshape(B, Q_CHUNK, G, R, top_n, SEL_BLOCK).astype(vg.dtype)
        o_s = jnp.einsum('bqgrnl,bqgnld->bqgrd', p_s, vg)
        kw_c = lax.dynamic_slice_in_dim(kw_pad, start, WINDOW_2 + Q_CHUNK, axis=1)
        vw_c = lax.dynamic_slice_in_dim(vw_pad, start, WINDOW_2 + Q_CHUNK, axis=1)
        kpos_w = start - WINDOW_2 + win_off
        m_w = (kpos_w[None, :] <= t[:, None]) & (t[:, None] - kpos_w[None, :] < WINDOW_2) & (kpos_w[None, :] >= 0)
        s_w = jnp.einsum('bqgrd,bkgd->bqgrk', qg, kw_c) * scale
        p_w = _masked_softmax(s_w, m_w[None, :, None, None, :])
        o_w = jnp.einsum('bqgrk,bkgd->bqgrd', p_w.astype(vw_c.dtype), vw_c)
        g = jax.nn.sigmoid(gl.astype(jnp.float32)).astype(qg.dtype)
        o = g[..., 0:1] * o_c + g[..., 1:2] * o_s + g[..., 2:3] * o_w
        return o.reshape(B, Q_CHUNK, NSA_WIDTH)

    out = lax.map(chunk_fn, (jnp.arange(n_chunks), q_chunks, g_chunks))
    return out.transpose(1, 0, 2, 3).reshape(B, T, NSA_WIDTH)

def _hgrn2(hq, hf, hi, hg, lb, norm_g):
    B, T = hq.shape[0], hq.shape[1]
    H, dk, dv, C = HGRN_HEADS, HGRN_EXPAND, HGRN_HEAD_V, HGRN_CHUNK
    f = lb + (1.0 - lb) * jax.nn.sigmoid(hf.astype(jnp.float32))
    log_f = jnp.log(f)
    k = 1.0 - f
    q = jax.nn.silu(hq.astype(jnp.float32))
    v = hi.astype(jnp.float32)
    nc = T // C

    def to_chunks(a, d):
        return a.reshape(B, nc, C, H, d).transpose(1, 0, 3, 2, 4)

    causal = jnp.tril(jnp.ones((C, C), dtype=bool))

    def step(S, xs):
        qc, kc, vc, lfc = xs
        b = jnp.cumsum(lfc, axis=2)
        b_end = b[:, :, -1:, :]
        q_dec = qc * jnp.exp(b)
        k_inv = kc * jnp.exp(-b)
        k_end = kc * jnp.exp(b_end - b)
        A = jnp.where(causal, jnp.einsum('bhtd,bhsd->bhts', q_dec, k_inv), 0.0)
        o = jnp.einsum('bhts,bhse->bhte', A, vc) + jnp.einsum('bhtd,bhde->bhte', q_dec, S)
        S = jnp.exp(b_end)[:, :, 0, :, None] * S + jnp.einsum('bhsd,bhse->bhde', k_end, vc)
        return S, o

    S0 = jnp.zeros((B, H, dk, dv), jnp.float32)
    _, o = lax.scan(step, S0, (to_chunks(q, dk), to_chunks(k, dk), to_chunks(v, dv), to_chunks(log_f, dk)))
    o = o.transpose(1, 0, 3, 2, 4).reshape(B, T, H, dv).astype(hq.dtype)
    o = _rmsnorm(o, norm_g) * jax.nn.silu(hg.reshape(B, T, H, dv))
    return o.reshape(B, T, HGRN_V_WIDTH)

def _hybrid_mixer(h, layer_lb, w_in, cmp_pos_k, cmp_pos_v, w_ck1, w_ck2, w_cv1, w_cv2, norm_g, w_branch, w_out):
    B, T = h.shape[0], h.shape[1]
    proj = h @ w_in
    cuts = np.cumsum(IN_SPLITS)[:-1].tolist()
    q, k_c, v_c, k_s, v_s, k_w, v_w, nsa_gl, hq, hf, hi, hg, merge = jnp.split(proj, cuts, axis=-1)
    pos = jnp.arange(T)

    def heads(a, n):
        return a.reshape(B, T, n, HEAD_DIM)

    q = _rope(heads(q, NSA_HEADS), pos)
    k_c = _rope(heads(k_c, NSA_KV_GROUPS), pos)
    k_s = _rope(heads(k_s, NSA_KV_GROUPS), pos)
    k_w = _rope(heads(k_w, NSA_KV_GROUPS), pos)
    o_nsa = _nsa(q, k_c, heads(v_c, NSA_KV_GROUPS), k_s, heads(v_s, NSA_KV_GROUPS), k_w, heads(v_w, NSA_KV_GROUPS), nsa_gl.reshape(B, T, NSA_HEADS, 3), cmp_pos_k, cmp_pos_v, w_ck1, w_ck2, w_cv1, w_cv2)
    o_hgrn = _hgrn2(hq, hf, hi, hg, layer_lb, norm_g)
    g_a, g_b = jnp.split(jax.nn.sigmoid(merge.astype(jnp.float32)).astype(h.dtype), 2, axis=-1)
    y = g_a * (o_nsa @ w_branch[0]) + g_b * (o_hgrn @ w_branch[1])
    return y @ w_out

def _peer(h, w_q, sub_keys, u_tab, v_tab):
    B, T, D = h.shape
    n = B * T
    K = PEER_TOPK
    xt = h.reshape(n, D)
    q = (xt @ w_q).reshape(n, PEER_HEADS, 2, PEER_QDIM // 2)
    s = jnp.einsum('nhpd,phkd->nhpk', q, sub_keys).astype(jnp.float32)
    s1, i1 = lax.top_k(s[:, :, 0], K)
    s2, i2 = lax.top_k(s[:, :, 1], K)
    comb = (s1[..., :, None] + s2[..., None, :]).reshape(n, PEER_HEADS, K * K)
    cand = (i1[..., :, None] * PEER_NKEYS + i2[..., None, :]).reshape(n, PEER_HEADS, K * K)
    top_s, pos = lax.top_k(comb, K)
    experts = jnp.take_along_axis(cand, pos, axis=-1)
    gate = jax.nn.softmax(top_s, axis=-1).astype(h.dtype)
    n_chunks = n // PEER_TOK_CHUNK

    def chunk_fn(args):
        xc, ec, gc = args
        a = jax.nn.gelu(jnp.einsum('nd,nhkd->nhk', xc, u_tab[ec]))
        return jnp.einsum('nhk,nhkd->nd', gc * a, v_tab[ec])

    y = lax.map(chunk_fn, (xt.reshape(n_chunks, PEER_TOK_CHUNK, D), experts.reshape(n_chunks, PEER_TOK_CHUNK, PEER_HEADS, K), gate.reshape(n_chunks, PEER_TOK_CHUNK, PEER_HEADS, K)))
    return y.reshape(B, T, D)

def second_inputs(seed: int = 0) -> dict:
    key = jax.random.key(seed)
    ks = jax.random.split(key, 22)

    def nrm(k, shape, s):
        return jax.random.normal(k, shape, jnp.float32) * s

    D = D_MODEL
    return {
        'x': nrm(ks[0], (BATCH, SEQ, D), 1.0),
        'c': nrm(ks[1], (BATCH, D), 1.0),
        'w_ada': nrm(ks[2], (DEPTH, D, 6 * D), 0.02),
        'b_ada': nrm(ks[3], (DEPTH, 6 * D), 0.02),
        'g_mix': 1.0 + nrm(ks[4], (DEPTH, D), 0.02),
        'g_ffn': 1.0 + nrm(ks[5], (DEPTH, D), 0.02),
        'w_in': nrm(ks[6], (DEPTH, D, IN_COLS), D ** -0.5),
        'cmp_pos_k': nrm(ks[7], (DEPTH, CMP_BLOCK, HEAD_DIM), 0.02),
        'cmp_pos_v': nrm(ks[8], (DEPTH, CMP_BLOCK, HEAD_DIM), 0.02),
        'w_ck1': nrm(ks[9], (DEPTH, CMP_BLOCK * HEAD_DIM, CMP_HIDDEN), (CMP_BLOCK * HEAD_DIM) ** -0.5),
        'w_ck2': nrm(ks[10], (DEPTH, CMP_HIDDEN, HEAD_DIM), CMP_HIDDEN ** -0.5),
        'w_cv1': nrm(ks[11], (DEPTH, CMP_BLOCK * HEAD_DIM, CMP_HIDDEN), (CMP_BLOCK * HEAD_DIM) ** -0.5),
        'w_cv2': nrm(ks[12], (DEPTH, CMP_HIDDEN, HEAD_DIM), CMP_HIDDEN ** -0.5),
        'hgrn_lb_logits': nrm(ks[13], (DEPTH + 1, HGRN_WIDTH), 0.5),
        'hgrn_out_norm': 1.0 + nrm(ks[14], (DEPTH, HGRN_HEAD_V), 0.02),
        'w_branch': nrm(ks[15], (DEPTH, 2, NSA_WIDTH, D), NSA_WIDTH ** -0.5),
        'w_out': nrm(ks[16], (DEPTH, D, D), D ** -0.5),
        'w_peer_q': nrm(ks[17], (DEPTH, D, PEER_HEADS * PEER_QDIM), D ** -0.5),
        'peer_sub_keys': nrm(ks[18], (DEPTH, 2, PEER_HEADS, PEER_NKEYS, PEER_QDIM // 2), (PEER_QDIM // 2) ** -0.5),
        'peer_u': nrm(ks[19], (DEPTH, PEER_NEXPERTS, D), D ** -0.5),
        'peer_v': nrm(ks[20], (DEPTH, PEER_NEXPERTS, D), 0.5),
        'g_final': 1.0 + nrm(ks[21], (D,), 0.02),
    }

def second_block(x, c, w_ada, b_ada, g_mix, g_ffn, w_in, cmp_pos_k, cmp_pos_v, w_ck1, w_ck2, w_cv1, w_cv2, hgrn_lb_logits, hgrn_out_norm, w_branch, w_out, w_peer_q, peer_sub_keys, peer_u, peer_v, g_final):
    lb_all = jnp.cumsum(jax.nn.softmax(hgrn_lb_logits.astype(jnp.float32), axis=0), axis=0)
    cs = jax.nn.silu(c)
    for l in range(DEPTH):
        mod = cs @ w_ada[l] + b_ada[l]
        sh_m, sc_m, gt_m, sh_f, sc_f, gt_f = [m[:, None, :] for m in jnp.split(mod, 6, axis=-1)]
        h = _rmsnorm(x, g_mix[l]) * (1.0 + sc_m) + sh_m
        y = _hybrid_mixer(h, lb_all[l], w_in[l], cmp_pos_k[l], cmp_pos_v[l], w_ck1[l], w_ck2[l], w_cv1[l], w_cv2[l], hgrn_out_norm[l], w_branch[l], w_out[l])
        x = x + gt_m * y
        h = _rmsnorm(x, g_ffn[l]) * (1.0 + sc_f) + sh_f
        x = x + gt_f * _peer(h, w_peer_q[l], peer_sub_keys[l], peer_u[l], peer_v[l])
    return _rmsnorm(x, g_final)


_first_inputs = second_inputs


def second_inputs(seed=0):
    import zlib

    import numpy as np

    out = dict(_first_inputs(seed))
    spreads = {}
    factors = {}
    for name, (base, spread) in spreads.items():
        noise = np.random.default_rng([zlib.crc32(name.encode()), seed]).standard_normal(out[name].shape)
        drawn = base * np.exp(spread * noise) if base else spread * noise
        out[name] = jnp.asarray(drawn.astype(out[name].dtype))
    for name, factor in factors.items():
        out[name] = (out[name] * factor).astype(out[name].dtype)
    return out


_narrow_inputs = second_inputs


def second_inputs(seed=0):

    out = dict(_narrow_inputs(seed))
    wider = {'g_mix': 6.74,
     'g_ffn': 3.86,
     'cmp_pos_k': 12.0,
     'cmp_pos_v': 11.55,
     'hgrn_lb_logits': 5.33,
     'hgrn_out_norm': 8.4,
     'g_final': 3.1}
    for name, times in wider.items():
        mean = out[name].mean()
        out[name] = (mean + times * (out[name] - mean)).astype(out[name].dtype)
    return out


ATTN_WIDTH = D_MODEL // 2
CONV_WIDTH = D_MODEL - ATTN_WIDTH
N_HEADS_3 = ATTN_WIDTH // HEAD_DIM
CONV_GROUPS = 8
MOBA_BLOCK = 256
MOBA_TOPK = 3
QUERY_CHUNK = 32
CONV_K = 3
D_FF_3 = 256 * math.ceil(8 * D_MODEL / 3 / 256)
IN_COLS_3 = 3 * ATTN_WIDTH + 3 * CONV_WIDTH
RMS_EPS = 1e-6
NEG_BIG = -1e30


def rmsnorm_3(x, g):
    xf = x.astype(jnp.float32)
    y = xf * lax.rsqrt(jnp.mean(xf * xf, axis=-1, keepdims=True) + RMS_EPS)
    return (y * g.astype(jnp.float32)).astype(x.dtype)

def causal_dwconv(x, w, b):
    K = w.shape[0]
    S = x.shape[1]
    xp = jnp.pad(x, ((0, 0), (K - 1, 0), (0, 0)))
    y = xp[:, 0:S] * w[0]
    for kk in range(1, K):
        y = y + xp[:, kk:kk + S] * w[kk]
    return y + b

def alibi_slopes(n_heads):
    return 2.0 ** (-8.0 * jnp.arange(1, n_heads + 1, dtype=jnp.float32) / n_heads)

def moba_attention(q, k, v, slopes):
    B, H, S, dh = q.shape
    nb = -(-S // MOBA_BLOCK)
    s_pad = nb * MOBA_BLOCK
    pad = ((0, 0), (0, 0), (0, s_pad - S), (0, 0))
    k_blocks = jnp.pad(k, pad).reshape(B, H, nb, MOBA_BLOCK, dh)
    v_blocks = jnp.pad(v, pad).reshape(B, H, nb, MOBA_BLOCK, dh)
    k_mean = jnp.mean(k_blocks.astype(jnp.float32), axis=3)
    n_sel = min(MOBA_TOPK, nb)
    scale = dh ** -0.5
    n_chunks = S // QUERY_CHUNK
    bi = jnp.arange(B)[:, None, None, None]
    hi = jnp.arange(H)[None, :, None, None]
    blk_pos = jnp.arange(MOBA_BLOCK)

    def one_chunk(ci):
        start = ci * QUERY_CHUNK
        qc = lax.dynamic_slice_in_dim(q, start, QUERY_CHUNK, axis=2).astype(jnp.float32)
        t = start + jnp.arange(QUERY_CHUNK)
        blk = start // MOBA_BLOCK
        gate = jnp.einsum('bhqd,bhnd->bhqn', qc, k_mean)
        gate = jnp.where(jnp.arange(nb) < blk, gate, NEG_BIG)
        _, idx = lax.top_k(gate, n_sel)
        sel_ok = idx < blk
        ks = k_blocks[bi, hi, idx].astype(jnp.float32)
        vs = v_blocks[bi, hi, idx].astype(jnp.float32)
        s_sel = jnp.einsum('bhqd,bhqnkd->bhqnk', qc, ks) * scale
        pos_sel = idx[..., None] * MOBA_BLOCK + blk_pos
        dist_sel = (t[None, None, :, None, None] - pos_sel).astype(jnp.float32)
        s_sel = s_sel - slopes[None, :, None, None, None] * dist_sel
        s_sel = jnp.where(sel_ok[..., None], s_sel, NEG_BIG)
        k_own = lax.dynamic_index_in_dim(k_blocks, blk, axis=2, keepdims=False).astype(jnp.float32)
        v_own = lax.dynamic_index_in_dim(v_blocks, blk, axis=2, keepdims=False).astype(jnp.float32)
        s_own = jnp.einsum('bhqd,bhkd->bhqk', qc, k_own) * scale
        dist_own = (t[:, None] - (blk * MOBA_BLOCK + blk_pos)[None, :]).astype(jnp.float32)
        s_own = s_own - slopes[None, :, None, None] * dist_own
        s_own = jnp.where(dist_own >= 0, s_own, NEG_BIG)
        scores = jnp.concatenate(
            [s_sel.reshape(B, H, QUERY_CHUNK, n_sel * MOBA_BLOCK), s_own], axis=-1)
        p = jax.nn.softmax(scores, axis=-1)
        p_sel = p[..., :n_sel * MOBA_BLOCK].reshape(B, H, QUERY_CHUNK, n_sel, MOBA_BLOCK)
        p_own = p[..., n_sel * MOBA_BLOCK:]
        out = (jnp.einsum('bhqnk,bhqnkd->bhqd', p_sel, vs)
               + jnp.einsum('bhqk,bhkd->bhqd', p_own, v_own))
        return out.astype(q.dtype)

    outs = lax.map(one_chunk, jnp.arange(n_chunks))
    return outs.transpose(1, 2, 0, 3, 4).reshape(B, H, S, dh)

def third_inputs(seed: int = 0) -> dict:
    key = jax.random.key(seed)
    ks = jax.random.split(key, 20)
    f32 = jnp.float32

    def nrm(k, shape, scale):
        return jax.random.normal(k, shape, f32) * scale

    L = DEPTH
    return {
        "x": nrm(ks[0], (BATCH, SEQ, D_MODEL), 1.0),
        "c": nrm(ks[1], (BATCH, D_MODEL), 1.0),
        "w_ada": nrm(ks[2], (L, D_MODEL, 6 * D_MODEL), 0.5 * D_MODEL ** -0.5),
        "b_ada": nrm(ks[3], (L, 6 * D_MODEL), 0.01),
        "g_mix": 1.0 + nrm(ks[4], (L, D_MODEL), 0.02),
        "w_in": nrm(ks[5], (L, D_MODEL, IN_COLS_3), D_MODEL ** -0.5),
        "conv_w": nrm(ks[6], (L, CONV_K, CONV_WIDTH), CONV_K ** -0.5),
        "conv_b": nrm(ks[7], (L, CONV_WIDTH), 0.01),
        "g_attn_out": 1.0 + nrm(ks[8], (L, ATTN_WIDTH), 0.02),
        "g_conv_out": 1.0 + nrm(ks[9], (L, CONV_WIDTH), 0.02),
        "w_out": nrm(ks[10], (L, D_MODEL, D_MODEL), D_MODEL ** -0.5),
        "g_ffn": 1.0 + nrm(ks[11], (L, D_MODEL), 0.02),
        "w_up": nrm(ks[12], (L, D_MODEL, 2 * D_FF_3), D_MODEL ** -0.5),
        "ffn_conv_w": nrm(ks[13], (L, CONV_K, 2 * D_FF_3), CONV_K ** -0.5),
        "ffn_conv_b": nrm(ks[14], (L, 2 * D_FF_3), 0.01),
        "w_down": nrm(ks[15], (L, D_FF_3, D_MODEL), D_FF_3 ** -0.5),
        "g_final": 1.0 + nrm(ks[16], (D_MODEL,), 0.02),
    }

def third_block(x, c, w_ada, b_ada, g_mix, w_in, conv_w, conv_b, g_attn_out, g_conv_out,
              w_out, g_ffn, w_up, ffn_conv_w, ffn_conv_b, w_down, g_final):
    B, S, D = x.shape
    slopes = alibi_slopes(N_HEADS_3)
    A, C = ATTN_WIDTH, CONV_WIDTH
    for l in range(DEPTH):
        mod = (jax.nn.silu(c) @ w_ada[l] + b_ada[l]).astype(x.dtype)
        sh1, sc1, gt1, sh2, sc2, gt2 = jnp.split(mod[:, None, :], 6, axis=-1)

        h = rmsnorm_3(x, g_mix[l]) * (1.0 + sc1) + sh1
        proj = h @ w_in[l]
        q, k, v, u, c_gate, b_gate = jnp.split(
            proj, [A, 2 * A, 3 * A, 3 * A + C, 3 * A + 2 * C], axis=-1)

        def heads(t):
            return t.reshape(B, S, N_HEADS_3, HEAD_DIM).transpose(0, 2, 1, 3)

        attn = moba_attention(heads(q), heads(k), heads(v), slopes)
        attn = attn.transpose(0, 2, 1, 3).reshape(B, S, A)
        conv = b_gate * causal_dwconv(c_gate * u, conv_w[l], conv_b[l])
        mixed = jnp.concatenate([rmsnorm_3(attn, g_attn_out[l]),
                                 rmsnorm_3(conv, g_conv_out[l])], axis=-1)
        x = x + gt1 * (mixed @ w_out[l])

        h = rmsnorm_3(x, g_ffn[l]) * (1.0 + sc2) + sh2
        up = causal_dwconv(h @ w_up[l], ffn_conv_w[l], ffn_conv_b[l])
        val, gte = jnp.split(up, 2, axis=-1)
        x = x + gt2 * ((jax.nn.silu(gte) * val) @ w_down[l])
    return rmsnorm_3(x, g_final)


_first_inputs_3 = third_inputs


def third_inputs(seed=0):
    import zlib

    import numpy as np

    out = dict(_first_inputs_3(seed))
    spreads = {}
    factors = {'b_ada': 3.99,
     'g_mix': 6.605,
     'conv_b': 64.0,
     'g_attn_out': 25.749,
     'g_conv_out': 25.562,
     'g_ffn': 8.0,
     'ffn_conv_b': 33.066,
     'g_final': 8.289}
    for name, (base, spread) in spreads.items():
        noise = np.random.default_rng([zlib.crc32(name.encode()), seed]).standard_normal(out[name].shape)
        drawn = base * np.exp(spread * noise) if base else spread * noise
        out[name] = __import__('jax').numpy.asarray(drawn.astype(out[name].dtype))
    for name, factor in factors.items():
        out[name] = (out[name] * factor).astype(out[name].dtype)
    return out


_narrow_inputs_3 = third_inputs


def third_inputs(seed=0):

    out = dict(_narrow_inputs_3(seed))
    wider = {'conv_b': 4.96, 'g_attn_out': 3.53, 'g_conv_out': 3.55, 'g_final': 3.28}
    for name, times in wider.items():
        mean = out[name].mean()
        out[name] = (mean + times * (out[name] - mean)).astype(out[name].dtype)
    return out


def setup_inputs(seed=0):
    out = dict(first_inputs(seed))
    for name, value in second_inputs(seed + 1).items():
        if name != "x":
            out[name + "_2"] = value
    for name, value in third_inputs(seed + 2).items():
        if name != "x":
            out[name + "_3"] = value
    return out


def reference(
    x, c, ctx, c_ctx, w_ada, b_ada, norm1_g, norm2_g, w_in, b_in, attn_sink, w_pool, pool_scale,
    w_attn_br, w_pool_br, w_out, w_router, b_router, w_gu, b_gu, w_down, b_down, final_g, c_2,
    w_ada_2, b_ada_2, g_mix_2, g_ffn_2, w_in_2, cmp_pos_k_2, cmp_pos_v_2, w_ck1_2, w_ck2_2,
    w_cv1_2, w_cv2_2, hgrn_lb_logits_2, hgrn_out_norm_2, w_branch_2, w_out_2, w_peer_q_2,
    peer_sub_keys_2, peer_u_2, peer_v_2, g_final_2, c_3, w_ada_3, b_ada_3, g_mix_3, w_in_3,
    conv_w_3, conv_b_3, g_attn_out_3, g_conv_out_3, w_out_3, g_ffn_3, w_up_3, ffn_conv_w_3,
    ffn_conv_b_3, w_down_3, g_final_3,
):
    x = first_block(
        x, c, ctx, c_ctx, w_ada, b_ada, norm1_g, norm2_g, w_in, b_in, attn_sink, w_pool,
        pool_scale, w_attn_br, w_pool_br, w_out, w_router, b_router, w_gu, b_gu, w_down, b_down,
        final_g,
    )
    x = second_block(
        x, c_2, w_ada_2, b_ada_2, g_mix_2, g_ffn_2, w_in_2, cmp_pos_k_2, cmp_pos_v_2, w_ck1_2,
        w_ck2_2, w_cv1_2, w_cv2_2, hgrn_lb_logits_2, hgrn_out_norm_2, w_branch_2, w_out_2,
        w_peer_q_2, peer_sub_keys_2, peer_u_2, peer_v_2, g_final_2,
    )
    return third_block(
        x, c_3, w_ada_3, b_ada_3, g_mix_3, w_in_3, conv_w_3, conv_b_3, g_attn_out_3,
        g_conv_out_3, w_out_3, g_ffn_3, w_up_3, ffn_conv_w_3, ffn_conv_b_3, w_down_3, g_final_3,
    )


_drawn_inputs = setup_inputs


def setup_inputs(seed=0):
    import zlib

    import numpy as np

    out = dict(_drawn_inputs(seed))
    spreads = {}
    factors = {'attn_sink': 8.0}
    for name, (base, spread) in spreads.items():
        noise = np.random.default_rng([zlib.crc32(name.encode()), seed]).standard_normal(out[name].shape)
        drawn = base * np.exp(spread * noise) if base else spread * noise
        out[name] = jnp.asarray(drawn.astype(out[name].dtype))
    for name, factor in factors.items():
        out[name] = (out[name] * factor).astype(out[name].dtype)
    return out
```

```python
from contextlib import ExitStack

import numpy as np

import concourse.bass as bass
from concourse import mybir

F32 = mybir.dt.float32
U32 = mybir.dt.uint32
ALU = mybir.AluOpType
ACT = mybir.ActivationFunctionType
AX_X = mybir.AxisListType.X

P = 128
T = 256
TT = T // P
D = 1024
DC = D // P
HD = 64
SLOTS = 4
SLOT = 2048
SCALE = HD ** -0.5
MASKED = -1e30
SENTINEL = -3e38

E_N = 32
CMP = 15
NSA_G = 2
HG_H = 4
HG_C = 32
PE_H = 8
PE_K = 16
PE_N = 128
CHUNK = 4
FF = 2816
FFC = FF // P
A3 = 512

PIECES = {
    1: [("ada1", 24), ("k1", 1), ("v1", 1), ("q1", 4), ("u1", 4), ("pool_m", 1), ("w_pool", 1),
        ("ga", 4), ("gp", 4), ("attn_br", 4), ("pool_br", 4), ("out1", 4), ("moe", 12 * E_N)],
    2: [("ada2", 24), ("kc", 1), ("ksw", 2), ("q2", 2), ("ck", 2), ("cv", 2), ("hq", 2), ("hf", 2),
        ("hi", 2), ("hg", 2), ("merge", 8), ("br_a", 2), ("br_b", 2), ("out2", 4),
        ("peer_q", 8), ("keys", 1), ("peer", PE_N)],
    3: [("ada3", 24), ("qk3", 4), ("v3", 2), ("ucb3", 6), ("out3", 4), ("up", FFC), ("down", FFC // 2)],
}


def piece_table(stages):
    first, n = {}, 0
    for s in stages:
        for name, k in PIECES[s]:
            first[name] = n
            n += k
    return first, n


VECS = {
    1: [("c", 16), ("b_ada", 48), ("g_mix", 8), ("g_ffn", 8), ("b_q", 8), ("b_k", 2), ("b_ga", 8),
        ("b_gp", 8), ("pool_scale", 8), ("g_final", 8), ("eps", 1), ("sink", 16)],
    2: [("c", 8), ("b_ada", 48), ("g_mix", 8), ("g_ffn", 8), ("g_final", 8), ("eps", 1),
        ("lb0", 4), ("lb1", 4), ("hg_norm", 1), ("pos_k", 32), ("pos_v", 32), ("iota", PE_N),
        ("head_mask", PE_H)],
    3: [("c", 8), ("b_ada", 48), ("g_mix", 8), ("g_ffn", 8), ("g_final", 8), ("eps", 1),
        ("conv_w", 12), ("conv_b", 4), ("g_attn", 4), ("g_conv", 4), ("f_w", 6 * FFC), ("f_b", 2 * FFC)],
}
ROWS = {
    1: [("cos", T), ("sin", T), ("rot", P), ("mask", 2 * P), ("b_v", 256), ("b_u", D), ("b_r", 32),
        ("iota", 32), ("w_r", DC * 32)],
    2: [("cos", T), ("sin", T), ("rot", P), ("mask", P), ("cmp_mask", 2 * 16), ("reset", T),
        ("hg_mask", 32), ("w_gl", DC * 24), ("w_ck2", HD), ("w_cv2", HD)],
    3: [("dist", 3 * P)],
}
V_LEN = {s: sum(n for _, n in v) for s, v in VECS.items()}
R_LEN = {s: sum(n for _, n in v) for s, v in ROWS.items()}
MOE_IN = [("b_gu", 16 * E_N), ("b_down", D), ("sel", E_N * P)]


def build(nc, stages, dram, known):
    first_piece, n_pieces = piece_table(stages)
    marks = {}
    ctx = ExitStack()
    with ctx:
        def sb(name, shape, dt=F32):
            return ctx.enter_context(nc.sbuf_tensor(name, shape, dt))

        all_sems = {}

        def sem(name):
            all_sems[name] = ctx.enter_context(nc.semaphore(name))
            return all_sems[name]

        class Signal:

            def __init__(self, name):
                self.name, self.sem, self.n = name, sem(name), 0

            def up(self, *names):
                self.n += 1
                for name in names:
                    assert name not in marks, name
                    marks[name] = (self.name, self.n)
                return self.sem, 1

            def now(self):
                return self.sem, self.n

        sems = {}

        def signal(name):
            if name not in sems:
                sems[name] = Signal(name)
            return sems[name]

        def at(name):
            if not known:
                return anything, 1
            return all_sems[known[name][0]], known[name][1]

        ring = sb("weight_ring", [P, SLOTS, SLOT])
        work = sb("work", [P, 32768])
        xT = sb("xT", [P, DC, T])
        hT = sb("hT", [P, DC, T])
        vec = sb("vec", [P, sum(V_LEN[s] for s in stages)])
        ident = sb("ident", [P, P])
        ones = sb("ones", [P, P])
        mods = {s: sb(f"mod{s}", [P, 48, 2 if s == 1 else 1]) for s in stages}
        amps = {s: sb(f"amp{s}", [P, 3, DC]) for s in stages}
        small = sb("small", [P, 256])
        chunkbuf = sb("chunkbuf", [P, 9, CHUNK * PE_N])
        psum = ctx.enter_context(nc.psum_tensor("psum", [P, 8, 512], F32))
        acc = psum[:, 0:4, :].rearrange("p b (a t) -> p (b a) t", a=2)

        class Arena:
            def __init__(self):
                self.at = 0

            def take(self, *shape):
                n = int(np.prod(shape))
                ap = work[:, self.at:self.at + n]
                self.at += n
                assert self.at <= 32768, self.at
                if len(shape) == 2:
                    ap = ap.rearrange("p (a b) -> p a b", a=shape[0])
                if len(shape) == 3:
                    ap = ap.rearrange("p (a b c) -> p a b c", a=shape[0], b=shape[1])
                return ap

        def table(spec, base):
            got, n = {}, 0
            for name, k in spec:
                got[name] = base[:, n:n + k]
                n += k
            return got

        ring_full = [sem(f"ring_full_{s}") for s in range(SLOTS)]
        used = signal("pieces_used")
        ones_set, silu_of_c = signal("ones_set"), signal("silu_of_c")
        tables_in = {s: sem(f"tables_in_{s}") for s in stages}
        moe_in = sem("moe_tables_in")
        x_in = sem("x_in")
        spilled = sem("x_spilled")
        restored = sem("x_restored")
        stored = sem("stored")
        moe_v = sem("moe_vector_steps")
        moe_free = sem("moe_banks_read")
        moe_s = sem("moe_sigmoids")
        tok_v = [sem(f"peer_onehots_{h}") for h in range(TT)]
        tok_p = [sem(f"peer_gate_blocks_{h}") for h in range(TT)]
        tok_e = [sem(f"peer_products_{h}") for h in range(TT)]
        tok_s = [sem(f"peer_copies_{h}") for h in range(TT)]
        blk_a = sem("peer_scores")
        blk_s = sem("peer_gelus")
        blk_v = sem("peer_weights")
        sections = []
        for s in stages:
            for part in ("mix", "ffn"):
                sections.append((s, part))
        sig = {}
        for s, part in sections:
            for eng in ("vector", "scalar", "tensor", "gpsimd"):
                sig[s, part, eng] = signal(f"{eng}_done_{part}{s}")
        anything = x_in

        class Banks:
            def __init__(self):
                self.tenant, self.next, self.where, self.turn = [None] * 8, 0, {}, 8

            def open(self, name, b=None):
                if b is None:
                    b = self.next % self.turn
                    self.next += 1
                before, self.tenant[b] = self.tenant[b], name
                self.where[name] = b
                return b, before

        banks = Banks()

        def bank_of(name):
            return psum[:, banks.where[name], :]

        A = {}

        def plan(stage):
            a = Arena()
            m = {}
            m["rows"] = a.take(sum(n for _, n in ROWS[stage]))
            m["r"] = table(ROWS[stage], m["rows"])
            v0 = sum(V_LEN[s] for s in stages if s < stage)
            m["vec"] = vec[:, v0:v0 + V_LEN[stage]]
            m["v"] = table(VECS[stage], m["vec"])
            c0 = {1: 0, 2: 64, 3: 72}[stage]
            m["csil"] = small[:, c0:c0 + (16 if stage == 1 else 8)].rearrange("p (c n) -> p c n", c=DC)
            m["sq"] = a.take(DC, T)
            m["rt"] = a.take(T)
            m["rs"] = a.take(T)
            m["probs"] = a.take(3, 512)
            m["probsT"] = a.take(2, 512)
            m["sm"] = small[:, 16:16 + 3 * 16].rearrange("p (a b) -> p a b", a=3)
            m["t1"] = a.take(2, T)
            m["t2"] = a.take(2, T)
            m["base"] = a.at
            if stage == 1:
                m["ctxT"] = a.take(DC, T)
                m["hcT"] = a.take(DC, T)
                m["qraw"] = a.take(DC, T)
                m["qT"] = a.take(DC, T)
                m["kraw"] = a.take(2, T)
                m["kT"] = a.take(2, T)
                m["kcT"] = a.take(2, T)
                m["v_x"] = a.take(TT, 256)
                m["v_c"] = a.take(TT, 256)
                m["oT"] = a.take(DC, T)
                m["u"] = a.take(TT, D)
                m["diffT"] = m["ctxT"]
                m["poolT"] = m["hcT"]
                m["siga"] = m["qraw"]
                m["sigp"] = m["sq"]
                m["merged"] = a.take(DC, T)
                m["tmp"] = a.take(2, T)
                a.at = m["base"]
                m["gb"] = a.take(E_N, T)
                m["act"] = a.take(8, T)
                m["moe_tables"] = a.take(sum(n for _, n in MOE_IN))
                m.update(table(MOE_IN, m["moe_tables"]))
                m["sel"] = m["sel"].rearrange("p (e k) -> p e k", e=E_N)
                for name in ("gateT", "g", "l", "l2", "gl2", "gated", "sg"):
                    m[name] = a.take(T)
                m["gate"], m["logit"], m["hot"] = a.take(TT, E_N), a.take(TT, E_N), a.take(TT, E_N)
                m["top"], m["top_f"], m["top_e"] = a.take(TT, 8), a.take(TT, 8), a.take(TT, 4)
                m["top_i"] = a.take(TT, 8).bitcast(U32)
                m["top_n"], m["top_s"], m["top_r"] = a.take(TT), a.take(TT), a.take(TT)
            if stage == 2:
                m["qraw"] = a.take(4, T)
                m["qT"] = a.take(4, T)
                m["kraw"] = a.take(3, T)
                m["kT"] = a.take(3, T)
                m["vcT"] = a.take(1, T)
                m["v_s"] = a.take(TT, P)
                m["v_w"] = a.take(TT, P)
                m["gl"] = a.take(TT, 24)
                m["hid"] = a.take(4, 16)
                m["hbias"] = a.take(4, 1)
                m["kcmp"] = a.take(16)
                m["vcmp"] = a.take(2, HD)
                m["pc"] = a.take(16, 16)
                m["pcT"] = a.take(16, P)
                m["oT"] = a.take(4, T)
                m["qg"] = a.take(4, T)
                m["siga"] = a.take(8, T)
                m["fg"], m["kg"] = m["siga"][:, 0:4, :], m["siga"][:, 4:8, :]
                m["bcum"] = a.take(4, T)
                m["eb"] = a.take(4, T)
                m["qdec"] = a.take(4, T)
                m["kinv"] = a.take(4, T)
                m["kendT"] = a.take(4, T)
                m["kend"] = a.take(TT, 512)
                m["hv"] = a.take(TT, 512)
                m["Asb"] = a.take(8, 32)
                m["S"] = a.take(8, 512)
                m["hoT"] = a.take(4, T)
                m["hgs"] = m["qg"]
                m["sigp"] = m["sq"]
                m["merged"] = m["S"].rearrange("p a (b c) -> p (a b) c", c=T)[:, 0:8, :]
                m["tmp"] = m["t2"]
                m["cmp_s"] = small[:, 144:240].rearrange("p (a b) -> p a b", a=6)
                a.at = m["base"]
                m["pqT"] = a.take(16, T)
                m["sc"] = a.take(TT, 16, PE_N)
                m["v16"] = a.take(TT, 16, 16)
                m["i16"] = a.take(TT, 16, 16).bitcast(U32)
                m["cut"], m["cut2"] = a.take(PE_N), a.take(256)
                m["idx"] = a.take(TT, 2, P)
                m["sel"] = a.take(TT, 2048)
                m["w8"], m["w8b"], m["zs"] = a.take(TT, 8, 8), a.take(8), a.take(2, 8)
                assert a.at <= 32768 - 4096
                m["pgate"] = work[:, 32768 - 4096:32768].rearrange("p (t k) -> p t k", t=TT)
                m["G"] = work[:, :].rearrange("p (t k) -> p t k", t=T)
                m["gT"] = xT[:, :, :].rearrange("p c t -> p (c t)").rearrange("p (a t) -> p a t", a=16)
                cb = [chunkbuf[:, i, :].rearrange("p (k n) -> p k n", k=CHUNK) for i in range(8)]
                m["oh1"], m["oh2"], m["bd"], m["rr"] = cb[0:2], cb[2:4], cb[4:6], cb[6:8]
                m["idxT"] = chunkbuf[:, 8, :].rearrange("p (q t) -> p q t", q=2)
                m["wt"] = chunkbuf[:, 0, :].rearrange("p (k t) -> p k t", k=2)
                m["ge"] = chunkbuf[:, 1, :].rearrange("p (k t) -> p k t", k=2)
                m["zero"] = chunkbuf[:, 2, 0:P]
            if stage == 3:
                m["qk"] = a.take(8, T)
                m["v_x"] = a.take(TT, A3)
                m["ssb"] = a.take(3, T)
                m["oT"] = a.take(4, T)
                m["ug"] = a.take(4, T)
                m["cx"] = a.take(4, T + 2)
                m["bg"] = a.take(4, T)
                m["cv"] = a.take(4, T)
                m["mixed"] = a.take(8, T)
                m["up"] = a.take(4, 2, T + 2)
                m["ffa"] = a.take(2, T)
                m["ffs"] = a.take(2, T)
                m["ffc"] = a.take(2, 2, T)
                m["act"] = a.take(FFC, T)
            return m

        for s in stages:
            A[s] = plan(s)

        def mod_cols(s, k, n=0):
            return mods[s][:, 8 * k:8 * k + 8, n]

        block = ctx.enter_context(nc.Block())

        @block.tensor
        def _(pe):
            def bank(name, b=None):
                b, before = banks.open(name, b)
                if before is not None:
                    pe.wait_ge(*at("free:" + before))
                return psum[:, b, :]

            def piece(name, i=0):
                n = first_piece[name] + i
                pe.wait_ge(ring_full[n % SLOTS], 16 * (n // SLOTS + 1))
                return ring[:, n % SLOTS, :]

            def modulation(s):
                n = 2 if s == 1 else 1
                csil = A[s]["csil"]
                pe.wait_ge(*at(f"csil{s}"))
                ps = bank(f"mod{s}")[:, 0:48 * n].rearrange("p (j n) -> p j n", n=n)
                for i in range(24):
                    w = piece(f"ada{s}", i).rearrange("p (c o) -> p c o", c=DC)
                    for j in range(2):
                        for c in range(DC):
                            mm = pe.matmul(ps[:, 2 * i + j, :], w[:, c, j * P:(j + 1) * P], csil[:, c, :],
                                           start=(i == 0 and j == 0 and c == 0), stop=True,
                                           skip_group_check=True)
                    mm.then_inc(*used.up(*([f"mod{s}"] if i == 23 else [])))

            def mean_square(tag, E, sq, chunks):
                pe.wait_ge(*at(f"sq:{tag}"))
                ps = bank(f"ms:{tag}")
                for c in range(chunks):
                    mm = pe.matmul(ps[:, 0:T], ones[:, :], sq[:, c, :], start=(c == 0), stop=(c == chunks - 1))
                mm.then_inc(*E.up(f"ms:{tag}"))

            def pair(w, ps, moving, chunks=DC):
                for j in range(2):
                    for c in range(chunks):
                        mm = pe.matmul(ps[:, j * T:(j + 1) * T], w[:, c, j * P:(j + 1) * P], moving[:, c, :],
                                       start=(j == 0 and c == 0), stop=True, skip_group_check=True)
                return mm

            def columns(tag, i, moving):
                ps = bank(f"{tag}:{i}")
                w = piece(tag, i).rearrange("p (c o) -> p c o", c=DC)
                pair(w, ps, moving).then_inc(*used.up(f"{tag}:{i}"))

            def natural(w, ps, moving, width):
                for t in range(TT):
                    for c in range(DC):
                        mm = pe.matmul(ps[:, t * width:(t + 1) * width], moving[:, c, t * P:(t + 1) * P],
                                       w[:, c, 0:width], start=(t == 0 and c == 0), stop=True,
                                       skip_group_check=True)
                return mm

            def rotate(tag, E, m, raw, n0, n):
                pe.wait_ge(*at(f"raw:{tag}"))
                ps = bank(f"rot:{tag}")
                pe.matmul(ps[:, 0:n * T], m["r"]["rot"], raw[:, n0:n0 + n, :], start=True, stop=True) \
                  .then_inc(*E.up(f"rot:{tag}"))

            def scores(s, u, E, m):
                tile, half, qt = u // 4, u // 2 % 2, u % 2
                lo, hi = half * HD, half * HD + HD
                nk = P * (qt + 1)
                ps = bank(f"S{s}:{u}")
                q = (m["qk"] if s == 3 else m["qT"])[lo:hi, tile, qt * P:(qt + 1) * P]
                if s == 1:
                    k, kc = m["kT"][lo:hi, tile // 4, :], m["kcT"][lo:hi, tile // 4, :]
                    pe.matmul(ps[:, 0:T], q, k, start=True, stop=True, skip_group_check=True)
                    pe.matmul(ps[:, T:2 * T], q, kc, start=False, stop=True, skip_group_check=True)
                    far = (1 - qt) * P
                    mm = pe.matmul(ps[:, far:far + P], ident[:, :], m["r"]["mask"][:, qt * P:(qt + 1) * P],
                                   start=False, stop=True, skip_group_check=True)
                if s == 2:
                    for b in range(2):
                        pe.matmul(ps[:, b * nk:(b + 1) * nk], q, m["kT"][lo:hi, 1 + b, 0:nk],
                                  start=(b == 0), stop=True, skip_group_check=True)
                    for b in range(2):
                        at0 = b * nk + qt * P
                        mm = pe.matmul(ps[:, at0:at0 + P], ident[:, :], m["r"]["mask"],
                                       start=False, stop=True, skip_group_check=True)
                if s == 3:
                    mm = pe.matmul(ps[:, 0:nk], q, m["qk"][lo:hi, 4 + tile, 0:nk], start=True, stop=True)
                mm.then_inc(*E.up(f"S{s}:{u}"))

            def blocks_of_keys(s, u):
                return 4 if s == 1 else (2 * (u % 2 + 1) if s == 2 else u % 2 + 1)

            def turn(s, u, E, m):
                pe.wait_ge(*at(f"P{s}:{u}"))
                ps = bank(f"T{s}:{u}")
                for b in range(blocks_of_keys(s, u)):
                    mm = pe.transpose(ps[:, b * P:(b + 1) * P], m["probs"][:, u % 3, b * P:(b + 1) * P], ident[:, :])
                mm.then_inc(*E.up(f"T{s}:{u}"))

            def values(s, u, E, m):
                tile, half, qt = u // 4, u // 2 % 2, u % 2
                lo, hi = half * HD, half * HD + HD
                pe.wait_ge(*at(f"PT{s}:{u}"))
                if u % 4 == 0:
                    bank(f"O{s}:{tile}", 6 + tile % 2)
                ps = bank_of(f"O{s}:{tile}")
                o = ps[lo:hi, qt * P:(qt + 1) * P]
                vs = []
                if s == 1:
                    g = 2 * (tile // 4) + half
                    vs = [m["v_x"][:, b, g * HD:(g + 1) * HD] for b in range(2)]
                    vs += [m["v_c"][:, b, g * HD:(g + 1) * HD] for b in range(2)]
                if s == 2:
                    for name in ("v_s", "v_w"):
                        vs += [m[name][:, b, lo:hi] for b in range(qt + 1)]
                if s == 3:
                    h = 2 * tile + half
                    vs = [m["v_x"][:, b, h * HD:(h + 1) * HD] for b in range(qt + 1)]
                for b, v in enumerate(vs):
                    mm = pe.matmul(o, v, m["probsT"][:, u % 2, b * P:(b + 1) * P],
                                   start=(b == 0 and qt == 0), stop=True, skip_group_check=True)
                if s == 2:
                    mm = pe.matmul(o, m["vcmp"][:, half, :], m["pcT"][:, u, :], start=False, stop=True,
                                   skip_group_check=True)
                mm.then_inc(*E.up(f"O{s}:{u}"))

            def attention(s, units, E, m):
                banks.turn = 6
                for i in range(units + 3):
                    if i < units:
                        scores(s, i, E, m)
                    if 0 <= i - 2 < units:
                        turn(s, i - 2, E, m)
                    if 0 <= i - 3 < units:
                        values(s, i - 3, E, m)
                banks.turn = 8

            def drain():
                for b in range(8):
                    if banks.tenant[b] is not None:
                        pe.wait_ge(*at("free:" + banks.tenant[b]))

            def mix1():
                m, E = A[1], sig[1, "mix", "tensor"]
                pe.wait_ge(tables_in[1], 32)
                modulation(1)
                mean_square("x1", E, m["sq"], DC)
                mean_square("ctx", E, m["sq"], DC)
                pe.wait_ge(*at("h:x1"))
                pe.wait_ge(*at("h:ctx"))
                w = piece("k1").rearrange("p (c o) -> p c o", c=DC)
                pair(w, bank("k1x"), hT).then_inc(*E.up("k1x"))
                pair(w, bank("k1c"), m["hcT"]).then_inc(*used.up("k1c"))
                w = piece("v1").rearrange("p (c o) -> p c o", c=DC)
                natural(w, bank("v1x"), hT, 256).then_inc(*E.up("v1x"))
                natural(w, bank("v1c"), m["hcT"], 256).then_inc(*used.up("v1c"))
                for i in range(4):
                    columns("q1", i, hT)
                rotate("k1", E, m, m["kraw"], 0, 2)
                for i in range(4):
                    rotate(f"q1:{i}", E, m, m["qraw"], 2 * i, 2)
                pe.wait_ge(*at("qT1"))
                pe.wait_ge(*at("v1c_sb"))
                attention(1, 32, E, m)
                for i in range(4):
                    ps = bank(f"u1:{i}")
                    w = piece("u1", i).rearrange("p (c o) -> p c o", c=DC)
                    natural(w, ps, hT, 256).then_inc(*used.up(f"u1:{i}"))
                w = piece("pool_m").rearrange("p (t g k) -> p t g k", t=TT, g=4)
                pe.wait_ge(*at("u1_sb"))
                for g in range(4):
                    ps = bank(f"diff:{g}")
                    for j in range(2):
                        for t in range(TT):
                            mm = pe.matmul(ps[:, j * T:(j + 1) * T], m["u"][:, t, g * 256 + j * P:g * 256 + (j + 1) * P],
                                           w[:, t, g, :], start=(j == 0 and t == 0), stop=True, skip_group_check=True)
                    mm.then_inc(*(used.up(f"diff:{g}") if g == 3 else E.up(f"diff:{g}")))
                w = piece("w_pool").rearrange("p (g c o) -> p g c o", g=4, c=2)
                for g in range(4):
                    pe.wait_ge(*at(f"diff_sb:{g}"))
                    ps = bank(f"pooled:{g}")
                    for j in range(2):
                        for c in range(2):
                            mm = pe.matmul(ps[:, j * T:(j + 1) * T], w[:, g, c, j * P:(j + 1) * P],
                                           m["diffT"][:, 2 * g + c, :], start=(j == 0 and c == 0), stop=True,
                                           skip_group_check=True)
                    mm.then_inc(*(used.up(f"pooled:{g}") if g == 3 else E.up(f"pooled:{g}")))
                for i in range(4):
                    columns("ga", i, hT)
                for i in range(4):
                    columns("gp", i, hT)
                pe.wait_ge(*at("oT1"))
                for i in range(4):
                    columns("attn_br", i, m["oT"])
                pe.wait_ge(*at("poolT"))
                for i in range(4):
                    columns("pool_br", i, m["poolT"])
                pe.wait_ge(*at("merged1"))
                for i in range(4):
                    columns("out1", i, m["merged"])

            def moe():
                m, E = A[1], sig[1, "ffn", "tensor"]
                mean_square("f1", E, m["sq"], DC)
                pe.wait_ge(*at("h:f1"))
                ps = bank("router")
                w = m["r"]["w_r"].rearrange("p (c e) -> p c e", c=DC)
                natural(w, ps, hT, E_N).then_inc(*E.up("router"))
                pe.wait_ge(*at("gates"))
                ps = bank("gateT")
                for t in range(TT):
                    mm = pe.transpose(ps[0:E_N, t * P:(t + 1) * P], m["gate"][:, t, :], ident[:, :])
                mm.then_inc(*E.up("gateT"))
                pe.wait_ge(*at("gateT_sb"))
                pe.wait_ge(moe_in, 16)
                sel = m["sel"]
                for i in range(E_N // 2):
                    ps = bank(f"gb:{i}")
                    for j in range(2):
                        mm = pe.matmul(ps[:, j * T:(j + 1) * T], sel[0:E_N, 2 * i + j, :], m["gateT"][0:E_N, :],
                                       start=(j == 0), stop=True, skip_group_check=True)
                    mm.then_inc(*E.up(f"gb:{i}"))
                drain()
                for c in range(DC):
                    mm = pe.matmul(acc[:, c, :], m["b_down"][0:E_N, c * P:(c + 1) * P], m["gateT"][0:E_N, :],
                                   start=(c % 2 == 0), stop=False, skip_group_check=True)
                mm.then_inc(*E.up("y_started"))
                base = first_piece["moe"]
                with pe.Fori(0, E_N) as e:
                    for j in range(8):
                        n = base + j
                        pe.wait_ge(ring_full[n % SLOTS], e * 48 + 16 * (n // SLOTS + 1))
                        pe.wait_ge(moe_free, e * 8 + j + 1)
                        w = ring[:, n % SLOTS, :].rearrange("p (c o) -> p c o", c=DC)
                        pair(w, psum[:, 4 + j % 4, :], hT).then_inc(used.sem, 1)
                    for k in range(4):
                        n = base + 8 + k
                        pe.wait_ge(ring_full[n % SLOTS], e * 48 + 16 * (n // SLOTS + 1))
                        pe.wait_ge(moe_v, e * 40 + 5 * (2 * k + 2))
                        w = ring[:, n % SLOTS, :].rearrange("p (f o) -> p f o", f=2)
                        for f in range(2):
                            for c in range(DC):
                                mm = pe.matmul(acc[:, c, :], w[:, f, c * P:(c + 1) * P], m["act"][:, 2 * k + f, :],
                                               start=False, stop=False, skip_group_check=True)
                        mm.then_inc(used.sem, 1)
                used.n += 12 * E_N
                marks["moe_y"] = (used.name, used.n)
                for b in range(4):
                    banks.tenant[b] = "moe_y"
                for b in range(4, 8):
                    banks.tenant[b] = None
                mean_square("o1", E, m["sq"], DC)

            def mix2():
                m, E = A[2], sig[2, "mix", "tensor"]
                pe.wait_ge(tables_in[2], 16)
                modulation(2)
                mean_square("x2", E, m["sq"], DC)
                pe.wait_ge(*at("h:x2"))
                columns("kc", 0, hT)
                for i in range(2):
                    w = piece("ksw", i).rearrange("p (c o) -> p c o", c=DC)
                    ps = bank(f"ks:{i}")
                    for c in range(DC):
                        mm = pe.matmul(ps[:, 0:T], w[:, c, 0:P], hT[:, c, :], start=(c == 0), stop=True,
                                       skip_group_check=True)
                    for t in range(TT):
                        for c in range(DC):
                            mm = pe.matmul(ps[:, T + t * P:T + (t + 1) * P], hT[:, c, t * P:(t + 1) * P], w[:, c, P:2 * P],
                                           start=False, stop=True, skip_group_check=True)
                    mm.then_inc(*used.up(f"ks:{i}"))
                for i in range(2):
                    columns("q2", i, hT)
                natural(m["r"]["w_gl"].rearrange("p (c o) -> p c o", c=DC), bank("gl"), hT, 24).then_inc(*E.up("gl"))
                rotate("k2a", E, m, m["kraw"], 0, 2)
                rotate("k2b", E, m, m["kraw"], 2, 1)
                for i in range(2):
                    rotate(f"q2:{i}", E, m, m["qraw"], 2 * i, 2)
                pe.wait_ge(*at("qT2"))
                pe.wait_ge(*at("vcT"))
                for kv, (name, src, pos) in enumerate((("ck", m["kT"][:, 0, :], "pos_k"), ("cv", m["vcT"][:, 0, :], "pos_v"))):
                    w = [piece(name, i).rearrange("p (l o) -> p l o", l=16) for i in range(2)]
                    ps = bank(f"hid:{kv}")
                    pos = m["v"][pos]
                    ps2 = bank(f"hid2:{kv}")
                    for g, dst in ((0, ps), (1, ps2)):
                        lo, hi = g * HD, g * HD + HD
                        for l in range(32):
                            mm = pe.matmul(dst[:, 0:CMP], w[l // 16][lo:hi, l % 16, :],
                                           src[lo:hi, l:l + 16 * (CMP - 1) + 1:16],
                                           start=(l == 0), stop=True, skip_group_check=True)
                            mm = pe.matmul(dst[:, CMP:CMP + 1], w[l // 16][lo:hi, l % 16, :], pos[lo:hi, l:l + 1],
                                           start=False, stop=True, skip_group_check=True)
                            if g == 1 and l == 15:
                                mm.then_inc(*used.up())
                    mm.then_inc(*used.up(f"hid:{kv}"))
                pe.wait_ge(*at("hidden"))
                ps = bank("kcmp")
                for g in range(2):
                    mm = pe.matmul(ps[g * HD:g * HD + HD, 0:CMP], m["r"]["w_ck2"], m["hid"][:, g, 0:CMP], start=True,
                                   stop=True, skip_group_check=True)
                mm.then_inc(*E.up("kcmp"))
                ps = bank("vcmp")
                for g in range(2):
                    mm = pe.matmul(ps[0:CMP, g * HD:(g + 1) * HD], m["hid"][:, 2 + g, 0:CMP], m["r"]["w_cv2"],
                                   start=(g == 0), stop=True, skip_group_check=True)
                mm.then_inc(*E.up("vcmp"))
                pe.wait_ge(*at("kcmp_sb"))
                ps0, ps1 = bank("cmpS"), bank("cmpS1")
                for u in range(16):
                    tile, half, qt = u // 4, u // 2 % 2, u % 2
                    lo, hi = half * HD, half * HD + HD
                    dst = ps0 if half == 0 else ps1
                    mm = pe.matmul(dst[:, u * 16:u * 16 + CMP], m["qT"][lo:hi, tile, qt * P:(qt + 1) * P],
                                   m["kcmp"][lo:hi, 0:CMP], start=(u in (0, 2)), stop=True, skip_group_check=True)
                mm.then_inc(*E.up("cmpS"))
                pe.wait_ge(*at("pc"))
                for i in range(4):
                    ps = bank(f"pcT:{i}")
                    for j in range(4):
                        mm = pe.transpose(ps[0:CMP, j * P:(j + 1) * P], m["pc"][:, 4 * i + j, 0:CMP], ident[:, :])
                    mm.then_inc(*E.up(f"pcT:{i}"))
                pe.wait_ge(*at("pcT_sb"))
                attention(2, 16, E, m)
                for tag in ("hq", "hf"):
                    for i in range(2):
                        columns(tag, i, hT)
                for i in range(2):
                    ps = bank(f"hi:{i}")
                    natural(piece("hi", i).rearrange("p (c o) -> p c o", c=DC), ps, hT, 256).then_inc(*used.up(f"hi:{i}"))
                for i in range(2):
                    columns("hg", i, hT)
                pe.wait_ge(*at("kend"))
                for t in range(TT):
                    ps = bank(f"kendT:{t}")
                    for h in range(HG_H):
                        mm = pe.transpose(ps[:, h * P:(h + 1) * P], m["kendT"][:, h, t * P:(t + 1) * P], ident[:, :])
                    mm.then_inc(*E.up(f"kendT:{t}"))
                pe.wait_ge(*at("hg_ready"))
                ps = bank("A")
                for h in range(HG_H):
                    for c in range(8):
                        r = 32 * (c % 4)
                        col = (h * 2 + c // 4) * 32
                        mm = pe.matmul(ps[r:r + 32, col:col + 32], m["kinv"][:, h, c * 32:(c + 1) * 32],
                                       m["qdec"][:, h, c * 32:(c + 1) * 32], start=(h == 0 and c // 4 == 0),
                                       stop=True, skip_group_check=True)
                mm.then_inc(*E.up("A"))
                pe.wait_ge(*at("kend_sb"))
                for c in range(7):
                    r = 32 * (c % 4)
                    ps = bank(f"KV:{c}")
                    for h in range(HG_H):
                        mm = pe.matmul(ps[:, h * P:(h + 1) * P], m["kend"][r:r + 32, c // 4, h * P:(h + 1) * P],
                                       m["hv"][r:r + 32, c // 4, h * P:(h + 1) * P], start=(h == 0), stop=True,
                                       skip_group_check=True, tile_position=(r, 0))
                    mm.then_inc(*E.up(f"KV:{c}"))
                pe.wait_ge(*at("A_sb"))
                pe.wait_ge(*at("S:7"))
                intra = [bank(f"hoA:{r}") for r in range(4)]
                for h in range(HG_H):
                    for c in range(8):
                        r = 32 * (c % 4)
                        at0 = (h * 2 + c // 4) * 32
                        mm = pe.matmul(intra[c % 4][:, at0:at0 + 32],
                                       m["hv"][r:r + 32, c // 4, h * P:(h + 1) * P],
                                       m["Asb"][r:r + 32, h * 2 + c // 4, :], start=(h == 0 and c // 4 == 0), stop=True,
                                       skip_group_check=True, tile_position=(r, 0))
                mm.then_inc(*E.up("hoA"))
                for i in range(2):
                    ps = bank(f"ho:{i}")
                    for j in range(2):
                        h = 2 * i + j
                        for c in range(1, 8):
                            mm = pe.matmul(ps[:, j * T + c * 32:j * T + (c + 1) * 32], m["S"][:, c, h * P:(h + 1) * P],
                                           m["qdec"][:, h, c * 32:(c + 1) * 32], start=(j == 0 and c == 1),
                                           stop=True, skip_group_check=True)
                    mm.then_inc(*E.up(f"ho:{i}"))
                pe.wait_ge(*at("ho_sq"))
                for i in range(2):
                    ps = bank(f"hms:{i}")
                    pe.matmul(ps[:, :], ones[:, :], m["eb"][:, 2 * i:2 * i + 2, :], start=True, stop=True) \
                      .then_inc(*E.up(f"hms:{i}"))
                for i in range(8):
                    columns("merge", i, hT)
                for tag, src in (("br_a", m["oT"]), ("br_b", m["hoT"])):
                    pe.wait_ge(*at("oT2" if tag == "br_a" else "hoT"))
                    for i in range(2):
                        w = piece(tag, i).rearrange("p (c o) -> p c o", c=4)
                        for k in range(2):
                            ps = bank(f"{tag}:{2 * i + k}")
                            mm = pair(w[:, :, k * 256:(k + 1) * 256], ps, src, 4)
                            mm.then_inc(*(used.up(f"{tag}:{2 * i + k}") if k else E.up(f"{tag}:{2 * i + k}")))
                pe.wait_ge(*at("merged2"))
                for i in range(4):
                    columns("out2", i, m["merged"])

            def peer():
                m, E = A[2], sig[2, "ffn", "tensor"]
                mean_square("f2", E, m["sq"], DC)
                pe.wait_ge(*at("h:f2"))
                for i in range(8):
                    columns("peer_q", i, hT)
                w = piece("keys").rearrange("p (j k) -> p j k", j=16)
                for i in range(8):
                    pe.wait_ge(*at(f"pq_sb:{i}"))
                    ps = bank(f"ps:{i}")
                    for j in range(2):
                        for t in range(TT):
                            mm = pe.matmul(ps[:, (j * TT + t) * P:(j * TT + t + 1) * P],
                                           m["pqT"][:, 2 * i + j, t * P:(t + 1) * P], w[:, 2 * i + j, :],
                                           start=(j == 0 and t == 0), stop=True, skip_group_check=True)
                    mm.then_inc(*(used.up(f"ps:{i}") if i == 7 else E.up(f"ps:{i}")))
                pe.wait_ge(*at("idx"))
                ps = bank("idxT")
                for p in range(2):
                    for t in range(TT):
                        mm = pe.transpose(ps[:, p * T + t * P:p * T + (t + 1) * P], m["idx"][:, t, p, :], ident[:, :])
                mm.then_inc(*E.up("idxT"))
                pe.wait_ge(*at("idxT_sb"))
                for t in range(TT):
                    pe.wait_ge(*at(f"pgate:{t}"))
                    for i in range(4):
                        ps = bank(f"gT{t}:{i}")
                        for j in range(4):
                            a = 4 * i + j
                            mm = pe.transpose(ps[:, j * P:(j + 1) * P],
                                              m["pgate"][:, t, a * P:(a + 1) * P],
                                              ident[:, :])
                        mm.then_inc(*E.up(f"gT{t}:{i}"))
                    drain()
                    n = P // CHUNK
                    oh1, oh2, bd, rr = m["oh1"], m["oh2"], m["bd"], m["rr"]

                    def rows(s):
                        for k in range(CHUNK):
                            mm = pe.matmul(psum[:, s, k * P:(k + 1) * P], bd[s][:, k, :], oh2[s][:, k, :],
                                           start=(k == 0), stop=True, skip_group_check=True)
                        mm.then_inc(tok_e[t], 1)

                    def gates(s):
                        for k in range(CHUNK):
                            mm = pe.matmul(psum[:, 2 + s, k * P:(k + 1) * P], rr[s][:, k, :], oh1[s][:, k, :],
                                           start=(k == 0), stop=True, skip_group_check=True)
                        mm.then_inc(tok_e[t], 1)

                    for c in range(2):
                        pe.wait_ge(tok_v[t], 2 * c + 1)
                        pe.wait_ge(tok_p[t], c + 1)
                        rows(c)
                    pe.wait_ge(tok_s[t], 1)
                    pe.wait_ge(tok_v[t], 2)
                    gates(0)
                    with pe.Fori(1, n // 2) as i:
                        for s in range(2):
                            pe.wait_ge(tok_v[t], i * 4 + (2 * s + 1))
                            pe.wait_ge(tok_p[t], i * 2 + (s + 1))
                            pe.wait_ge(tok_s[t], i * 4 + (2 * s - 3))
                            rows(s)
                            pe.wait_ge(tok_s[t], i * 4 + (2 * s - 2))
                            pe.wait_ge(tok_v[t], i * 4 + 2 * s)
                            gates(1 - s)
                    pe.wait_ge(tok_s[t], 2 * n - 2)
                    pe.wait_ge(tok_v[t], 2 * n)
                    gates((n - 1) % 2)
                    for b in range(4):
                        banks.tenant[b] = f"G{t}"
                    for b in range(4, 8):
                        banks.tenant[b] = None
                drain()
                pe.wait_ge(*at("zero"))
                for b in range(4):
                    mm = pe.matmul(psum[:, b, :], m["zero"], hT[:, 0:2, :], start=True, stop=False,
                                   skip_group_check=True)
                mm.then_inc(*E.up("zeroed"))
                base = first_piece["peer"]

                def scores_of(n, s):
                    w = ring[:, (base + s) % SLOTS, 0:D].rearrange("p (c k) -> p c k", c=DC)
                    for c in range(DC):
                        mm = pe.matmul(psum[:, 4 + s % 4, 0:T], w[:, c, :], hT[:, c, :], start=(c == 0), stop=True,
                                       skip_group_check=True)
                    mm.then_inc(blk_a, 1)

                def values_of(s):
                    w = ring[:, (base + s) % SLOTS, D:2 * D]
                    for c in range(DC):
                        mm = pe.matmul(acc[:, c, :], w[:, c * P:(c + 1) * P], m["wt"][:, s % 2, :], start=False,
                                       stop=False, skip_group_check=True)
                    mm.then_inc(used.sem, 1)

                def landed(s):
                    return ring_full[(base + s) % SLOTS], 16 * ((base + s) // SLOTS + 1)

                pe.wait_ge(*landed(0))
                scores_of(0, 0)
                with pe.Fori(0, PE_N // 4 - 1) as i:
                    for s in range(4):
                        q, v = landed(s + 1)
                        pe.wait_ge(q, i * 16 + v)
                        scores_of(i, s + 1)
                        pe.wait_ge(blk_v, i * 4 + s + 1)
                        values_of(s)
                for s in range(4):
                    k = PE_N - 4 + s
                    if s < 3:
                        pe.wait_ge(*landed(k + 1))
                        scores_of(0, s + 1)
                    pe.wait_ge(blk_v, k + 1)
                    values_of(s)
                used.n += PE_N
                marks["peer_y"] = (used.name, used.n)
                for b in range(4):
                    banks.tenant[b] = "peer_y"
                mean_square("o2", E, m["sq"], DC)

            def mix3():
                m, E = A[3], sig[3, "mix", "tensor"]
                pe.wait_ge(tables_in[3], 16)
                modulation(3)
                mean_square("x3", E, m["sq"], DC)
                pe.wait_ge(*at("h:x3"))
                for i in range(4):
                    columns("qk3", i, hT)
                for i in range(2):
                    ps = bank(f"v3:{i}")
                    natural(piece("v3", i).rearrange("p (c o) -> p c o", c=DC), ps, hT, 256).then_inc(*used.up(f"v3:{i}"))
                pe.wait_ge(*at("qk3_sb"))
                pe.wait_ge(*at("v3_sb"))
                attention(3, 16, E, m)
                for i in range(6):
                    columns("ucb3", i, hT)
                mean_square("attn3", E, m["sq"][:, 0:4, :], 4)
                mean_square("conv3", E, m["sq"][:, 4:8, :], 4)
                pe.wait_ge(*at("h:attn3"))
                pe.wait_ge(*at("h:conv3"))
                for i in range(4):
                    columns("out3", i, m["mixed"])

            def ffn3():
                m, E = A[3], sig[3, "ffn", "tensor"]
                mean_square("f3", E, m["sq"], DC)
                pe.wait_ge(*at("h:f3"))
                for i in range(FFC):
                    columns("up", i, hT)
                drain()
                for i in range(FFC // 2):
                    pe.wait_ge(*at(f"act:{2 * i + 1}"))
                    w = piece("down", i).rearrange("p (f o) -> p f o", f=2)
                    for f in range(2):
                        for c in range(DC):
                            mm = pe.matmul(acc[:, c, :], w[:, f, c * P:(c + 1) * P], m["act"][:, 2 * i + f, :],
                                           start=(i == 0 and f == 0 and c % 2 == 0), stop=True, skip_group_check=True)
                    mm.then_inc(*used.up(*(["ffn_y"] if i == FFC // 2 - 1 else [])))
                for b in range(4):
                    banks.tenant[b] = "ffn_y"
                mean_square("o3", E, m["sq"], DC)

            pe.wait_ge(x_in, 48)
            pe.wait_ge(*at("ones"))
            if 1 in stages:
                mix1()
                moe()
            if 2 in stages:
                mix2()
                peer()
            if 3 in stages:
                mix3()
                ffn3()

        @block.sync
        def _(sp):
            stream = dram["stream"]
            for s in range(SLOTS):
                sp.dma_start(ring[:, s, :], stream[s]).then_inc(ring_full[s], 16)
            with sp.Fori(1, n_pieces // SLOTS) as i:
                for s in range(SLOTS):
                    sp.wait_ge(used.sem, i * SLOTS + (s - SLOTS + 1))
                    sp.dma_start(ring[:, s, :], stream[i * SLOTS + s]).then_inc(ring_full[s], 16)
            for n in range(n_pieces // SLOTS * SLOTS, n_pieces):
                sp.wait_ge(used.sem, n - SLOTS + 1)
                sp.dma_start(ring[:, n % SLOTS, :], stream[n]).then_inc(ring_full[n % SLOTS], 16)

        @block.vector
        def _(ve):
            def tt(V, out, a, b, op, *names):
                ve.tensor_tensor(out, a, b, op).then_inc(*V.up(*names))

            def ts(V, out, a, s1, s2, op0, op1, *names):
                if s2 is None:
                    ve.tensor_scalar(out, a, s1, None, op0).then_inc(*V.up(*names))
                else:
                    ve.tensor_scalar(out, a, s1, s2, op0, op1).then_inc(*V.up(*names))

            def wait_own(V):
                ve.wait_ge(*V.now())

            def modulation(s, V, m):
                ve.wait_ge(tables_in[s], 32 if s == 1 else 16)
                n = 2 if s == 1 else 1
                ve.wait_ge(*at(f"mod{s}"))
                ps = bank_of(f"mod{s}")[:, 0:48 * n].rearrange("p (j n) -> p j n", n=n)
                tt(V, mods[s][:, :, :], ps, m["v"]["b_ada"].unsqueeze(2).to_broadcast([P, 48, n]), ALU.add, f"free:mod{s}")
                wait_own(V)
                for k, (col, g, j) in enumerate(((1, "g_mix", 0), (4, "g_ffn", 0), (1, "g_mix", n - 1))):
                    ve.scalar_tensor_tensor(amps[s][:, k, :], mod_cols(s, col, j), 1.0, m["v"][g], ALU.add, ALU.mult) \
                      .then_inc(*V.up())
                wait_own(V)

            def norm(tag, V, m, src, dst, gain, shift, chunks=DC, sq=None):
                sq = m["sq"] if sq is None else sq
                ve.wait_ge(*at(f"rt:{tag}"))
                ve.reciprocal(m["rs"], m["rt"]).then_inc(*V.up())
                wait_own(V)
                tt(V, sq[:, 0:chunks, :], src, m["rs"].unsqueeze(1).to_broadcast([P, chunks, T]), ALU.mult)
                wait_own(V)
                for c in range(chunks):
                    last = [f"h:{tag}"] if c == chunks - 1 else []
                    if shift is None:
                        ts(V, dst[:, c, :], sq[:, c, :], gain[:, c:c + 1], None, ALU.mult, None, *last)
                    else:
                        ts(V, dst[:, c, :], sq[:, c, :], gain[:, c:c + 1], shift[:, c:c + 1], ALU.mult, ALU.add, *last)

            def halves(ap):
                return ap.rearrange("p (j t) -> p j t", j=2)

            def rope(tag, V, m, raw, dst, n0, n, *names):
                ve.wait_ge(*at(f"rot:{tag}"))
                wait_own(V)
                ps = bank_of(f"rot:{tag}")[:, 0:n * T].rearrange("p (j t) -> p j t", j=n)
                cos = m["r"]["cos"].unsqueeze(1).to_broadcast([P, n, T])
                sin = m["r"]["sin"].unsqueeze(1).to_broadcast([P, n, T])
                tt(V, m["t1"][:, 0:n, :], raw[:, n0:n0 + n, :], cos, ALU.mult)
                tt(V, m["t2"][:, 0:n, :], ps, sin, ALU.mult, f"free:rot:{tag}")
                wait_own(V)
                tt(V, dst[:, n0:n0 + n, :], m["t1"][:, 0:n, :], m["t2"][:, 0:n, :], ALU.add, *names)

            def softmax_a(s, u, V, m):
                qt = u % 2
                nk = P * (qt + 1)
                c = m["sm"][:, u % 3, :]
                ps = bank_of(f"S{s}:{u}")
                ve.wait_ge(*at(f"S{s}:{u}"))
                if u >= 3:
                    wait_own(V)
                if s == 1:
                    ve.tensor_reduce(c[:, 0:1], ps, AX_X, ALU.max).then_inc(*V.up())
                    wait_own(V)
                    ts(V, c[:, 1:2], c[:, 0:1], SCALE, m["v"]["sink"][:, u // 2:u // 2 + 1], ALU.mult, ALU.max)
                    wait_own(V)
                    ts(V, c[:, 2:3], c[:, 1:2], -1.0, None, ALU.mult, None, f"max{s}:{u}")
                if s == 2:
                    ve.tensor_reduce(c[:, 0:2], ps[:, 0:2 * nk].rearrange("p (b k) -> p b k", b=2), AX_X, ALU.max) \
                      .then_inc(*V.up())
                    wait_own(V)
                    ts(V, c[:, 2:4], c[:, 0:2], -SCALE, None, ALU.mult, None, f"max{s}:{u}")
                if s == 3:
                    h = 2 * (u // 4) + u // 2 % 2
                    slope = 2.0 ** (-(h + 1)) / SCALE
                    dist = m["r"]["dist"][:, 0:P] if qt == 0 else m["r"]["dist"][:, P:3 * P]
                    if u >= 3:
                        ve.wait_ge(*at(f"exp{s}:{u - 3}"))
                    ve.scalar_tensor_tensor(m["ssb"][:, u % 3, 0:nk], dist, slope, ps[:, 0:nk], ALU.mult, ALU.add) \
                      .then_inc(*V.up(f"free:S{s}:{u}"))
                    wait_own(V)
                    ve.tensor_reduce(c[:, 0:1], m["ssb"][:, u % 3, 0:nk], AX_X, ALU.max).then_inc(*V.up())
                    wait_own(V)
                    ts(V, c[:, 2:3], c[:, 0:1], -SCALE, None, ALU.mult, None, f"max{s}:{u}")

            def softmax_b(s, u, V, m):
                nk = P * (u % 2 + 1)
                c = m["sm"][:, u % 3, :]
                p = m["probs"][:, u % 3, :]
                ve.wait_ge(*at(f"exp{s}:{u}"))
                if s == 1:
                    tt(V, c[:, 5:6], c[:, 4:5], c[:, 6:7], ALU.add)
                    wait_own(V)
                    ve.reciprocal(c[:, 7:8], c[:, 5:6]).then_inc(*V.up())
                    wait_own(V)
                    ts(V, p, p, c[:, 7:8], None, ALU.mult, None, f"P{s}:{u}")
                if s == 2:
                    h = 4 * (u // 2 % 2) + u // 4
                    ts(V, c[:, 9:11], c[:, 4:6], 1e-30, None, ALU.max, None)
                    wait_own(V)
                    ve.reciprocal(c[:, 7:9], c[:, 9:11]).then_inc(*V.up())
                    wait_own(V)
                    g = m["gl"][:, u % 2, 3 * h:3 * h + 3]
                    tt(V, c[:, 11:13], c[:, 7:9], g[:, 1:3], ALU.mult)
                    wait_own(V)
                    for b in range(2):
                        ts(V, p[:, b * nk:(b + 1) * nk], p[:, b * nk:(b + 1) * nk], c[:, 11 + b:12 + b], None,
                           ALU.mult, None, *([f"P{s}:{u}"] if b else []))
                if s == 3:
                    ve.reciprocal(c[:, 7:8], c[:, 4:5]).then_inc(*V.up())
                    wait_own(V)
                    ts(V, p[:, 0:nk], p[:, 0:nk], c[:, 7:8], None, ALU.mult, None, f"P{s}:{u}")

            def attention(s, units, V, m):
                for i in range(units + 5):
                    if i < units:
                        softmax_a(s, i, V, m)
                    if 0 <= i - 1 < units:
                        softmax_b(s, i - 1, V, m)
                    k = i - 5
                    if 0 <= k < units and k % 4 == 3:
                        ve.wait_ge(*at(f"O{s}:{k}"))
                        ve.tensor_copy(m["oT"][:, k // 4, :], bank_of(f"O{s}:{k // 4}")[:, 0:T]) \
                          .then_inc(*V.up(f"free:O{s}:{k // 4}", *([f"oT{s}"] if k == units - 1 else [])))

            def gated(s, V, m, a, b, na, nb):
                for i in range(4):
                    ve.wait_ge(*at(f"{a}:{i}"))
                    ve.wait_ge(*at(f"{na}:3"))
                    tt(V, m["merged"][:, 2 * i:2 * i + 2, :], m["siga"][:, 2 * i:2 * i + 2, :],
                       halves(bank_of(f"{a}:{i}")), ALU.mult, f"free:{a}:{i}")
                for i in range(4):
                    ve.wait_ge(*at(f"{b}:{i}"))
                    ve.wait_ge(*at(f"{nb}:3"))
                    wait_own(V)
                    tt(V, m["tmp"], m["sigp"][:, 2 * i:2 * i + 2, :], halves(bank_of(f"{b}:{i}")), ALU.mult,
                       f"free:{b}:{i}")
                    wait_own(V)
                    tt(V, m["merged"][:, 2 * i:2 * i + 2, :], m["merged"][:, 2 * i:2 * i + 2, :], m["tmp"], ALU.add,
                       *([f"merged{s}"] if i == 3 else []))

            def residual(s, tag, V, gate, n0=None):
                for i in range(4):
                    ve.wait_ge(*at(f"{tag}:{i}"))
                    ps = bank_of(f"{tag}:{i}")
                    for j in range(2):
                        c = 2 * i + j
                        names = ([f"free:{tag}:{i}"] if j else []) + ([f"x_mixed{s}"] if c == 7 else [])
                        ve.scalar_tensor_tensor(xT[:, c, :], ps[:, j * T:(j + 1) * T], gate[:, c:c + 1], xT[:, c, :],
                                                ALU.mult, ALU.add).then_inc(*V.up(*names))

            def residual_sum(s, tag, V, gate):
                for c in range(DC):
                    names = [f"x_out{s}", f"free:{tag}"] if c == 7 else []
                    ve.scalar_tensor_tensor(xT[:, c, :], acc[:, c, :], gate[:, c:c + 1], xT[:, c, :],
                                            ALU.mult, ALU.add).then_inc(*V.up(*names))

            def mix1():
                m, V = A[1], sig[1, "mix", "vector"]
                modulation(1, V, m)
                norm("x1", V, m, xT[:, :, :], hT, amps[1][:, 0, :], mod_cols(1, 0))
                norm("ctx", V, m, m["ctxT"], m["hcT"], amps[1][:, 2, :], mod_cols(1, 0, 1))
                for tag, src, dst in (("v1x", "v1x", "v_x"), ("v1c", "v1c", "v_c")):
                    ve.wait_ge(*at(src))
                    tt(V, m[dst], bank_of(src).rearrange("p (t o) -> p t o", t=TT),
                       m["r"]["b_v"].unsqueeze(1).to_broadcast([P, TT, 256]), ALU.add, f"free:{src}", f"{tag}_sb")
                rope("k1", V, m, m["kraw"], m["kT"], 0, 2)
                for i in range(4):
                    rope(f"q1:{i}", V, m, m["qraw"], m["qT"], 2 * i, 2, *(["qT1"] if i == 3 else []))
                attention(1, 32, V, m)
                for i in range(4):
                    ve.wait_ge(*at(f"u1:{i}"))
                    tt(V, m["u"][:, :, i * 256:(i + 1) * 256], bank_of(f"u1:{i}").rearrange("p (t o) -> p t o", t=TT),
                       m["r"]["b_u"][:, i * 256:(i + 1) * 256].unsqueeze(1).to_broadcast([P, TT, 256]), ALU.add,
                       f"free:u1:{i}", *(["u1_sb"] if i == 3 else []))
                for g in range(4):
                    ve.wait_ge(*at(f"diff:{g}"))
                    ve.tensor_copy(m["diffT"][:, 2 * g:2 * g + 2, :], halves(bank_of(f"diff:{g}"))) \
                      .then_inc(*V.up(f"free:diff:{g}", f"diff_sb:{g}"))
                for g in range(4):
                    ve.wait_ge(*at(f"pooled:{g}"))
                    for j in range(2):
                        c = 2 * g + j
                        ts(V, m["poolT"][:, c, :], bank_of(f"pooled:{g}")[:, j * T:(j + 1) * T],
                           m["v"]["pool_scale"][:, c:c + 1], None, ALU.mult, None,
                           *([f"free:pooled:{g}"] if j else []), *(["poolT"] if c == 7 else []))
                gated(1, V, m, "attn_br", "pool_br", "siga1", "sigp1")
                residual(1, "out1", V, mod_cols(1, 2))

            def moe():
                m, V = A[1], sig[1, "ffn", "vector"]
                norm("f1", V, m, xT[:, :, :], hT, amps[1][:, 1, :], mod_cols(1, 3))
                ve.wait_ge(*at("router"))
                logit = m["logit"]
                tt(V, logit, bank_of("router")[:, 0:TT * E_N].rearrange("p (t e) -> p t e", t=TT),
                   m["r"]["b_r"].unsqueeze(1).to_broadcast([P, TT, E_N]), ALU.add, "free:router")
                wait_own(V)
                top, idx, idf = m["top"], m["top_i"], m["top_f"]
                for t in range(TT):
                    ve.max(top[:, t, :], logit[:, t, :]).then_inc(*V.up())
                wait_own(V)
                for t in range(TT):
                    ve.max_index(idx[:, t, :], top[:, t, :], logit[:, t, :]).then_inc(*V.up())
                ts(V, m["top_n"], top[:, :, 0], -1.0, None, ALU.mult, None, "top_n")
                wait_own(V)
                ve.tensor_copy(idf, idx).then_inc(*V.up())
                ve.wait_ge(*at("top_exp"))
                ve.reciprocal(m["top_r"], m["top_s"]).then_inc(*V.up())
                wait_own(V)
                tt(V, m["top_e"], m["top_e"], m["top_r"].unsqueeze(2).to_broadcast([P, TT, 4]), ALU.mult)
                wait_own(V)
                for k in range(4):
                    for t in range(TT):
                        ts(V, m["hot"][:, t, :] if k else m["gate"][:, t, :], m["r"]["iota"], idf[:, t, k:k + 1],
                           m["top_e"][:, t, k:k + 1], ALU.is_equal, ALU.mult)
                    wait_own(V)
                    if k:
                        tt(V, m["gate"], m["gate"], m["hot"], ALU.add, *(["gates"] if k == 3 else []))
                        wait_own(V)
                ve.wait_ge(*at("gateT"))
                ve.tensor_copy(m["gateT"][0:E_N, :], bank_of("gateT")[0:E_N, 0:T]).then_inc(*V.up("free:gateT", "gateT_sb"))
                for k in range(4):
                    ve.memset(small[:, 240 + k:241 + k], 0.0).then_inc(moe_free, 1)
                ve.wait_ge(*at("gb_sb"))
                ve.wait_ge(moe_in, 16)
                bias = m["b_gu"]
                base = first_piece["moe"]
                with ve.Fori(0, E_N) as e:
                    for j in range(8):
                        ps = psum[:, 4 + j % 4, :]
                        k = 5 * j
                        ve.wait_ge(used.sem, e * 12 + (base + j + 1))
                        ve.tensor_scalar(m["g"], ps[:, 0:T], bias[:, bass.ds(e * 16 + j, 1)], 7.0, ALU.add, ALU.min) \
                          .then_inc(moe_v, 1)
                        ve.tensor_scalar(m["l"], ps[:, T:2 * T], bias[:, bass.ds(e * 16 + (8 + j), 1)], 7.0,
                                         ALU.add, ALU.min).then_inc(moe_free, 1)
                        ve.wait_ge(moe_free, e * 8 + (4 + j + 1))
                        ve.tensor_scalar(m["l2"], m["l"], -7.0, 1.0, ALU.max, ALU.add).then_inc(moe_v, 1)
                        ve.wait_ge(moe_v, e * 40 + (k + 2))
                        ve.tensor_tensor(m["gl2"], m["g"], m["l2"], ALU.mult).then_inc(moe_v, 1)
                        ve.wait_ge(moe_v, e * 40 + (k + 3))
                        ve.tensor_tensor(m["gated"], m["gl2"], m["gb"][:, bass.ds(e, 1), :].rearrange("p a t -> p (a t)"),
                                         ALU.mult).then_inc(moe_v, 1)
                        ve.wait_ge(moe_v, e * 40 + (k + 4))
                        ve.wait_ge(moe_s, e * 8 + j + 1)
                        ve.tensor_tensor(m["act"][:, j, :], m["gated"], m["sg"], ALU.mult).then_inc(moe_v, 1)
                ve.wait_ge(moe_v, 40 * E_N)
                ve.wait_ge(*at("moe_y"))
                residual_sum(1, "moe_y", V, mod_cols(1, 5))
                norm("o1", V, m, xT[:, :, :], xT, m["v"]["g_final"], None)

            def mix2():
                m, V = A[2], sig[2, "mix", "vector"]
                modulation(2, V, m)
                ve.memset(m["vcmp"], 0.0).then_inc(*V.up())
                ve.memset(m["pcT"], 0.0).then_inc(*V.up())
                norm("x2", V, m, xT[:, :, :], hT, amps[2][:, 0, :], mod_cols(2, 0))
                ve.wait_ge(*at("kc:0"))
                ps = bank_of("kc:0")
                ve.tensor_copy(m["kraw"][:, 0, :], ps[:, 0:T]).then_inc(*V.up())
                ve.tensor_copy(m["vcT"][:, 0, :], ps[:, T:2 * T]).then_inc(*V.up("free:kc:0", "vcT"))
                for i, v in enumerate(("v_s", "v_w")):
                    ve.wait_ge(*at(f"ks:{i}"))
                    ps = bank_of(f"ks:{i}")
                    ve.tensor_copy(m["kraw"][:, 1 + i, :], ps[:, 0:T]).then_inc(*V.up(*(["raw:k2a"] if i == 0 else ["raw:k2b"])))
                    ve.tensor_copy(m[v], ps[:, T:2 * T].rearrange("p (t o) -> p t o", t=TT)) \
                      .then_inc(*V.up(f"free:ks:{i}", f"{v}_sb"))
                rope("k2a", V, m, m["kraw"], m["kT"], 0, 2)
                rope("k2b", V, m, m["kraw"], m["kT"], 2, 1)
                for i in range(2):
                    rope(f"q2:{i}", V, m, m["qraw"], m["qT"], 2 * i, 2, *(["qT2"] if i == 1 else []))
                ve.wait_ge(*at("kcmp"))
                ve.tensor_copy(m["kcmp"][:, 0:CMP], bank_of("kcmp")[:, 0:CMP]).then_inc(*V.up("free:kcmp", "kcmp_sb"))
                ve.wait_ge(*at("vcmp"))
                ve.tensor_copy(m["vcmp"][0:CMP, :, :], bank_of("vcmp")[0:CMP, 0:P].rearrange("p (g d) -> p g d", g=2)) \
                  .then_inc(*V.up("free:vcmp"))
                ve.wait_ge(*at("cmpS"))
                cm = m["r"]["cmp_mask"].rearrange("p (t n) -> p t n", t=2)
                pc = m["pc"]
                for half in range(2):
                    src = bank_of("cmpS" if half == 0 else "cmpS1")[:, 0:256].rearrange("p (u n) -> p u n", n=16)
                    for tile in range(4):
                        u = 4 * tile + 2 * half
                        ve.scalar_tensor_tensor(pc[:, u:u + 2, 0:CMP], src[:, u:u + 2, 0:CMP], SCALE, cm[:, :, 0:CMP],
                                                ALU.mult, ALU.add) \
                          .then_inc(*V.up(*(["free:cmpS" if half == 0 else "free:cmpS1"] if tile == 3 else [])))
                wait_own(V)
                q = m["cmp_s"]
                ve.tensor_reduce(q[:, 0, :], pc[:, :, 0:CMP], AX_X, ALU.max).then_inc(*V.up())
                wait_own(V)
                ts(V, q[:, 1, :], q[:, 0, :], -1e20, None, ALU.max, None)
                wait_own(V)
                tt(V, pc[:, :, 0:CMP], pc[:, :, 0:CMP], q[:, 1, :].unsqueeze(2).to_broadcast([P, 16, CMP]),
                   ALU.subtract, "pc_raw")
                ve.wait_ge(*at("pc_exp"))
                ve.tensor_reduce(q[:, 2, :], pc[:, :, 0:CMP], AX_X, ALU.add).then_inc(*V.up())
                wait_own(V)
                ts(V, q[:, 3, :], q[:, 2, :], 1e-30, None, ALU.max, None)
                wait_own(V)
                ve.reciprocal(q[:, 4, :], q[:, 3, :]).then_inc(*V.up())
                wait_own(V)
                for u in range(16):
                    h = 4 * (u // 2 % 2) + u // 4
                    ts(V, q[:, 5, u:u + 1], q[:, 4, u:u + 1], m["gl"][:, u % 2, 3 * h:3 * h + 1], None, ALU.mult, None)
                wait_own(V)
                tt(V, pc[:, :, 0:CMP], pc[:, :, 0:CMP], q[:, 5, :].unsqueeze(2).to_broadcast([P, 16, CMP]), ALU.mult, "pc")
                for i in range(4):
                    ve.wait_ge(*at(f"pcT:{i}"))
                    ve.tensor_copy(m["pcT"][0:CMP, 4 * i:4 * i + 4, :],
                                   bank_of(f"pcT:{i}")[0:CMP, :].rearrange("p (u t) -> p u t", u=4)) \
                      .then_inc(*V.up(f"free:pcT:{i}", *(["pcT_sb"] if i == 3 else [])))
                attention(2, 16, V, m)
                lb, one_lb = small[:, 128:132], small[:, 132:136]
                tt(V, small[:, 136:140], m["v"]["lb0"], m["v"]["lb1"], ALU.subtract, "lb_diff")
                ve.wait_ge(*at("lb"))
                ts(V, one_lb, lb, -1.0, 1.0, ALU.mult, ALU.add)
                ve.wait_ge(*at("hf:sig"))
                wait_own(V)
                for h in range(4):
                    ts(V, m["fg"][:, h, :], m["kg"][:, h, :], one_lb[:, h:h + 1], lb[:, h:h + 1], ALU.mult, ALU.add,
                       *(["fg"] if h == 3 else []))
                wait_own(V)
                ts(V, m["kg"], m["fg"], -1.0, 1.0, ALU.mult, ALU.add)
                ve.wait_ge(*at("logf"))
                for h in range(4):
                    ve.tensor_tensor_scan(m["bcum"][:, h, :], m["r"]["reset"], m["eb"][:, h, :], 0.0, ALU.mult, ALU.add) \
                      .then_inc(*V.up())
                wait_own(V)
                b4 = m["bcum"].rearrange("p h (c k) -> p (h c) k", k=32)
                tt(V, m["kendT"].rearrange("p h (c k) -> p (h c) k", k=32),
                   b4[:, :, 31:32].to_broadcast([P, 32, 32]), b4, ALU.subtract, "bcum")
                ve.wait_ge(*at("eb"))
                tt(V, m["qdec"], m["qg"], m["eb"], ALU.mult)
                ve.wait_ge(*at("einv"))
                tt(V, m["kinv"], m["kg"], m["fg"], ALU.mult, "hg_ready")
                ve.wait_ge(*at("eend"))
                tt(V, m["kendT"], m["kg"], m["kendT"], ALU.mult, "kend")
                for i in range(2):
                    ve.wait_ge(*at(f"hi:{i}"))
                    ve.tensor_copy(m["hv"][:, :, i * 256:(i + 1) * 256],
                                   bank_of(f"hi:{i}").rearrange("p (t o) -> p t o", t=TT)).then_inc(*V.up(f"free:hi:{i}"))
                for t in range(TT):
                    ve.wait_ge(*at(f"kendT:{t}"))
                    ve.tensor_copy(m["kend"][:, t, :], bank_of(f"kendT:{t}")) \
                      .then_inc(*V.up(f"free:kendT:{t}", *(["kend_sb"] if t else [])))
                ve.wait_ge(*at("A"))
                tt(V, m["Asb"], bank_of("A")[:, 0:256].rearrange("p (c k) -> p c k", c=8),
                   m["r"]["hg_mask"].unsqueeze(1).to_broadcast([P, 8, 32]), ALU.mult, "free:A", "A_sb")
                ve.memset(m["S"][:, 0, :], 0.0).then_inc(*V.up())
                for c in range(7):
                    ve.wait_ge(*at(f"KV:{c}"))
                    wait_own(V)
                    for h in range(HG_H):
                        ve.scalar_tensor_tensor(m["S"][:, c + 1, h * P:(h + 1) * P], m["S"][:, c, h * P:(h + 1) * P],
                                                m["eb"][:, h, 32 * c + 31:32 * c + 32], bank_of(f"KV:{c}")[:, h * P:(h + 1) * P],
                                                ALU.mult, ALU.add) \
                          .then_inc(*V.up(*([f"free:KV:{c}"] if h == 3 else []), *([f"S:{c + 1}"] if h == 3 else [])))
                ve.wait_ge(*at("hoA"))
                ho = m["hoT"]
                for r in range(4):
                    ve.tensor_copy(ho.rearrange("p h (a c k) -> p (h a) c k", a=2, k=32)[:, :, r, :],
                                   bank_of(f"hoA:{r}")[:, 0:256].rearrange("p (g k) -> p g k", k=32)) \
                      .then_inc(*V.up(f"free:hoA:{r}"))
                wait_own(V)
                for i in range(2):
                    ve.wait_ge(*at(f"ho:{i}"))
                    ps = halves(bank_of(f"ho:{i}"))[:, :, 32:T]
                    tt(V, ho[:, 2 * i:2 * i + 2, 32:T], ho[:, 2 * i:2 * i + 2, 32:T], ps, ALU.add, f"free:ho:{i}",
                       *(["ho"] if i else []))
                for i in range(2):
                    ve.wait_ge(*at(f"hrt:{i}"))
                    wait_own(V)
                    ve.reciprocal(m["t2"], m["t1"]).then_inc(*V.up(f"hrt_read:{i}"))
                    wait_own(V)
                    tt(V, ho[:, 2 * i:2 * i + 2, :], ho[:, 2 * i:2 * i + 2, :], m["t2"], ALU.mult)
                wait_own(V)
                ve.wait_ge(*at("hg_silu"))
                ve.scalar_tensor_tensor(ho, ho, m["v"]["hg_norm"], m["hgs"], ALU.mult, ALU.mult).then_inc(*V.up("hoT"))
                gated(2, V, m, "br_a", "br_b", "siga2", "sigp2")
                residual(2, "out2", V, mod_cols(2, 2))

            def peer():
                m, V = A[2], sig[2, "ffn", "vector"]
                norm("f2", V, m, xT[:, :, :], hT, amps[2][:, 1, :], mod_cols(2, 3))
                sc, v8, i8, keep = m["sc"], m["v16"], m["i16"], m["cut"]
                for i in range(8):
                    ve.wait_ge(*at(f"ps_sb:{i}"))
                    for j in range(2):
                        for t in range(TT):
                            k = 2 * i + j
                            s = sc[:, t, k, :]
                            ve.max(v8[:, t, k, 0:8], s).then_inc(*V.up())
                            wait_own(V)
                            ve.max_index(i8[:, t, k, 0:8], v8[:, t, k, 0:8], s).then_inc(*V.up())
                            ve.match_replace(keep, v8[:, t, k, 0:8], s, SENTINEL).then_inc(*V.up())
                            wait_own(V)
                            ve.max(v8[:, t, k, 8:16], keep).then_inc(*V.up())
                            wait_own(V)
                            ve.max_index(i8[:, t, k, 8:16], v8[:, t, k, 8:16], keep).then_inc(*V.up())
                wait_own(V)
                for t in range(TT):
                    ve.tensor_copy(m["idx"][:, t, :, :].rearrange("p q (h a) -> p q h a", h=8),
                                   i8[:, t, :, :].rearrange("p (h q) a -> p q h a", q=2)) \
                      .then_inc(*V.up(*(["idx"] if t else [])))
                for t in range(TT):
                    for h in range(PE_H):
                        a = v8[:, t, 2 * h, :].unsqueeze(2).to_broadcast([P, 16, 16])
                        b = v8[:, t, 2 * h + 1, :].unsqueeze(1).to_broadcast([P, 16, 16])
                        tt(V, m["pgate"][:, t, h * 256:(h + 1) * 256].rearrange("p (a b) -> p a b", a=16), a, b, ALU.add)
                wait_own(V)
                for t in range(TT):
                    for h in range(PE_H):
                        cand = m["pgate"][:, t, h * 256:(h + 1) * 256]
                        cut = m["sel"][:, t, h * 256:(h + 1) * 256]
                        w8 = m["w8"][:, t, h, :]
                        ve.max(w8, cand).then_inc(*V.up())
                        wait_own(V)
                        ve.match_replace(cut, w8, cand, SENTINEL).then_inc(*V.up())
                        wait_own(V)
                        ve.max(m["w8b"], cut).then_inc(*V.up())
                        wait_own(V)
                        ve.match_replace(m["cut2"], m["w8b"], cut, SENTINEL).then_inc(*V.up())
                        wait_own(V)
                        ts(V, cut, m["cut2"], -1e38, None, ALU.is_le, None)
                    wait_own(V)
                    cand = m["pgate"][:, t, :].rearrange("p (h k) -> p h k", h=8)
                    tt(V, cand, cand, m["w8"][:, t, :, 0:1].to_broadcast([P, 8, 256]), ALU.subtract, f"cand:{t}")
                    ve.wait_ge(*at(f"cand_exp:{t}"))
                    picked = m["sel"][:, t, :].rearrange("p (h k) -> p h k", h=8)
                    tt(V, picked, cand, picked, ALU.mult)
                    wait_own(V)
                    ve.tensor_reduce(m["zs"][:, 0, :], picked, AX_X, ALU.add).then_inc(*V.up())
                    wait_own(V)
                    ve.reciprocal(m["zs"][:, 1, :], m["zs"][:, 0, :]).then_inc(*V.up())
                    wait_own(V)
                    for h in range(PE_H):
                        ts(V, m["pgate"][:, t, :].rearrange("p (a h b) -> p a h b", a=16, h=8)[:, :, h, :],
                           picked[:, h, :].rearrange("p (a b) -> p a b", a=16), m["zs"][:, 1, h:h + 1], None,
                           ALU.mult, None, *([f"pgate:{t}"] if h == PE_H - 1 else []))
                ve.wait_ge(*at("idxT"))
                ve.tensor_copy(m["idxT"], bank_of("idxT").rearrange("p (q t) -> p q t", q=2)) \
                  .then_inc(*V.up("free:idxT", "idxT_sb"))
                ve.wait_ge(spilled, 16)
                for t in range(TT):
                    for i in range(4):
                        ve.wait_ge(*at(f"gT{t}:{i}"))
                        ve.tensor_copy(m["gT"][:, 4 * i:4 * i + 4, :], bank_of(f"gT{t}:{i}").rearrange("p (a k) -> p a k", a=4)) \
                          .then_inc(*V.up(f"free:gT{t}:{i}", *([f"gT_sb{t}"] if i == 3 else [])))
                    wait_own(V)

                    def onehot(q, place, at0):
                        ve.tensor_tensor(place, m["v"]["iota"].unsqueeze(1).to_broadcast([P, CHUNK, PE_N]),
                                         m["idxT"][:, q, bass.ds(at0 + t * P, CHUNK)].unsqueeze(2)
                                         .to_broadcast([P, CHUNK, PE_N]), ALU.is_equal).then_inc(tok_v[t], 1)

                    for s in range(2):
                        onehot(1, m["oh2"][s], CHUNK * s)
                        onehot(0, m["oh1"][s], CHUNK * s)
                    with ve.Fori(1, P // CHUNK // 2) as i:
                        for s in range(2):
                            ve.wait_ge(tok_e[t], i * 4 + (2 * s - 3))
                            onehot(1, m["oh2"][s], i * (2 * CHUNK) + CHUNK * s)
                            ve.wait_ge(tok_e[t], i * 4 + (2 * s - 1))
                            onehot(0, m["oh1"][s], i * (2 * CHUNK) + CHUNK * s)
                    ve.wait_ge(tok_e[t], 2 * P // CHUNK)
                    ve.wait_ge(tok_v[t], 2 * P // CHUNK)
                ve.memset(m["zero"], 0.0).then_inc(*V.up("zero"))
                ve.wait_ge(tok_s[1], 2 * P // CHUNK)
                G = m["G"]
                def weight(s, n):
                    ve.tensor_tensor(m["wt"][:, s % 2, :], m["ge"][:, s % 2, :],
                                     G[:, :, bass.ds(n, 1)].rearrange("p t a -> p (t a)"), ALU.mult).then_inc(blk_v, 1)
                with ve.Fori(0, PE_N // 4) as i:
                    for s in range(4):
                        ve.wait_ge(blk_s, i * 4 + s + 1)
                        ve.wait_ge(blk_a, i * 4 + s + 1)
                        weight(s, i * 4 + s)
                ve.wait_ge(blk_v, PE_N)
                ve.wait_ge(*at("peer_y"))
                ve.wait_ge(restored, 16)
                residual_sum(2, "peer_y", V, mod_cols(2, 5))
                norm("o2", V, m, xT[:, :, :], xT, m["v"]["g_final"], None)

            def mix3():
                m, V = A[3], sig[3, "mix", "vector"]
                modulation(3, V, m)
                norm("x3", V, m, xT[:, :, :], hT, amps[3][:, 0, :], mod_cols(3, 0))
                for i in range(2):
                    ve.wait_ge(*at(f"v3:{i}"))
                    ve.tensor_copy(m["v_x"][:, :, i * 256:(i + 1) * 256],
                                   bank_of(f"v3:{i}").rearrange("p (t o) -> p t o", t=TT)) \
                      .then_inc(*V.up(f"free:v3:{i}", *(["v3_sb"] if i else [])))
                ve.memset(m["cx"][:, :, 0:2], 0.0).then_inc(*V.up())
                ve.memset(m["up"][:, :, :, 0:2].rearrange("p a b c -> p (a b) c"), 0.0).then_inc(*V.up())
                attention(3, 16, V, m)
                for i in range(2):
                    ve.wait_ge(*at(f"ucb3:{2 + i}"))
                    ve.wait_ge(*at(f"ug:{i}"))
                    tt(V, m["cx"][:, 2 * i:2 * i + 2, 2:T + 2], halves(bank_of(f"ucb3:{2 + i}")),
                       m["ug"][:, 2 * i:2 * i + 2, :], ALU.mult, f"free:ucb3:{2 + i}")
                wait_own(V)
                w = m["v"]["conv_w"]
                for c in range(4):
                    ts(V, m["cv"][:, c, :], m["cx"][:, c, 0:T], w[:, c:c + 1], m["v"]["conv_b"][:, c:c + 1], ALU.mult, ALU.add)
                for k in (1, 2):
                    wait_own(V)
                    for c in range(4):
                        ve.scalar_tensor_tensor(m["cv"][:, c, :], m["cx"][:, c, k:k + T], w[:, 4 * k + c:4 * k + c + 1],
                                                m["cv"][:, c, :], ALU.mult, ALU.add).then_inc(*V.up())
                wait_own(V)
                for i in range(2):
                    ve.wait_ge(*at(f"ucb3:{4 + i}"))
                    tt(V, m["cv"][:, 2 * i:2 * i + 2, :], halves(bank_of(f"ucb3:{4 + i}")), m["cv"][:, 2 * i:2 * i + 2, :],
                       ALU.mult, f"free:ucb3:{4 + i}", *(["cv"] if i else []))
                norm("attn3", V, m, m["oT"], m["mixed"][:, 0:4, :], m["v"]["g_attn"], None, 4, m["ug"])
                wait_own(V)
                norm("conv3", V, m, m["cv"], m["mixed"][:, 4:8, :], m["v"]["g_conv"], None, 4, m["bg"])
                residual(3, "out3", V, mod_cols(3, 2))

            def ffn3():
                m, V = A[3], sig[3, "ffn", "vector"]
                norm("f3", V, m, xT[:, :, :], hT, amps[3][:, 1, :], mod_cols(3, 3))
                fw, fb = m["v"]["f_w"], m["v"]["f_b"]
                for i in range(FFC):
                    ve.wait_ge(*at(f"up_sb:{i}"))
                    y = m["ffa"]
                    wait_own(V)
                    src = m["up"][:, i % 4, :, :]
                    for j in range(2):
                        ch = j * FFC + i
                        ts(V, y[:, j, :], src[:, j, 0:T], fw[:, ch:ch + 1], fb[:, ch:ch + 1], ALU.mult, ALU.add)
                    for k in (1, 2):
                        wait_own(V)
                        for j in range(2):
                            ch = k * 2 * FFC + j * FFC + i
                            if k == 2 and j == 0 and i >= 2:
                                ve.wait_ge(*at(f"act:{i - 2}"))
                            dst = y if k == 1 else m["ffc"][:, i % 2, :, :]
                            ve.scalar_tensor_tensor(dst[:, j, :], src[:, j, k:k + T], fw[:, ch:ch + 1], y[:, j, :],
                                                    ALU.mult, ALU.add) \
                              .then_inc(*V.up(*([f"conv:{i}"] if k == 2 and j else [])))
                    if i >= 1:
                        act(i - 1, V, m)
                act(FFC - 1, V, m)
                ve.wait_ge(*at("ffn_y"))
                residual_sum(3, "ffn_y", V, mod_cols(3, 5))
                norm("o3", V, m, xT[:, :, :], xT, m["v"]["g_final"], None)

            def act(i, V, m):
                ve.wait_ge(*at(f"silu:{i}"))
                tt(V, m["act"][:, i, :], m["ffs"][:, i % 2, :], m["ffc"][:, i % 2, 0, :], ALU.mult, f"act:{i}")

            ve.memset(ones[:, :], 1.0).then_inc(*ones_set.up("ones"))
            ve.wait_ge(x_in, 48)
            if 1 in stages:
                mix1()
                moe()
            if 2 in stages:
                mix2()
                peer()
            if 3 in stages:
                mix3()
                ffn3()

        @block.scalar
        def _(sc):
            def act(A_, out_, in_, func, *names, **kw):
                sc.activation(out_, in_, func, **kw).then_inc(*A_.up(*names))

            def root(tag, A_, m, src, chunks, sq=None, wait=None):
                if wait:
                    sc.wait_ge(*at(wait))
                act(A_, (m["sq"] if sq is None else sq)[:, 0:chunks, :], src, ACT.Square, f"sq:{tag}")
                sc.wait_ge(*at(f"ms:{tag}"))
                act(A_, m["rt"], bank_of(f"ms:{tag}")[:, 0:T], ACT.Sqrt, f"rt:{tag}", f"free:ms:{tag}",
                    scale=1.0 / (chunks * P), bias=m["v"]["eps"])

            def evict(A_, tag, i, dst, func, bias=None, *names):
                sc.wait_ge(*at(f"{tag}:{i}"))
                ps = bank_of(f"{tag}:{i}")
                if bias is None:
                    act(A_, dst, ps.rearrange("p (j t) -> p j t", j=2), func, f"free:{tag}:{i}", *names)
                    return
                for j in range(2):
                    act(A_, dst[:, j, :], ps[:, j * T:(j + 1) * T], func, *([f"free:{tag}:{i}", *names] if j else []),
                        bias=bias[:, j:j + 1])

            def exponentials(s, u, A_, m):
                qt = u % 2
                nk = P * (qt + 1)
                c = m["sm"][:, u % 3, :]
                ps = bank_of(f"S{s}:{u}")
                sc.wait_ge(*at(f"max{s}:{u}"))
                if u >= 3:
                    sc.wait_ge(*at(f"T{s}:{u - 3}"))
                p = m["probs"][:, u % 3, :]
                if s == 1:
                    act(A_, c[:, 6:7], m["v"]["sink"][:, u // 2:u // 2 + 1], ACT.Exp, bias=c[:, 2:3])
                    act(A_, p, ps, ACT.Exp, f"free:S{s}:{u}", f"exp{s}:{u}", bias=c[:, 2:3], scale=SCALE,
                        accum_out=c[:, 4:5])
                if s == 2:
                    for b in range(2):
                        act(A_, p[:, b * nk:(b + 1) * nk], ps[:, b * nk:(b + 1) * nk], ACT.Exp,
                            *([f"free:S{s}:{u}", f"exp{s}:{u}"] if b else []), bias=c[:, 2 + b:3 + b], scale=SCALE,
                            accum_out=c[:, 4 + b:5 + b])
                if s == 3:
                    act(A_, p[:, 0:nk], m["ssb"][:, u % 3, 0:nk], ACT.Exp, f"exp{s}:{u}", bias=c[:, 2:3], scale=SCALE,
                        accum_out=c[:, 4:5])

            def attention(s, units, A_, m):
                for i in range(units + 2):
                    if i < units:
                        exponentials(s, i, A_, m)
                    k = i - 2
                    if 0 <= k < units:
                        n = P * (4 if s == 1 else (2 * (k % 2 + 1) if s == 2 else k % 2 + 1))
                        sc.wait_ge(*at(f"T{s}:{k}"))
                        if k >= 2:
                            sc.wait_ge(*at(f"O{s}:{k - 2}"))
                        act(A_, m["probsT"][:, k % 2, 0:n], bank_of(f"T{s}:{k}")[:, 0:n], ACT.Copy, f"PT{s}:{k}",
                            f"free:T{s}:{k}")

            def mix1():
                m, A_ = A[1], sig[1, "mix", "scalar"]
                root("x1", A_, m, xT[:, :, :], DC)
                sc.wait_ge(tables_in[1], 32)
                root("ctx", A_, m, m["ctxT"], DC, wait="h:x1")
                for tag, dst in (("k1x", "kraw"), ("k1c", "kcT")):
                    sc.wait_ge(*at(tag))
                    for j in range(2):
                        act(A_, m[dst][:, j, :], bank_of(tag)[:, j * T:(j + 1) * T], ACT.Identity,
                            *([f"free:{tag}"] if j else []), *(["raw:k1"] if j and tag == "k1x" else []),
                            bias=m["v"]["b_k"][:, j:j + 1])
                for i in range(4):
                    evict(A_, "q1", i, m["qraw"][:, 2 * i:2 * i + 2, :], ACT.Identity, m["v"]["b_q"][:, 2 * i:2 * i + 2],
                          f"raw:q1:{i}")
                attention(1, 32, A_, m)
                for tag, dst in (("ga", "siga"), ("gp", "sigp")):
                    for i in range(4):
                        evict(A_, tag, i, m[dst][:, 2 * i:2 * i + 2, :], ACT.Sigmoid,
                              m["v"]["b_" + tag][:, 2 * i:2 * i + 2], f"{dst}1:{i}")

            def moe():
                m, A_ = A[1], sig[1, "ffn", "scalar"]
                root("f1", A_, m, xT[:, :, :], DC, wait="x_mixed1")
                sc.wait_ge(*at("top_n"))
                for t in range(TT):
                    act(A_, m["top_e"][:, t, :], m["top"][:, t, 0:4], ACT.Exp, *(["top_exp"] if t else []),
                        bias=m["top_n"][:, t:t + 1], accum_out=m["top_s"][:, t:t + 1])
                for i in range(E_N // 2):
                    evict(A_, "gb", i, m["gb"][:, 2 * i:2 * i + 2, :], ACT.Copy, None, *(["gb_sb"] if i == 15 else []))
                with sc.Fori(0, E_N) as e:
                    for j in range(8):
                        sc.wait_ge(moe_v, e * 40 + (5 * j + 1))
                        sc.activation(m["sg"], m["g"], ACT.Sigmoid, scale=1.702).then_inc(moe_s, 1)
                root("o1", A_, m, xT[:, :, :], DC, wait="x_out1")

            def mix2():
                m, A_ = A[2], sig[2, "mix", "scalar"]
                root("x2", A_, m, xT[:, :, :], DC, wait="h:o1" if 1 in stages else None)
                for i in range(2):
                    evict(A_, "q2", i, m["qraw"][:, 2 * i:2 * i + 2, :], ACT.Copy, None, f"raw:q2:{i}")
                sc.wait_ge(*at("gl"))
                act(A_, m["gl"], bank_of("gl")[:, 0:TT * 24].rearrange("p (t k) -> p t k", t=TT), ACT.Sigmoid, "free:gl",
                    "gl_sb")
                for kv in range(2):
                    sc.wait_ge(*at(f"hid:{kv}"))
                    for g in range(2):
                        ps = bank_of(f"hid:{kv}" if g == 0 else f"hid2:{kv}")
                        act(A_, m["hbias"][:, 2 * kv + g, :], ps[:, CMP:CMP + 1], ACT.Copy)
                        sc.wait_ge(*A_.now())
                        act(A_, m["hid"][:, 2 * kv + g, 0:CMP], ps[:, 0:CMP], ACT.Gelu_apprx_tanh,
                            f"free:hid:{kv}" if g == 0 else f"free:hid2:{kv}", *(["hidden"] if kv and g else []),
                            bias=m["hbias"][:, 2 * kv + g, :])
                sc.wait_ge(*at("pc_raw"))
                act(A_, m["pc"][:, :, 0:CMP], m["pc"][:, :, 0:CMP], ACT.Exp, "pc_exp")
                attention(2, 16, A_, m)
                for i in range(2):
                    evict(A_, "hq", i, m["qg"][:, 2 * i:2 * i + 2, :], ACT.Silu)
                for i in range(2):
                    evict(A_, "hf", i, m["kg"][:, 2 * i:2 * i + 2, :], ACT.Sigmoid, None, *(["hf:sig"] if i else []))
                sc.wait_ge(*at("lb_diff"))
                act(A_, small[:, 128:132], small[:, 136:140], ACT.Sigmoid, "lb")
                sc.wait_ge(*at("fg"))
                act(A_, m["eb"], m["fg"], ACT.Ln, "logf")
                sc.wait_ge(*at("bcum"))
                act(A_, m["eb"], m["bcum"], ACT.Exp, "eb")
                act(A_, m["fg"], m["bcum"], ACT.Exp, "einv", scale=-1.0)
                act(A_, m["kendT"], m["kendT"], ACT.Exp, "eend")
                sc.wait_ge(*at("hg_ready"))
                for i in range(2):
                    evict(A_, "hg", i, m["hgs"][:, 2 * i:2 * i + 2, :], ACT.Silu, None, *(["hg_silu"] if i else []))
                sc.wait_ge(*at("ho"))
                act(A_, m["eb"], m["hoT"], ACT.Square, "ho_sq")
                for i in range(2):
                    sc.wait_ge(*at(f"hms:{i}"))
                    if i:
                        sc.wait_ge(*at("hrt_read:0"))
                    act(A_, m["t1"], bank_of(f"hms:{i}").rearrange("p (j t) -> p j t", j=2), ACT.Sqrt, f"hrt:{i}",
                        f"free:hms:{i}", scale=1.0 / P, bias=m["v"]["eps"])
                sc.wait_ge(*at("kend"))
                for i in range(8):
                    dst = m["siga"] if i < 4 else m["sigp"]
                    k = 2 * (i % 4)
                    evict(A_, "merge", i, dst[:, k:k + 2, :], ACT.Sigmoid, None, f"sig{'a' if i < 4 else 'p'}2:{i % 4}")

            def peer():
                m, A_ = A[2], sig[2, "ffn", "scalar"]
                root("f2", A_, m, xT[:, :, :], DC, wait="x_mixed2")
                for i in range(8):
                    evict(A_, "peer_q", i, m["pqT"][:, 2 * i:2 * i + 2, :], ACT.Copy, None, f"pq_sb:{i}")
                for i in range(8):
                    sc.wait_ge(*at(f"ps:{i}"))
                    act(A_, m["sc"][:, :, 2 * i:2 * i + 2, :].rearrange("p t j k -> p j t k"),
                        bank_of(f"ps:{i}").rearrange("p (j t k) -> p j t k", j=2, t=TT), ACT.Copy, f"free:ps:{i}",
                        f"ps_sb:{i}")
                for t in range(TT):
                    sc.wait_ge(*at(f"cand:{t}"))
                    act(A_, m["pgate"][:, t, :], m["pgate"][:, t, :], ACT.Exp, f"cand_exp:{t}")
                for t in range(TT):
                    G = m["G"].rearrange("p t k -> p (t k)")

                    def copy_r(s):
                        sc.copy(m["rr"][s].rearrange("p k n -> p (k n)"), psum[:, s, :]).then_inc(tok_s[t], 1)

                    def copy_g(s, at0):
                        sc.copy(G[:, bass.ds(at0 + t * (P * PE_N), CHUNK * PE_N)], psum[:, 2 + s, :]).then_inc(tok_s[t], 1)

                    sc.wait_ge(tok_e[t], 1)
                    copy_r(0)
                    sc.wait_ge(tok_e[t], 2)
                    copy_r(1)
                    sc.wait_ge(tok_e[t], 3)
                    copy_g(0, 0)
                    with sc.Fori(1, P // CHUNK // 2) as i:
                        for s in range(2):
                            sc.wait_ge(tok_e[t], i * 4 + 2 * s)
                            copy_r(s)
                            sc.wait_ge(tok_e[t], i * 4 + (2 * s + 1))
                            copy_g(1 - s, i * (2 * CHUNK * PE_N) + (s - 1) * CHUNK * PE_N)
                    sc.wait_ge(tok_e[t], 2 * P // CHUNK)
                    copy_g(1, (P - CHUNK) * PE_N)
                    marks[f"free:G{t}"] = (f"peer_copies_{t}", 2 * P // CHUNK)

                def gelu(s):
                    sc.activation(m["ge"][:, s % 2, :], psum[:, 4 + s, 0:T], ACT.Gelu_apprx_tanh).then_inc(blk_s, 1)

                for s in range(4):
                    sc.wait_ge(blk_a, s + 1)
                    if s >= 2:
                        sc.wait_ge(blk_v, s - 1)
                    gelu(s)
                with sc.Fori(1, PE_N // 4) as i:
                    for s in range(4):
                        sc.wait_ge(blk_a, i * 4 + s + 1)
                        sc.wait_ge(blk_v, i * 4 + (s - 1))
                        gelu(s)
                root("o2", A_, m, xT[:, :, :], DC, wait="x_out2")

            def mix3():
                m, A_ = A[3], sig[3, "mix", "scalar"]
                root("x3", A_, m, xT[:, :, :], DC, wait="h:o2" if 2 in stages else None)
                for i in range(4):
                    evict(A_, "qk3", i, m["qk"][:, 2 * i:2 * i + 2, :], ACT.Copy, None, *(["qk3_sb"] if i == 3 else []))
                attention(3, 16, A_, m)
                for i in range(2):
                    evict(A_, "ucb3", i, m["ug"][:, 2 * i:2 * i + 2, :], ACT.Copy, None, f"ug:{i}")
                root("attn3", A_, m, m["oT"], 4, wait="oT3")
                sc.wait_ge(*at("cv"))
                act(A_, m["sq"][:, 4:8, :], m["cv"], ACT.Square, "sq:conv3")
                sc.wait_ge(*at("h:attn3"))
                sc.wait_ge(*at("ms:conv3"))
                act(A_, m["rt"], bank_of("ms:conv3")[:, 0:T], ACT.Sqrt, "rt:conv3", "free:ms:conv3",
                    scale=1.0 / A3, bias=m["v"]["eps"])

            def ffn3():
                m, A_ = A[3], sig[3, "ffn", "scalar"]
                root("f3", A_, m, xT[:, :, :], DC, wait="x_mixed3")

                def silu(i):
                    sc.wait_ge(*at(f"conv:{i}"))
                    if i >= 2:
                        sc.wait_ge(*at(f"act:{i - 2}"))
                    act(A_, m["ffs"][:, i % 2, :], m["ffc"][:, i % 2, 1, :], ACT.Silu, f"silu:{i}")

                for i in range(FFC):
                    if i >= 4:
                        sc.wait_ge(*at(f"conv:{i - 4}"))
                    evict(A_, "up", i, m["up"][:, i % 4, :, 2:T + 2], ACT.Copy, None, f"up_sb:{i}")
                    if i >= 1:
                        silu(i - 1)
                silu(FFC - 1)
                root("o3", A_, m, xT[:, :, :], DC, wait="x_out3")

            sc.wait_ge(x_in, 48)
            for s in stages:
                src = A[s]["v"]["c"].rearrange("p (c n) -> p c n", c=DC)
                act(silu_of_c, A[s]["csil"], src, ACT.Silu, f"csil{s}")
            if 1 in stages:
                mix1()
                moe()
            if 2 in stages:
                mix2()
                peer()
            if 3 in stages:
                mix3()
                ffn3()

        @block.gpsimd
        def _(gp):
            gp.dma_start(xT[:, :, :], dram["x"]).then_inc(x_in, 16)
            gp.dma_start(vec[:, :], dram["vec"]).then_inc(x_in, 16)
            gp.dma_start(ident[:, :], dram["ident"]).then_inc(x_in, 16)
            if 1 in stages:
                m = A[1]
                gp.dma_start(m["rows"], dram["rows1"]).then_inc(tables_in[1], 16)
                gp.dma_start(m["ctxT"], dram["ctx"]).then_inc(tables_in[1], 16)
                gp.wait_ge(*at("x_mixed1"))
                gp.dma_start(m["moe_tables"], dram["moe"]).then_inc(moe_in, 16)
            if 2 in stages:
                m = A[2]
                if 1 in stages:
                    gp.wait_ge(*at("h:o1"))
                gp.dma_start(m["rows"], dram["rows2"]).then_inc(tables_in[2], 16)
                gp.wait_ge(*at("x_mixed2"))
                gp.dma_start(dram["spill"], xT[:, :, :]).then_inc(spilled, 16)
                for t in range(TT):
                    def block(s, at0):
                        gp.tensor_tensor(m["bd"][s].rearrange("p k (h a) -> p k h a", h=8),
                                         m["gT"][:, :, bass.ds(at0, CHUNK)].rearrange("p a k -> p k a").unsqueeze(2)
                                         .to_broadcast([P, CHUNK, 8, 16]),
                                         m["v"]["head_mask"].unsqueeze(1).unsqueeze(3).to_broadcast([P, CHUNK, 8, 16]),
                                         ALU.mult).then_inc(tok_p[t], 1)

                    gp.wait_ge(*at(f"gT_sb{t}"))
                    for s in range(2):
                        block(s, CHUNK * s)
                    with gp.Fori(1, P // CHUNK // 2) as i:
                        for s in range(2):
                            gp.wait_ge(tok_e[t], i * 4 + (2 * s - 3))
                            block(s, i * (2 * CHUNK) + CHUNK * s)
                gp.wait_ge(tok_p[1], P // CHUNK)
                gp.wait_ge(spilled, 16)
                gp.dma_start(xT[:, :, :], dram["spill"]).then_inc(restored, 16)
            if 3 in stages:
                m = A[3]
                if 2 in stages:
                    gp.wait_ge(*at("h:o2"))
                gp.dma_start(m["rows"], dram["rows3"]).then_inc(tables_in[3], 16)
            gp.wait_ge(*at(f"h:o{stages[-1]}"))
            gp.dma_start(dram["out"], xT[:, :, :]).then_inc(stored, 16)
            gp.wait_ge(stored, 16)
        return marks


def shapes(stages):
    _, n = piece_table(stages)
    got = {"stream": (n, P, SLOT), "x": (P, DC, T), "vec": (P, sum(V_LEN[s] for s in stages)), "ident": (P, P)}
    if 1 in stages:
        got["ctx"] = (P, DC, T)
        got["moe"] = (P, sum(k for _, k in MOE_IN))
    for s in stages:
        got[f"rows{s}"] = (P, R_LEN[s])
    return got


def program(new_core, stages):
    known = {}
    for _ in range(2):
        nc = new_core()
        dram = {n: nc.dram_tensor("in_" + n, s, F32, kind="ExternalInput").ap() for n, s in shapes(stages).items()}
        dram["spill"] = nc.dram_tensor("x_spill", (P, DC, T), F32).ap()
        dram["out"] = nc.dram_tensor("out_x", (P, DC, T), F32, kind="ExternalOutput").ap()
        known = build(nc, stages, dram, known)
    return nc


def chan(v):
    return np.ascontiguousarray(v).reshape(-1, P).T


def by_columns(w, step=256):
    k, n = w.shape
    return w.reshape(k // P, P, n // step, step).transpose(2, 1, 0, 3).reshape(n // step, P, -1)


def by_rows(w, rows=2):
    k, n = w.shape
    return w.reshape(k // (rows * P), rows, P, n).transpose(0, 2, 1, 3).reshape(k // (rows * P), P, -1)


def turned(x):
    return np.ascontiguousarray(x.T.reshape(-1, P, x.shape[0]).transpose(1, 0, 2))


def everywhere(v):
    return np.broadcast_to(np.asarray(v).reshape(1, -1), (P, np.asarray(v).size))


def rope_tables(angle, half):
    rot = np.zeros((P, P), np.float32)
    for p in range(P):
        if p % (2 * half) < half:
            rot[p + half, p] = -1.0
        else:
            rot[p - half, p] = 1.0
    return np.cos(angle).astype(np.float32), np.sin(angle).astype(np.float32), rot


def layout1(a):
    D_, W = D, {}
    w_in, b_in = a["w_in"][0], a["b_in"][0]
    order = [(2 * (t // 4) + half) * 4 + t % 4 for t in range(8) for half in range(2)]
    perm = np.concatenate([np.arange(h * HD, (h + 1) * HD) for h in order])
    cut = [0, 1024, 1280, 1536, 2560, 3584, 4608]
    parts = [slice(cut[i], cut[i + 1]) for i in range(6)]
    t = np.arange(T)
    i, j = np.arange(P)[:, None], np.arange(P)[None, :]
    pool = np.zeros((T, 4, T), np.float32)
    for g, w in enumerate((2, 4, 8, 16)):
        for k in range(T):
            lo, hi = max(k - w // 2, 0), min(k + w // 2, T)
            pool[lo:hi, g, k] = np.float32(1.0) / np.float32(hi - lo)
            pool[k, g, k] -= 1.0
    pool = pool.reshape(TT, P, 4, T).transpose(1, 0, 2, 3).reshape(1, P, -1)
    gu, dn = a["w_gu"][0], a["w_down"][0]
    gu = gu.reshape(E_N, DC, P, 2, 8, P).transpose(0, 4, 2, 1, 3, 5).reshape(E_N, 8, P, SLOT)
    dn = dn.reshape(E_N, 4, 2, P, D_).transpose(0, 1, 3, 2, 4).reshape(E_N, 4, P, SLOT)
    W["stream"] = [by_columns(a["w_ada"][0]), by_columns(w_in[:, parts[1]]), by_columns(w_in[:, parts[2]]),
                   by_columns(w_in[:, parts[0]][:, perm]), by_columns(w_in[:, parts[3]]), pool,
                   a["w_pool"][0].reshape(4, 2, P, 256).transpose(2, 0, 1, 3).reshape(1, P, -1),
                   by_columns(w_in[:, parts[4]]), by_columns(w_in[:, parts[5]]),
                   by_columns(a["w_attn_br"][0][perm]), by_columns(a["w_pool_br"][0]), by_columns(a["w_out"][0]),
                   np.concatenate([gu, dn], 1).reshape(12 * E_N, P, SLOT)]
    c2 = np.stack([chan(a["c"][0]), chan(a["c_ctx"])], 2).reshape(P, -1)
    W["vec"] = [c2, chan(a["b_ada"][0]), chan(a["norm1_g"][0]), chan(a["norm2_g"][0]), chan(b_in[parts[0]][perm]),
                chan(b_in[parts[1]]), chan(b_in[parts[4]]), chan(b_in[parts[5]]), chan(a["pool_scale"][0]),
                chan(a["final_g"]), np.full((P, 1), 1e-5, np.float32), everywhere(a["attn_sink"][0][order])]
    p = np.arange(P)
    inv = np.float32(10000.0) ** (-np.arange(16, dtype=np.float32) / np.float32(16))
    pos = np.where((p[:, None] % 64) // 32 == 0, t[None, :] // 64, t[None, :] % 64).astype(np.float32)
    cos, sin, rot = rope_tables(pos * inv[p % 16][:, None], 16)
    mask = np.concatenate([np.where(j <= i, 0, MASKED), np.where(j >= i, 0, MASKED)], 1).astype(np.float32)
    W["rows"] = [cos, sin, rot, mask, everywhere(b_in[parts[2]]), everywhere(b_in[parts[3]]),
                 everywhere(a["b_router"][0]), everywhere(np.arange(32, dtype=np.float32)),
                 a["w_router"][0].reshape(DC, P, 32).transpose(1, 0, 2).reshape(P, -1)]
    sel = np.zeros((P, E_N, P), np.float32)
    for e in range(E_N):
        sel[e, e] = 1.0
    bd = np.zeros((P, D_), np.float32)
    bd[:E_N] = a["b_down"][0]
    bgu = a["b_gu"][0].reshape(E_N * 16, P).T
    W["moe"] = np.concatenate([bgu, bd, sel.reshape(P, -1)], 1)
    W["ctx"] = turned(a["ctx"][0])
    return W


def layout2(a):
    W = {}
    w_in = a["w_in_2"][0]
    names = ["q", "kc", "vc", "ks", "vs", "kw", "vw", "gl", "hq", "hf", "hi", "hg", "merge"]
    widths = [512, 128, 128, 128, 128, 128, 128, 24, 512, 512, 512, 512, 2048]
    at = dict(zip(names, np.cumsum([0] + widths[:-1])))
    col = {n: w_in[:, at[n]:at[n] + w] for n, w in zip(names, widths)}
    perm = np.concatenate([np.arange(h * HD, (h + 1) * HD) for t in range(4) for h in (t, 4 + t)])

    def both(*n):
        return by_columns(np.concatenate([col[k] for k in n], 1))

    def compress(w):
        w = w.reshape(32, HD, P).transpose(1, 0, 2)
        w = np.concatenate([w, w], 0)
        return w.reshape(P, 2, 16 * P).transpose(1, 0, 2)

    def branch(w):
        return by_columns(w, 512)

    keys = a["peer_sub_keys_2"][0].transpose(3, 1, 0, 2).reshape(1, P, -1)
    u = a["peer_u_2"][0].reshape(PE_N, PE_N, DC, P).transpose(0, 3, 2, 1).reshape(PE_N, P, D)
    v = a["peer_v_2"][0].reshape(PE_N, PE_N, D)
    W["stream"] = [by_columns(a["w_ada_2"][0]), both("kc", "vc"), both("ks", "vs"), both("kw", "vw"),
                   by_columns(col["q"][:, perm]), compress(a["w_ck1_2"][0]), compress(a["w_cv1_2"][0]),
                   both("hq"), both("hf"), both("hi"), both("hg"), both("merge"),
                   branch(a["w_branch_2"][0, 0][perm]), branch(a["w_branch_2"][0, 1]), by_columns(a["w_out_2"][0]),
                   by_columns(a["w_peer_q_2"][0]), keys, np.concatenate([u, v], 2)]

    def pos(w):
        w = w.T
        return np.concatenate([w, w], 0)

    head_mask = np.zeros((P, PE_H), np.float32)
    head_mask[np.arange(P), np.arange(P) // 16] = 1.0
    lb = a["hgrn_lb_logits_2"]
    W["vec"] = [chan(a["c_2"][0]), chan(a["b_ada_2"][0]), chan(a["g_mix_2"][0]), chan(a["g_ffn_2"][0]),
                chan(a["g_final_2"]), np.full((P, 1), 1e-6, np.float32), chan(lb[0]), chan(lb[1]),
                chan(a["hgrn_out_norm_2"][0]), pos(a["cmp_pos_k_2"][0]), pos(a["cmp_pos_v_2"][0]),
                everywhere(np.arange(PE_N, dtype=np.float32)), head_mask]
    p, t = np.arange(P), np.arange(T)
    inv = np.float32(10000.0) ** (-np.arange(32, dtype=np.float32) / np.float32(32))
    cos, sin, rot = rope_tables(t.astype(np.float32)[None, :] * inv[p % 32][:, None], 32)
    i, j = np.arange(P)[:, None], np.arange(P)[None, :]
    end = np.arange(16) * 16 + 31
    cmp_mask = np.where(end[None, None, :] <= (i[:, :, None] + P * np.arange(2)[None, :, None]), 0, MASKED)
    reset = np.broadcast_to((t % HG_C != 0).astype(np.float32)[None, :], (P, T))
    hg_mask = np.arange(32)[None, :] >= (p % 32)[:, None]
    w_gl = col["gl"].reshape(DC, P, 24).transpose(1, 0, 2).reshape(P, -1)
    W["rows"] = [cos, sin, rot, np.where(j <= i, 0, MASKED).astype(np.float32),
                 cmp_mask.astype(np.float32).reshape(P, -1), reset, hg_mask.astype(np.float32), w_gl,
                 a["w_ck2_2"][0], a["w_cv2_2"][0]]
    return W


def layout3(a):
    W = {}
    w_in = a["w_in_3"][0]
    up = a["w_up_3"][0].reshape(DC, P, 2, FFC, P).transpose(3, 1, 0, 2, 4).reshape(FFC, P, SLOT)
    W["stream"] = [by_columns(a["w_ada_3"][0]), by_columns(w_in[:, 0:1024]), by_columns(w_in[:, 1024:1536]),
                   by_columns(w_in[:, 1536:3072]), by_columns(a["w_out_3"][0]), up, by_rows(a["w_down_3"][0])]

    def taps(w):
        return np.concatenate([chan(w[k]) for k in range(3)], 1)

    W["vec"] = [chan(a["c_3"][0]), chan(a["b_ada_3"][0]), chan(a["g_mix_3"][0]), chan(a["g_ffn_3"][0]),
                chan(a["g_final_3"]), np.full((P, 1), 1e-6, np.float32), taps(a["conv_w_3"][0]),
                chan(a["conv_b_3"][0]), chan(a["g_attn_out_3"][0]), chan(a["g_conv_out_3"][0]),
                taps(a["ffn_conv_w_3"][0]), chan(a["ffn_conv_b_3"][0])]
    i, j = np.arange(P)[:, None], np.arange(T)[None, :]
    first = np.where(j[:, :P] <= i, j[:, :P] - i, MASKED)
    second = np.where(j <= i + P, j - i - P, MASKED)
    W["rows"] = [first.astype(np.float32), second.astype(np.float32)]
    return W


def arrays(a, stages):
    W = {s: {1: layout1, 2: layout2, 3: layout3}[s](a) for s in stages}
    got = {"in_stream": np.concatenate([w for s in stages for w in W[s]["stream"]], 0),
           "in_x": turned(a["x"][0]), "in_vec": np.concatenate([v for s in stages for v in W[s]["vec"]], 1),
           "in_ident": np.eye(P, dtype=np.float32)}
    if 1 in stages:
        got["in_ctx"], got["in_moe"] = W[1]["ctx"], W[1]["moe"]
    for s in stages:
        got[f"in_rows{s}"] = np.concatenate(W[s]["rows"], 1)
    return {k: np.ascontiguousarray(v) for k, v in got.items()}


STAGES = (1, 2, 3)


def kernel(**inputs):
    from concourse import bacc
    from concourse.bass_utils import run_bass_kernel_spmd

    nc = program(lambda: bacc.Bacc("TRN2", target_bir_lowering=False, num_devices=1), STAGES)
    r = run_bass_kernel_spmd(nc, [arrays(inputs, STAGES)], core_ids=[0])
    out = r.results[0]["out_x"]
    return np.ascontiguousarray(out.transpose(2, 1, 0).reshape(1, T, D))
```

```python
from contextlib import ExitStack

import numpy as np

import concourse.bass as bass
from concourse import mybir

F32 = mybir.dt.float32
F32R = mybir.dt.float32r
U32 = mybir.dt.uint32
I32 = mybir.dt.int32
ALU = mybir.AluOpType
ACT = mybir.ActivationFunctionType
AX_X = mybir.AxisListType.X

P = 128
T = 256
TT = T // P
D = 1024
DC = D // P
HD = 64
SLOTS = 4
SLOT = 2048
SCALE = HD ** -0.5
MASKED = -1e30
SENTINEL = -3e38

E_N = 32
SEATS = 80
CMP = 15
NSA_G = 2
HG_H = 4
HG_C = 32
PE_H = 8
PE_K = 16
PE_N = 128
CHUNK = 4
FF = 2816
FFC = FF // P
A3 = 512

PIECES = {
    1: [("ada1", 24), ("k1", 1), ("v1", 1), ("q1", 4), ("u1", 4), ("pool_m", 1), ("w_pool", 1),
        ("ga", 4), ("gp", 4), ("attn_br", 4), ("pool_br", 4), ("out1", 4), ("moe", 12 * E_N)],
    2: [("ada2", 24), ("kc", 1), ("ksw", 2), ("q2", 2), ("ck", 2), ("cv", 2), ("hq", 2), ("hf", 2),
        ("hi", 2), ("hg", 2), ("merge", 8), ("br_a", 2), ("br_b", 2), ("out2", 4),
        ("peer_q", 8), ("keys", 1), ("peer", PE_N)],
    3: [("ada3", 24), ("qk3", 4), ("v3", 2), ("ucb3", 6), ("out3", 4), ("up", FFC), ("down", FFC // 2)],
}


def ahead(parts, stages):
    parts = {s: list(parts[s]) for s in stages}
    for s in (2, 3):
        if s in stages and s - 1 in stages:
            parts[s - 1].insert(-1, parts[s].pop(0))
    return [x for s in stages for x in parts[s]]


def piece_table(stages):
    first, n = {}, 0
    for name, k in ahead(PIECES, stages):
        first[name] = n
        n += k
    return first, n


VECS = {
    1: [("c", 16), ("b_ada", 48), ("g_mix", 8), ("g_ffn", 8), ("b_q", 8), ("b_k", 2), ("b_ga", 8),
        ("b_gp", 8), ("pool_scale", 8), ("g_final", 8), ("eps", 1), ("sink", 16)],
    2: [("c", 8), ("b_ada", 48), ("g_mix", 8), ("g_ffn", 8), ("g_final", 8), ("eps", 1),
        ("lb0", 4), ("lb1", 4), ("hg_norm", 1), ("pos_k", 32), ("pos_v", 32), ("iota", PE_N),
        ("head_mask", PE_H)],
    3: [("c", 8), ("b_ada", 48), ("g_mix", 8), ("g_ffn", 8), ("g_final", 8), ("eps", 1),
        ("conv_w", 12), ("conv_b", 4), ("g_attn", 4), ("g_conv", 4), ("f_w", 6 * FFC), ("f_b", 2 * FFC)],
}
ROWS = {
    1: [("cos", T), ("sin", T), ("rot", P), ("mask", 2 * P), ("b_v", 256), ("b_u", D), ("b_r", 32),
        ("iota", 32), ("seat", SEATS), ("w_r", DC * 32)],
    2: [("cos", T), ("sin", T), ("rot", P), ("mask", P), ("cmp_mask", 2 * 16), ("reset", T),
        ("hg_mask", 32), ("w_gl", DC * 24), ("w_ck2", HD), ("w_cv2", HD)],
    3: [("dist", 3 * P)],
}
V_LEN = {s: sum(n for _, n in v) for s, v in VECS.items()}
R_LEN = {s: sum(n for _, n in v) for s, v in ROWS.items()}
MOE_IN = [("b_gu", 16 * E_N), ("b_down", D)]


def build(nc, stages, dram, known):
    first_piece, n_pieces = piece_table(stages)
    marks = {}
    ctx = ExitStack()
    with ctx:
        def sb(name, shape, dt=F32):
            return ctx.enter_context(nc.sbuf_tensor(name, shape, dt))

        all_sems = {}

        def sem(name):
            all_sems[name] = ctx.enter_context(nc.semaphore(name))
            return all_sems[name]

        class Signal:

            def __init__(self, name):
                self.name, self.sem, self.n = name, sem(name), 0

            def up(self, *names):
                self.n += 1
                for name in names:
                    assert name not in marks, name
                    marks[name] = (self.name, self.n)
                return self.sem, 1

            def now(self):
                return self.sem, self.n

        sems = {}

        def signal(name):
            if name not in sems:
                sems[name] = Signal(name)
            return sems[name]

        def at(name):
            if not known:
                return anything, 1
            return all_sems[known[name][0]], known[name][1]

        def laid(spec, dt):
            with ExitStack() as scope:
                return [scope.enter_context(nc.sbuf_tensor(name, shape, dt)) for name, shape in spec]

        ring, hT, xT, chunkbuf = laid([("weight_ring", [P, SLOTS, SLOT]), ("hT", [P, DC, T]), ("xT", [P, DC, T]),
                                       ("chunkbuf", [P, 9, CHUNK * PE_N])], F32)
        ring_parts, h_low, v_high, parts = [sb(name, shape, F32R) for name, shape in (
            ("ring_parts", [P, SLOTS, SLOT]), ("h_low", [P, DC, T]), ("v_high", [P, 2, D]),
            ("peer_parts", [P, 9, CHUNK * PE_N]))]
        work = sb("work", [P, 32768])
        h_high = sb("h_high", [P, DC, T], F32R) if 2 in stages else None
        vec = sb("vec", [P, sum(V_LEN[s] for s in stages)])
        ident = sb("ident", [P, P])
        ones = sb("ones", [P, P])
        mods = {s: sb(f"mod{s}", [P, 48, 2 if s == 1 else 1]) for s in stages}
        amps = {s: sb(f"amp{s}", [P, 3, DC]) for s in stages}
        small = sb("small", [P, 256])
        psum = ctx.enter_context(nc.psum_tensor("psum", [P, 8, 512], F32))
        acc = psum[:, 0:4, :].rearrange("p b (a t) -> p (b a) t", a=2)

        class Arena:
            def __init__(self):
                self.at = 0

            def take(self, *shape):
                n = int(np.prod(shape))
                ap = work[:, self.at:self.at + n]
                self.at += n
                assert self.at <= 32768, self.at
                if len(shape) == 2:
                    ap = ap.rearrange("p (a b) -> p a b", a=shape[0])
                if len(shape) == 3:
                    ap = ap.rearrange("p (a b c) -> p a b c", a=shape[0], b=shape[1])
                return ap

        def table(spec, base):
            got, n = {}, 0
            for name, k in spec:
                got[name] = base[:, n:n + k]
                n += k
            return got

        ring_full = [sem(f"ring_full_{s}") for s in range(SLOTS)]
        used = signal("pieces_used")
        ones_set, silu_of_c = signal("ones_set"), signal("silu_of_c")
        tables_in = {s: sem(f"tables_in_{s}") for s in stages}
        moe_in = sem("moe_tables_in")
        x_in = sem("x_in")
        spilled = sem("x_spilled")
        restored = sem("x_restored")
        stored = sem("stored")
        moe_v = sem("moe_vector_steps")
        moe_free = sem("moe_banks_read")
        moe_s = sem("moe_sigmoids")
        nar_v = sem("narrow_vector_steps")
        nar_s = sem("narrow_scalar_steps")
        nar_e = sem("narrow_tokens_gathered")
        tok_v = [sem(f"peer_onehots_{h}") for h in range(TT)]
        tok_p = [sem(f"peer_gate_blocks_{h}") for h in range(TT)]
        tok_e = [sem(f"peer_products_{h}") for h in range(TT)]
        tok_s = [sem(f"peer_copies_{h}") for h in range(TT)]
        blk_a = sem("peer_scores")
        blk_s = sem("peer_gelus")
        blk_uh = sem("peer_u_high")
        blk_ul = sem("peer_u_low")
        blk_v = sem("peer_weights")
        blk_h = sem("peer_v_high")
        blk_w = sem("peer_parts")
        sections = []
        for s in stages:
            for part in ("mix", "ffn"):
                sections.append((s, part))
        sig = {}
        for s, part in sections:
            for eng in ("vector", "scalar", "tensor", "gpsimd"):
                sig[s, part, eng] = signal(f"{eng}_done_{part}{s}")
        if 1 in stages:
            for path in ("narrow", "wide"):
                for eng in ("vector", "scalar", "tensor"):
                    signal(f"{path}_{eng}")
        anything = x_in

        class Banks:
            def __init__(self):
                self.tenant, self.next, self.where, self.turn = [None] * 8, 0, {}, 8

            def open(self, name, b=None):
                if b is None:
                    b = self.next % self.turn
                    self.next += 1
                before, self.tenant[b] = self.tenant[b], name
                self.where[name] = b
                return b, before

        banks = Banks()

        def bank_of(name):
            return psum[:, banks.where[name], :]

        A = {}

        def plan(stage):
            a = Arena()
            m = {}
            m["rows"] = a.take(sum(n for _, n in ROWS[stage]))
            m["r"] = table(ROWS[stage], m["rows"])
            v0 = sum(V_LEN[s] for s in stages if s < stage)
            m["vec"] = vec[:, v0:v0 + V_LEN[stage]]
            m["v"] = table(VECS[stage], m["vec"])
            c0 = {1: 0, 2: 64, 3: 72}[stage]
            m["csil"] = small[:, c0:c0 + (16 if stage == 1 else 8)].rearrange("p (c n) -> p c n", c=DC)
            m["sq"] = a.take(DC, T)
            m["rt"] = a.take(T)
            m["rs"] = a.take(T)
            m["scratch"] = a.at
            m["probs"] = a.take(3, 512)
            m["probsT"] = a.take(2, 512)
            m["sm"] = small[:, 16:16 + 3 * 16].rearrange("p (a b) -> p a b", a=3)
            m["t1"] = a.take(2, T)
            m["t2"] = a.take(2, T)
            m["mod_row"] = [m[k].rearrange("p j t -> p (j t)") for k in ("t1", "t2")]
            m["base"] = a.at
            if stage == 1:
                m["ctxT"] = a.take(DC, T)
                m["hcT"] = a.take(DC, T)
                m["qraw"] = a.take(DC, T)
                m["qT"] = a.take(DC, T)
                m["kraw"] = a.take(2, T)
                m["kT"] = a.take(2, T)
                m["kcT"] = a.take(2, T)
                m["v_x"] = a.take(TT, 256)
                m["v_c"] = a.take(TT, 256)
                m["oT"] = a.take(DC, T)
                m["u"] = a.take(TT, D)
                m["diffT"] = m["ctxT"]
                m["poolT"] = m["hcT"]
                m["siga"] = m["qraw"]
                m["sigp"] = m["sq"]
                m["merged"] = a.take(DC, T)
                m["tmp"] = a.take(2, T)
                a.at = m["base"]
                m["moe_tables"] = a.take(sum(n for _, n in MOE_IN))
                m.update(table(MOE_IN, m["moe_tables"]))
                for name in ("gateT", "selT", "count", "g", "l", "l2", "gl2", "gated", "sg"):
                    m[name] = a.take(T)
                m["over"], m["flag"] = a.take(1), a.take(1).bitcast(I32)
                m["seatT"] = m["g"]
                m["gate"], m["logit"], m["hot"] = a.take(TT, E_N), a.take(TT, E_N), a.take(TT, E_N)
                m["top"], m["top_f"], m["top_e"] = a.take(TT, 8), a.take(TT, 8), a.take(TT, 4)
                m["top_i"] = a.take(TT, 8).bitcast(U32)
                m["top_n"], m["top_s"], m["top_r"] = a.take(TT), a.take(TT), a.take(TT)
                m["seat_of"] = a.take(TT, E_N)
                m["paths"] = a.at
                m["gb"] = a.take(E_N, T)
                m["act"] = a.take(8, T)
                a.at = m["paths"]
                m["x_nat"] = a.take(TT, D)
                m["enter"] = a.take(TT, (E_N + 1) * SEATS).rearrange("p t (e k) -> p t e k", k=SEATS)
                m["leave"] = a.take(E_N + 1, T)
                m["xe"] = m["sq"].rearrange("p c t -> p (c t)")[:, 0:2 * DC * SEATS] \
                    .rearrange("p (n c k) -> p n c k", n=2, c=DC)
                m["act_e"] = a.take(8, SEATS)
                m["y_e"] = a.take(D)
                q = TT * 8 * SEATS
                m["gated_enter"] = [work[:, m["scratch"] + i * q:m["scratch"] + (i + 1) * q]
                                    .rearrange("p (t e k) -> p t e k", t=TT, k=SEATS) for i in range(2)]
            if stage == 2:
                m["qraw"] = a.take(4, T)
                m["qT"] = a.take(4, T)
                m["kraw"] = a.take(3, T)
                m["kT"] = a.take(3, T)
                m["vcT"] = a.take(1, T)
                m["v_s"] = a.take(TT, P)
                m["v_w"] = a.take(TT, P)
                m["gl"] = a.take(TT, 24)
                m["hid"] = a.take(4, 16)
                m["hbias"] = a.take(4, 1)
                m["kcmp"] = a.take(16)
                m["vcmp"] = a.take(2, HD)
                m["pc"] = a.take(16, 16)
                m["pcT"] = a.take(16, P)
                m["oT"] = a.take(4, T)
                m["qg"] = a.take(4, T)
                m["siga"] = a.take(8, T)
                m["fg"], m["kg"] = m["siga"][:, 0:4, :], m["siga"][:, 4:8, :]
                m["bcum"] = a.take(4, T)
                m["eb"] = a.take(4, T)
                m["qdec"] = a.take(4, T)
                m["kinv"] = a.take(4, T)
                m["kendT"] = a.take(4, T)
                m["kend"] = a.take(TT, 512)
                m["hv"] = a.take(TT, 512)
                m["Asb"] = a.take(8, 32)
                m["S"] = a.take(8, 512)
                m["win"] = m["S"][:, 0:2, :].rearrange("p k (l n) -> p k l n", n=16)
                m["hid_rows"] = m["S"][:, 2, :].rearrange("p (k o) -> p k o", k=2)
                m["hoT"] = a.take(4, T)
                m["hgs"] = m["qg"]
                m["sigp"] = m["sq"]
                m["merged"] = m["S"].rearrange("p a (b c) -> p (a b) c", c=T)[:, 0:8, :]
                m["tmp"] = m["t2"]
                m["cmp_s"] = small[:, 144:240].rearrange("p (a b) -> p a b", a=6)
                a.at = m["base"]
                m["pqT"] = a.take(16, T)
                m["sc"] = a.take(TT, 16, PE_N)
                m["v16"] = a.take(TT, 16, 16)
                m["i16"] = a.take(TT, 16, 16).bitcast(U32)
                m["cut"], m["cut2"] = a.take(PE_N), a.take(256)
                m["idx"] = a.take(TT, 2, P)
                m["sel"] = a.take(TT, 2048)
                m["w8"], m["w8b"], m["zs"] = a.take(TT, 8, 8), a.take(8), a.take(2, 8)
                assert a.at <= 32768 - 4096
                m["pgate"] = work[:, 32768 - 4096:32768].rearrange("p (t k) -> p t k", t=TT)
                m["G"] = work[:, :].rearrange("p (t k) -> p t k", t=T)
                m["gT"] = xT[:, :, :].rearrange("p c t -> p (c t)").rearrange("p (a t) -> p a t", a=16)
                cb = [chunkbuf[:, i, :].rearrange("p (k n) -> p k n", k=CHUNK) for i in range(8)]
                m["oh1"], m["oh2"], m["bd"], m["rr"] = cb[0:2], cb[2:4], cb[4:6], cb[6:8]
                m["idxT"] = chunkbuf[:, 8, :].rearrange("p (q t) -> p q t", q=2)
                m["wt"] = chunkbuf[:, 0, :].rearrange("p (k t) -> p k t", k=2)
                m["ge"] = chunkbuf[:, 1, :].rearrange("p (k t) -> p k t", k=2)
                m["zero"] = chunkbuf[:, 2, 0:P]
                m["h_low"] = h_low[:, :, :]
                m["u_high"] = parts[:, 5:9, :].rearrange("p a b -> p (a b)") \
                    .rearrange("p (k d) -> p k d", k=2)
                m["wt_high"] = parts[:, 3, :].rearrange("p (k t) -> p k t", k=2)
                m["wt_low"] = parts[:, 4, :].rearrange("p (k t) -> p k t", k=2)
                m["v_high"] = v_high
            if stage == 3:
                m["qk"] = a.take(8, T)
                m["v_x"] = a.take(TT, A3)
                m["ssb"] = a.take(3, T)
                m["oT"] = a.take(4, T)
                m["ug"] = a.take(4, T)
                m["cx"] = a.take(4, T + 2)
                m["bg"] = a.take(4, T)
                m["cv"] = a.take(4, T)
                m["mixed"] = a.take(8, T)
                m["up"] = a.take(4, 2, T + 2)
                m["ffa"] = a.take(2, T)
                m["ffs"] = a.take(2, T)
                m["ffc"] = a.take(2, 2, T)
                m["act"] = a.take(FFC, T)
            return m

        for s in stages:
            A[s] = plan(s)

        def mod_cols(s, k, n=0):
            return mods[s][:, 8 * k:8 * k + 8, n]

        block = ctx.enter_context(nc.Block())

        @block.tensor
        def _(pe):
            def bank(name, b=None):
                b, before = banks.open(name, b)
                if before is not None:
                    pe.wait_ge(*at("free:" + before))
                return psum[:, b, :]

            def piece(name, i=0):
                n = first_piece[name] + i
                pe.wait_ge(ring_full[n % SLOTS], 16 * (n // SLOTS + 1))
                return ring[:, n % SLOTS, :]

            def modulation(s, E, m):
                n = 2 if s == 1 else 1
                csil = A[s]["csil"]
                pe.wait_ge(*at(f"csil{s}"))
                whole = bank(f"mod{s}", 7)

                def turned_row(k):
                    pe.wait_ge(*at(f"mod_row{s}:{k}"))
                    for j in range(4):
                        at0 = (4 * k + j) * n
                        mm = pe.transpose(whole[:, at0:at0 + n], m["mod_row"][k % 2][0:n, j * P:(j + 1) * P],
                                          ident[0:n, 0:n])
                    mm.then_inc(*E.up(f"mod_turned{s}:{k}", *([f"mod{s}"] if k == 11 else [])))

                for k in range(12):
                    ps = bank(f"mod{s}:{k}", 5 + k % 2)
                    for h in range(2):
                        w = piece(f"ada{s}", 2 * k + h).rearrange("p (c o) -> p c o", c=DC)
                        for c in range(DC):
                            mm = pe.matmul(ps[0:n, h * 256:(h + 1) * 256], csil[:, c, :], w[:, c, :],
                                           start=(h == 0 and c == 0), stop=True, skip_group_check=True)
                        mm.then_inc(*used.up(*([f"mod{s}:{k}"] if h else [])))
                    if k:
                        turned_row(k - 1)
                turned_row(11)

            def mean_square(tag, E, sq, chunks):
                pe.wait_ge(*at(f"sq:{tag}"))
                ps = bank(f"ms:{tag}")
                for c in range(chunks):
                    mm = pe.matmul(ps[:, 0:T], ones[:, :], sq[:, c, :], start=(c == 0), stop=(c == chunks - 1))
                mm.then_inc(*E.up(f"ms:{tag}"))

            def pair(w, ps, moving, chunks=DC):
                for j in range(2):
                    for c in range(chunks):
                        mm = pe.matmul(ps[:, j * T:(j + 1) * T], w[:, c, j * P:(j + 1) * P], moving[:, c, :],
                                       start=(j == 0 and c == 0), stop=True, skip_group_check=True)
                return mm

            def columns(tag, i, moving):
                ps = bank(f"{tag}:{i}")
                w = piece(tag, i).rearrange("p (c o) -> p c o", c=DC)
                pair(w, ps, moving).then_inc(*used.up(f"{tag}:{i}"))

            def natural(w, ps, moving, width):
                for t in range(TT):
                    for c in range(DC):
                        mm = pe.matmul(ps[:, t * width:(t + 1) * width], moving[:, c, t * P:(t + 1) * P],
                                       w[:, c, 0:width], start=(t == 0 and c == 0), stop=True,
                                       skip_group_check=True)
                return mm

            def rotate(tag, E, m, raw, n0, n):
                pe.wait_ge(*at(f"raw:{tag}"))
                ps = bank(f"rot:{tag}")
                pe.matmul(ps[:, 0:n * T], m["r"]["rot"], raw[:, n0:n0 + n, :], start=True, stop=True) \
                  .then_inc(*E.up(f"rot:{tag}"))

            def scores(s, u, E, m):
                tile, half, qt = u // 4, u // 2 % 2, u % 2
                lo, hi = half * HD, half * HD + HD
                nk = P * (qt + 1)
                ps = bank(f"S{s}:{u}")
                q = (m["qk"] if s == 3 else m["qT"])[lo:hi, tile, qt * P:(qt + 1) * P]
                if s == 1:
                    k, kc = m["kT"][lo:hi, tile // 4, :], m["kcT"][lo:hi, tile // 4, :]
                    pe.matmul(ps[:, 0:T], q, k, start=True, stop=True, skip_group_check=True)
                    pe.matmul(ps[:, T:2 * T], q, kc, start=False, stop=True, skip_group_check=True)
                    far = (1 - qt) * P
                    mm = pe.matmul(ps[:, far:far + P], ident[:, :], m["r"]["mask"][:, qt * P:(qt + 1) * P],
                                   start=False, stop=True, skip_group_check=True)
                if s == 2:
                    for b in range(2):
                        pe.matmul(ps[:, b * nk:(b + 1) * nk], q, m["kT"][lo:hi, 1 + b, 0:nk],
                                  start=(b == 0), stop=True, skip_group_check=True)
                    for b in range(2):
                        at0 = b * nk + qt * P
                        mm = pe.matmul(ps[:, at0:at0 + P], ident[:, :], m["r"]["mask"],
                                       start=False, stop=True, skip_group_check=True)
                if s == 3:
                    mm = pe.matmul(ps[:, 0:nk], q, m["qk"][lo:hi, 4 + tile, 0:nk], start=True, stop=True)
                mm.then_inc(*E.up(f"S{s}:{u}"))

            def blocks_of_keys(s, u):
                return 4 if s == 1 else (2 * (u % 2 + 1) if s == 2 else u % 2 + 1)

            def turn(s, u, E, m):
                pe.wait_ge(*at(f"P{s}:{u}"))
                ps = bank(f"T{s}:{u}")
                for b in range(blocks_of_keys(s, u)):
                    mm = pe.transpose(ps[:, b * P:(b + 1) * P], m["probs"][:, u % 3, b * P:(b + 1) * P], ident[:, :])
                mm.then_inc(*E.up(f"T{s}:{u}"))

            def values(s, u, E, m):
                tile, half, qt = u // 4, u // 2 % 2, u % 2
                lo, hi = half * HD, half * HD + HD
                pe.wait_ge(*at(f"PT{s}:{u}"))
                if u % 4 == 0:
                    bank(f"O{s}:{tile}", 6 + tile % 2)
                ps = bank_of(f"O{s}:{tile}")
                o = ps[lo:hi, qt * P:(qt + 1) * P]
                vs = []
                if s == 1:
                    g = 2 * (tile // 4) + half
                    vs = [m["v_x"][:, b, g * HD:(g + 1) * HD] for b in range(2)]
                    vs += [m["v_c"][:, b, g * HD:(g + 1) * HD] for b in range(2)]
                if s == 2:
                    for name in ("v_s", "v_w"):
                        vs += [m[name][:, b, lo:hi] for b in range(qt + 1)]
                if s == 3:
                    h = 2 * tile + half
                    vs = [m["v_x"][:, b, h * HD:(h + 1) * HD] for b in range(qt + 1)]
                for b, v in enumerate(vs):
                    mm = pe.matmul(o, v, m["probsT"][:, u % 2, b * P:(b + 1) * P],
                                   start=(b == 0 and qt == 0), stop=True, skip_group_check=True)
                if s == 2:
                    mm = pe.matmul(o, m["vcmp"][:, half, :], m["pcT"][:, u, :], start=False, stop=True,
                                   skip_group_check=True)
                mm.then_inc(*E.up(f"O{s}:{u}"))

            def attention(s, units, E, m):
                banks.turn = 6
                for i in range(units + 3):
                    if i < units:
                        scores(s, i, E, m)
                    if 0 <= i - 2 < units:
                        turn(s, i - 2, E, m)
                    if 0 <= i - 3 < units:
                        values(s, i - 3, E, m)
                banks.turn = 8

            def drain():
                for b in range(8):
                    if banks.tenant[b] is not None:
                        pe.wait_ge(*at("free:" + banks.tenant[b]))

            def mix1():
                m, E = A[1], sig[1, "mix", "tensor"]
                pe.wait_ge(tables_in[1], 32)
                mean_square("x1", E, m["sq"], DC)
                modulation(1, E, m)
                mean_square("ctx", E, m["sq"], DC)
                pe.wait_ge(*at("h:x1"))
                pe.wait_ge(*at("h:ctx"))
                w = piece("k1").rearrange("p (c o) -> p c o", c=DC)
                pair(w, bank("k1x"), hT).then_inc(*E.up("k1x"))
                pair(w, bank("k1c"), m["hcT"]).then_inc(*used.up("k1c"))
                w = piece("v1").rearrange("p (c o) -> p c o", c=DC)
                natural(w, bank("v1x"), hT, 256).then_inc(*E.up("v1x"))
                natural(w, bank("v1c"), m["hcT"], 256).then_inc(*used.up("v1c"))
                for i in range(4):
                    columns("q1", i, hT)
                rotate("k1", E, m, m["kraw"], 0, 2)
                for i in range(4):
                    rotate(f"q1:{i}", E, m, m["qraw"], 2 * i, 2)
                pe.wait_ge(*at("qT1"))
                pe.wait_ge(*at("v1c_sb"))
                attention(1, 32, E, m)
                for i in range(4):
                    ps = bank(f"u1:{i}")
                    w = piece("u1", i).rearrange("p (c o) -> p c o", c=DC)
                    natural(w, ps, hT, 256).then_inc(*used.up(f"u1:{i}"))
                w = piece("pool_m").rearrange("p (t g k) -> p t g k", t=TT, g=4)
                pe.wait_ge(*at("u1_sb"))
                for g in range(4):
                    ps = bank(f"diff:{g}")
                    for j in range(2):
                        for t in range(TT):
                            mm = pe.matmul(ps[:, j * T:(j + 1) * T], m["u"][:, t, g * 256 + j * P:g * 256 + (j + 1) * P],
                                           w[:, t, g, :], start=(j == 0 and t == 0), stop=True, skip_group_check=True)
                    mm.then_inc(*(used.up(f"diff:{g}") if g == 3 else E.up(f"diff:{g}")))
                w = piece("w_pool").rearrange("p (g c o) -> p g c o", g=4, c=2)
                for g in range(4):
                    pe.wait_ge(*at(f"diff_sb:{g}"))
                    ps = bank(f"pooled:{g}")
                    for j in range(2):
                        for c in range(2):
                            mm = pe.matmul(ps[:, j * T:(j + 1) * T], w[:, g, c, j * P:(j + 1) * P],
                                           m["diffT"][:, 2 * g + c, :], start=(j == 0 and c == 0), stop=True,
                                           skip_group_check=True)
                    mm.then_inc(*(used.up(f"pooled:{g}") if g == 3 else E.up(f"pooled:{g}")))
                for i in range(4):
                    columns("ga", i, hT)
                for i in range(4):
                    columns("gp", i, hT)
                pe.wait_ge(*at("oT1"))
                for i in range(4):
                    columns("attn_br", i, m["oT"])
                pe.wait_ge(*at("poolT"))
                for i in range(4):
                    columns("pool_br", i, m["poolT"])
                pe.wait_ge(*at("merged1"))
                for i in range(4):
                    columns("out1", i, m["merged"])

            def narrow(m):
                E = signal("narrow_tensor")
                banks.tenant = [None] * 8
                pe.wait_ge(*at("seatT"))
                ps = bank("seat_of", 4)
                for t in range(TT):
                    mm = pe.transpose(ps[:, t * E_N:(t + 1) * E_N], m["seatT"][0:E_N, t * P:(t + 1) * P],
                                      ident[0:E_N, 0:E_N])
                mm.then_inc(*E.up("seat_of"))

                def gather(e):
                    for h in range(2):
                        for c in range(4):
                            for t in range(TT):
                                moving = m["enter"][:, t, 0, :] if e is None else \
                                    m["enter"][:, t, bass.ds(e, 1), :].rearrange("p a k -> p (a k)")
                                mm = pe.matmul(psum[:, 6 + h, c * SEATS:(c + 1) * SEATS],
                                               m["x_nat"][:, t, (4 * h + c) * P:(4 * h + c + 1) * P], moving,
                                               start=(c == 0 and t == 0), stop=True, skip_group_check=True)
                    mm.then_inc(nar_e, 1)

                def scatter(e):
                    for c in range(DC):
                        mm = pe.matmul(acc[:, c, :], m["y_e"][0:SEATS, c * P:(c + 1) * P],
                                       m["leave"][0:SEATS, bass.ds(e, 1), :].rearrange("p a t -> p (a t)"),
                                       start=False, stop=False, skip_group_check=True)
                    return mm

                pe.wait_ge(*at("enter"))
                pe.wait_ge(*at("x_nat_sb"))
                for k in range(E_N // 2):
                    if k % 4 == 0:
                        pe.wait_ge(*at(f"gated_enter:{k // 4}"))
                    ps = bank(f"leave:{k}", (4, 6, 7, 5)[k % 4])
                    for j in range(2):
                        for t in range(TT):
                            mm = pe.transpose(ps[0:SEATS, (2 * j + t) * P:(2 * j + t + 1) * P],
                                              m["gated_enter"][k // 4 % 2][:, t, (2 * k + j) % 8, :], ident[:, :])
                    mm.then_inc(*E.up(f"leave:{k}"))
                for k in range(12, 16):
                    pe.wait_ge(*at(f"free:leave:{k}"))
                gather(None)
                base = first_piece["moe"]
                pe.wait_ge(nar_s, 4)
                with pe.Fori(0, E_N) as e:
                    for j in range(8):
                        n = base + j
                        pe.wait_ge(ring_full[n % SLOTS], e * 48 + 16 * (n // SLOTS + 1))
                        if j >= 2:
                            pe.wait_ge(nar_v, e * 40 + (5 * (j - 2) + 2))
                        w = ring[:, n % SLOTS, :].rearrange("p (c o) -> p c o", c=DC)
                        for q in range(2):
                            for c in range(DC):
                                mm = pe.matmul(psum[:, 4 + j % 2, q * SEATS:(q + 1) * SEATS],
                                               w[:, c, q * P:(q + 1) * P],
                                               m["xe"][:, bass.ds(e % 2, 1), c, :].rearrange("p n k -> p (n k)"),
                                               start=(q == 0 and c == 0), stop=True, skip_group_check=True)
                        mm.then_inc(used.sem, 1)
                        if j == 1:
                            pe.wait_ge(nar_s, e * 12 + 4)
                            scatter(e)
                            gather(e + 1)
                    pe.wait_ge(nar_s, e * 12 + 8)
                    for k in range(4):
                        n = base + 8 + k
                        pe.wait_ge(ring_full[n % SLOTS], e * 48 + 16 * (n // SLOTS + 1))
                        pe.wait_ge(nar_v, e * 40 + 5 * (2 * k + 2))
                        w = ring[:, n % SLOTS, :].rearrange("p (f o) -> p f o", f=2)
                        for f in range(2):
                            for h in range(2):
                                mm = pe.matmul(psum[0:SEATS, 6 + h, :], m["act_e"][:, 2 * k + f, :],
                                               w[:, f, h * 512:(h + 1) * 512],
                                               start=(k == 0 and f == 0), stop=(k == 3 and f == 1))
                        mm.then_inc(used.sem, 1)
                pe.wait_ge(nar_s, 12 * E_N + 4)
                scatter(E_N).then_inc(nar_e, 1)

            def wide(m):
                E = signal("wide_tensor")
                banks.tenant = [None] * 8
                for i in range(E_N // 2):
                    ps = bank(f"gb:{i}", 4 + i % 4)
                    for j in range(2):
                        e = 2 * i + j
                        mm = pe.matmul(ps[:, j * T:(j + 1) * T], ident[0:E_N, e:e + 1].to_broadcast([E_N, P]),
                                       m["gateT"][0:E_N, :], start=(j == 0), stop=True, skip_group_check=True)
                    mm.then_inc(*E.up(f"gb:{i}"))
                for i in range(12, 16):
                    pe.wait_ge(*at(f"free:gb:{i}"))
                base = first_piece["moe"]
                with pe.Fori(0, E_N) as e:
                    for j in range(8):
                        n = base + j
                        pe.wait_ge(ring_full[n % SLOTS], e * 48 + 16 * (n // SLOTS + 1))
                        pe.wait_ge(moe_free, e * 8 + j + 1)
                        w = ring[:, n % SLOTS, :].rearrange("p (c o) -> p c o", c=DC)
                        pair(w, psum[:, 4 + j % 4, :], hT).then_inc(used.sem, 1)
                    for k in range(4):
                        n = base + 8 + k
                        pe.wait_ge(ring_full[n % SLOTS], e * 48 + 16 * (n // SLOTS + 1))
                        pe.wait_ge(moe_v, e * 40 + 5 * (2 * k + 2))
                        w = ring[:, n % SLOTS, :].rearrange("p (f o) -> p f o", f=2)
                        for f in range(2):
                            for c in range(DC):
                                mm = pe.matmul(acc[:, c, :], w[:, f, c * P:(c + 1) * P], m["act"][:, 2 * k + f, :],
                                               start=False, stop=False, skip_group_check=True)
                        mm.then_inc(used.sem, 1)

            def moe():
                m, E = A[1], sig[1, "ffn", "tensor"]
                mean_square("f1", E, m["sq"], DC)
                pe.wait_ge(*at("h:f1"))
                ps = bank("router")
                w = m["r"]["w_r"].rearrange("p (c e) -> p c e", c=DC)
                natural(w, ps, hT, E_N).then_inc(*E.up("router"))
                if 2 in stages:
                    modulation(2, E, m)
                pe.wait_ge(*at("gates"))
                ps = bank("gateT")
                for t in range(TT):
                    mm = pe.transpose(ps[0:E_N, t * P:(t + 1) * P], m["gate"][:, t, :], ident[:, :])
                mm.then_inc(*E.up("gateT"))
                for i in range(4):
                    ps = bank(f"x_nat:{i}")
                    for j in range(4):
                        t, c = i // 2, 4 * (i % 2) + j
                        mm = pe.transpose(ps[:, j * P:(j + 1) * P], hT[:, c, t * P:(t + 1) * P], ident[:, :])
                    mm.then_inc(*E.up(f"x_nat:{i}"))
                pe.wait_ge(*at("over"))
                ps = bank("flag")
                pe.matmul(ps[0:1, 0:1], m["over"][0:E_N, :], ones[0:E_N, 0:1], start=True, stop=True) \
                  .then_inc(*E.up("flag"))
                drain()
                pe.wait_ge(*at("gateT_sb"))
                pe.wait_ge(moe_in, 16)
                for c in range(DC):
                    mm = pe.matmul(acc[:, c, :], m["b_down"][0:E_N, c * P:(c + 1) * P], m["gateT"][0:E_N, :],
                                   start=(c % 2 == 0), stop=False, skip_group_check=True)
                mm.then_inc(*E.up("y_started"))
                pe.wait_ge(*at("flag_set"))
                crowded = pe.value_load(m["flag"][0:1, :])
                with pe.If(crowded == 0):
                    narrow(m)
                with pe.Else():
                    wide(m)
                used.n += 12 * E_N
                banks.tenant = ["moe_y"] * 4 + [None] * 4
                mean_square("o1", E, m["sq"], DC)

            def mix2():
                m, E = A[2], sig[2, "mix", "tensor"]
                pe.wait_ge(tables_in[2], 16)
                if 1 not in stages:
                    modulation(2, E, m)
                mean_square("x2", E, m["sq"], DC)
                pe.wait_ge(*at("h:x2"))
                columns("kc", 0, hT)
                for i in range(2):
                    w = piece("ksw", i).rearrange("p (c o) -> p c o", c=DC)
                    ps = bank(f"ks:{i}")
                    for c in range(DC):
                        mm = pe.matmul(ps[:, 0:T], w[:, c, 0:P], hT[:, c, :], start=(c == 0), stop=True,
                                       skip_group_check=True)
                    for t in range(TT):
                        for c in range(DC):
                            mm = pe.matmul(ps[:, T + t * P:T + (t + 1) * P], hT[:, c, t * P:(t + 1) * P], w[:, c, P:2 * P],
                                           start=False, stop=True, skip_group_check=True)
                    mm.then_inc(*used.up(f"ks:{i}"))
                for i in range(2):
                    columns("q2", i, hT)
                natural(m["r"]["w_gl"].rearrange("p (c o) -> p c o", c=DC), bank("gl"), hT, 24).then_inc(*E.up("gl"))
                rotate("k2a", E, m, m["kraw"], 0, 2)
                rotate("k2b", E, m, m["kraw"], 2, 1)
                for i in range(2):
                    rotate(f"q2:{i}", E, m, m["qraw"], 2 * i, 2)
                pe.wait_ge(*at("windows"))
                for kv, name in enumerate(("ck", "cv")):
                    w = [piece(name, i).rearrange("p (l o) -> p l o", l=16) for i in range(2)]
                    ps = bank(f"hid:{kv}:0"), bank(f"hid:{kv}:1")
                    for l in range(32):
                        for g in range(2):
                            lo, hi = g * HD, g * HD + HD
                            mm = pe.matmul(ps[g][0:16, 0:P], m["win"][lo:hi, kv, l, :], w[l // 16][lo:hi, l % 16, :],
                                           start=(l == 0), stop=(l == 31))
                        if l == 15:
                            mm.then_inc(*used.up())
                    mm.then_inc(*used.up(f"hid:{kv}"))
                pe.wait_ge(*at("hid_rows:1"))
                ps = bank("hidT")
                for i in range(4):
                    mm = pe.transpose(ps[:, i * 16:(i + 1) * 16], m["hid_rows"][0:16, i // 2, i % 2 * P:(i % 2 + 1) * P],
                                      ident[0:16, 0:16])
                mm.then_inc(*E.up("hidT"))
                pe.wait_ge(*at("hidden"))
                ps = bank("kcmp")
                for g in range(2):
                    mm = pe.matmul(ps[g * HD:g * HD + HD, 0:CMP], m["r"]["w_ck2"], m["hid"][:, g, 0:CMP], start=True,
                                   stop=True, skip_group_check=True)
                mm.then_inc(*E.up("kcmp"))
                ps = bank("vcmp")
                for g in range(2):
                    mm = pe.matmul(ps[0:CMP, g * HD:(g + 1) * HD], m["hid"][:, 2 + g, 0:CMP], m["r"]["w_cv2"],
                                   start=(g == 0), stop=True, skip_group_check=True)
                mm.then_inc(*E.up("vcmp"))
                pe.wait_ge(*at("kcmp_sb"))
                ps0, ps1 = bank("cmpS"), bank("cmpS1")
                for u in range(16):
                    tile, half, qt = u // 4, u // 2 % 2, u % 2
                    lo, hi = half * HD, half * HD + HD
                    dst = ps0 if half == 0 else ps1
                    mm = pe.matmul(dst[:, u * 16:u * 16 + CMP], m["qT"][lo:hi, tile, qt * P:(qt + 1) * P],
                                   m["kcmp"][lo:hi, 0:CMP], start=(u in (0, 2)), stop=True, skip_group_check=True)
                mm.then_inc(*E.up("cmpS"))
                pe.wait_ge(*at("pc"))
                for i in range(4):
                    ps = bank(f"pcT:{i}")
                    for j in range(4):
                        mm = pe.transpose(ps[0:CMP, j * P:(j + 1) * P], m["pc"][:, 4 * i + j, 0:CMP], ident[:, :])
                    mm.then_inc(*E.up(f"pcT:{i}"))
                pe.wait_ge(*at("pcT_sb"))
                attention(2, 16, E, m)
                for tag in ("hq", "hf"):
                    for i in range(2):
                        columns(tag, i, hT)
                for i in range(2):
                    ps = bank(f"hi:{i}")
                    natural(piece("hi", i).rearrange("p (c o) -> p c o", c=DC), ps, hT, 256).then_inc(*used.up(f"hi:{i}"))
                for i in range(2):
                    columns("hg", i, hT)
                pe.wait_ge(*at("kend"))
                for t in range(TT):
                    ps = bank(f"kendT:{t}")
                    for h in range(HG_H):
                        mm = pe.transpose(ps[:, h * P:(h + 1) * P], m["kendT"][:, h, t * P:(t + 1) * P], ident[:, :])
                    mm.then_inc(*E.up(f"kendT:{t}"))
                pe.wait_ge(*at("hg_ready"))
                ps = bank("A")
                for h in range(HG_H):
                    for c in range(8):
                        r = 32 * (c % 4)
                        col = (h * 2 + c // 4) * 32
                        mm = pe.matmul(ps[r:r + 32, col:col + 32], m["kinv"][:, h, c * 32:(c + 1) * 32],
                                       m["qdec"][:, h, c * 32:(c + 1) * 32], start=(h == 0 and c // 4 == 0),
                                       stop=True, skip_group_check=True)
                mm.then_inc(*E.up("A"))
                pe.wait_ge(*at("kend_sb"))
                for c in range(7):
                    r = 32 * (c % 4)
                    ps = bank(f"KV:{c}")
                    for h in range(HG_H):
                        mm = pe.matmul(ps[:, h * P:(h + 1) * P], m["kend"][r:r + 32, c // 4, h * P:(h + 1) * P],
                                       m["hv"][r:r + 32, c // 4, h * P:(h + 1) * P], start=(h == 0), stop=True,
                                       skip_group_check=True, tile_position=(r, 0))
                    mm.then_inc(*E.up(f"KV:{c}"))
                pe.wait_ge(*at("A_sb"))
                pe.wait_ge(*at("S:7"))
                intra = [bank(f"hoA:{r}") for r in range(4)]
                for h in range(HG_H):
                    for c in range(8):
                        r = 32 * (c % 4)
                        at0 = (h * 2 + c // 4) * 32
                        mm = pe.matmul(intra[c % 4][:, at0:at0 + 32],
                                       m["hv"][r:r + 32, c // 4, h * P:(h + 1) * P],
                                       m["Asb"][r:r + 32, h * 2 + c // 4, :], start=(h == 0 and c // 4 == 0), stop=True,
                                       skip_group_check=True, tile_position=(r, 0))
                mm.then_inc(*E.up("hoA"))
                for i in range(2):
                    ps = bank(f"ho:{i}")
                    for j in range(2):
                        h = 2 * i + j
                        for c in range(1, 8):
                            mm = pe.matmul(ps[:, j * T + c * 32:j * T + (c + 1) * 32], m["S"][:, c, h * P:(h + 1) * P],
                                           m["qdec"][:, h, c * 32:(c + 1) * 32], start=(j == 0 and c == 1),
                                           stop=True, skip_group_check=True)
                    mm.then_inc(*E.up(f"ho:{i}"))
                pe.wait_ge(*at("ho_sq"))
                for i in range(2):
                    ps = bank(f"hms:{i}")
                    pe.matmul(ps[:, :], ones[:, :], m["eb"][:, 2 * i:2 * i + 2, :], start=True, stop=True) \
                      .then_inc(*E.up(f"hms:{i}"))
                for i in range(8):
                    columns("merge", i, hT)
                for tag, src in (("br_a", m["oT"]), ("br_b", m["hoT"])):
                    pe.wait_ge(*at("oT2" if tag == "br_a" else "hoT"))
                    for i in range(2):
                        w = piece(tag, i).rearrange("p (c o) -> p c o", c=4)
                        for k in range(2):
                            ps = bank(f"{tag}:{2 * i + k}")
                            mm = pair(w[:, :, k * 256:(k + 1) * 256], ps, src, 4)
                            mm.then_inc(*(used.up(f"{tag}:{2 * i + k}") if k else E.up(f"{tag}:{2 * i + k}")))
                pe.wait_ge(*at("merged2"))
                for i in range(4):
                    columns("out2", i, m["merged"])

            def peer():
                m, E = A[2], sig[2, "ffn", "tensor"]
                mean_square("f2", E, m["sq"], DC)
                pe.wait_ge(*at("h:f2"))
                for i in range(8):
                    columns("peer_q", i, hT)
                w = piece("keys").rearrange("p (j k) -> p j k", j=16)
                for i in range(8):
                    pe.wait_ge(*at(f"pq_sb:{i}"))
                    ps = bank(f"ps:{i}")
                    for j in range(2):
                        for t in range(TT):
                            mm = pe.matmul(ps[:, (j * TT + t) * P:(j * TT + t + 1) * P],
                                           m["pqT"][:, 2 * i + j, t * P:(t + 1) * P], w[:, 2 * i + j, :],
                                           start=(j == 0 and t == 0), stop=True, skip_group_check=True)
                    mm.then_inc(*(used.up(f"ps:{i}") if i == 7 else E.up(f"ps:{i}")))
                if 3 in stages:
                    modulation(3, E, m)
                pe.wait_ge(*at("idx"))
                ps = bank("idxT")
                for p in range(2):
                    for t in range(TT):
                        mm = pe.transpose(ps[:, p * T + t * P:p * T + (t + 1) * P], m["idx"][:, t, p, :], ident[:, :])
                mm.then_inc(*E.up("idxT"))
                pe.wait_ge(*at("idxT_sb"))
                for t in range(TT):
                    pe.wait_ge(*at(f"pgate:{t}"))
                    for i in range(4):
                        ps = bank(f"gT{t}:{i}")
                        for j in range(4):
                            a = 4 * i + j
                            mm = pe.transpose(ps[:, j * P:(j + 1) * P],
                                              m["pgate"][:, t, a * P:(a + 1) * P],
                                              ident[:, :])
                        mm.then_inc(*E.up(f"gT{t}:{i}"))
                    drain()
                    n = P // CHUNK
                    oh1, oh2, bd, rr = m["oh1"], m["oh2"], m["bd"], m["rr"]

                    def rows(s):
                        for k in range(CHUNK):
                            mm = pe.matmul(psum[:, s, k * P:(k + 1) * P], bd[s][:, k, :], oh2[s][:, k, :],
                                           start=(k == 0), stop=True, skip_group_check=True)
                        mm.then_inc(tok_e[t], 1)

                    def gates(s):
                        for k in range(CHUNK):
                            mm = pe.matmul(psum[:, 2 + s, k * P:(k + 1) * P], rr[s][:, k, :], oh1[s][:, k, :],
                                           start=(k == 0), stop=True, skip_group_check=True)
                        mm.then_inc(tok_e[t], 1)

                    for c in range(2):
                        pe.wait_ge(tok_v[t], 2 * c + 1)
                        pe.wait_ge(tok_p[t], c + 1)
                        rows(c)
                    pe.wait_ge(tok_s[t], 1)
                    pe.wait_ge(tok_v[t], 2)
                    gates(0)
                    with pe.Fori(1, n // 2) as i:
                        for s in range(2):
                            pe.wait_ge(tok_v[t], i * 4 + (2 * s + 1))
                            pe.wait_ge(tok_p[t], i * 2 + (s + 1))
                            pe.wait_ge(tok_s[t], i * 4 + (2 * s - 3))
                            rows(s)
                            pe.wait_ge(tok_s[t], i * 4 + (2 * s - 2))
                            pe.wait_ge(tok_v[t], i * 4 + 2 * s)
                            gates(1 - s)
                    pe.wait_ge(tok_s[t], 2 * n - 2)
                    pe.wait_ge(tok_v[t], 2 * n)
                    gates((n - 1) % 2)
                    for b in range(4):
                        banks.tenant[b] = f"G{t}"
                    for b in range(4, 8):
                        banks.tenant[b] = None
                drain()
                pe.wait_ge(*at("zero"))
                for b in range(4):
                    mm = pe.matmul(psum[:, b, :], m["zero"], hT[:, 0:2, :], start=True, stop=False,
                                   skip_group_check=True)
                mm.then_inc(*E.up("zeroed"))
                base = first_piece["peer"]

                def scores_of(s):
                    low = ring_parts[:, (base + s) % SLOTS, 0:D]
                    high = m["u_high"][:, s % 2, :]
                    for k, (u, h) in enumerate(((high, h_high), (high, m["h_low"]), (low, h_high))):
                        for c in range(DC):
                            mm = pe.matmul(psum[:, 4 + s % 4, 0:T], u[:, c * P:(c + 1) * P], h[:, c, :],
                                           start=(k == 0 and c == 0), stop=True, skip_group_check=True)
                    mm.then_inc(blk_a, 1)

                def values_of(s):
                    low = ring_parts[:, (base + s) % SLOTS, D:2 * D]
                    high = m["v_high"][:, s % 2, :]
                    for v, wt in ((high, "wt_high"), (high, "wt_low"), (low, "wt_high")):
                        for c in range(DC):
                            mm = pe.matmul(acc[:, c, :], v[:, c * P:(c + 1) * P], m[wt][:, s % 2, :], start=False,
                                           stop=False, skip_group_check=True)
                    mm.then_inc(used.sem, 1)

                pe.wait_ge(*at("h_parts"))
                pe.wait_ge(blk_ul, 1)
                scores_of(0)
                with pe.Fori(0, PE_N // 4 - 1) as i:
                    for s in range(4):
                        pe.wait_ge(blk_ul, i * 4 + (s + 2))
                        scores_of(s + 1)
                        pe.wait_ge(blk_w, i * 12 + 3 * (s + 1))
                        values_of(s)
                for s in range(4):
                    k = PE_N - 4 + s
                    if s < 3:
                        pe.wait_ge(blk_ul, k + 2)
                        scores_of(s + 1)
                    pe.wait_ge(blk_w, 3 * (k + 1))
                    values_of(s)
                used.n += PE_N
                marks["peer_y"] = (used.name, used.n)
                for b in range(4):
                    banks.tenant[b] = "peer_y"
                mean_square("o2", E, m["sq"], DC)

            def mix3():
                m, E = A[3], sig[3, "mix", "tensor"]
                pe.wait_ge(tables_in[3], 16)
                if 2 not in stages:
                    modulation(3, E, m)
                mean_square("x3", E, m["sq"], DC)
                pe.wait_ge(*at("h:x3"))
                for i in range(4):
                    columns("qk3", i, hT)
                for i in range(2):
                    ps = bank(f"v3:{i}")
                    natural(piece("v3", i).rearrange("p (c o) -> p c o", c=DC), ps, hT, 256).then_inc(*used.up(f"v3:{i}"))
                pe.wait_ge(*at("qk3_sb"))
                pe.wait_ge(*at("v3_sb"))
                attention(3, 16, E, m)
                for i in range(6):
                    columns("ucb3", i, hT)
                mean_square("attn3", E, m["sq"][:, 0:4, :], 4)
                mean_square("conv3", E, m["sq"][:, 4:8, :], 4)
                pe.wait_ge(*at("h:attn3"))
                pe.wait_ge(*at("h:conv3"))
                for i in range(4):
                    columns("out3", i, m["mixed"])

            def ffn3():
                m, E = A[3], sig[3, "ffn", "tensor"]
                mean_square("f3", E, m["sq"], DC)
                pe.wait_ge(*at("h:f3"))
                for i in range(FFC):
                    columns("up", i, hT)
                drain()
                for i in range(FFC // 2):
                    pe.wait_ge(*at(f"act:{2 * i + 1}"))
                    w = piece("down", i).rearrange("p (f o) -> p f o", f=2)
                    for f in range(2):
                        for c in range(DC):
                            mm = pe.matmul(acc[:, c, :], w[:, f, c * P:(c + 1) * P], m["act"][:, 2 * i + f, :],
                                           start=(i == 0 and f == 0 and c % 2 == 0), stop=True, skip_group_check=True)
                    mm.then_inc(*used.up(*(["ffn_y"] if i == FFC // 2 - 1 else [])))
                for b in range(4):
                    banks.tenant[b] = "ffn_y"
                mean_square("o3", E, m["sq"], DC)

            pe.wait_ge(x_in, 48)
            pe.wait_ge(*at("ones"))
            if 1 in stages:
                mix1()
                moe()
            if 2 in stages:
                mix2()
                peer()
            if 3 in stages:
                mix3()
                ffn3()

        @block.sync
        def _(sp):
            stream = dram["stream"]
            for s in range(SLOTS):
                sp.dma_start(ring[:, s, :], stream[s]).then_inc(ring_full[s], 16)
            with sp.Fori(1, n_pieces // SLOTS) as i:
                for s in range(SLOTS):
                    sp.wait_ge(used.sem, i * SLOTS + (s - SLOTS + 1))
                    sp.dma_start(ring[:, s, :], stream[i * SLOTS + s]).then_inc(ring_full[s], 16)
            for n in range(n_pieces // SLOTS * SLOTS, n_pieces):
                sp.wait_ge(used.sem, n - SLOTS + 1)
                sp.dma_start(ring[:, n % SLOTS, :], stream[n]).then_inc(ring_full[n % SLOTS], 16)

        @block.vector
        def _(ve):
            def tt(V, out, a, b, op, *names):
                ve.tensor_tensor(out, a, b, op).then_inc(*V.up(*names))

            def ts(V, out, a, s1, s2, op0, op1, *names):
                if s2 is None:
                    ve.tensor_scalar(out, a, s1, None, op0).then_inc(*V.up(*names))
                else:
                    ve.tensor_scalar(out, a, s1, s2, op0, op1).then_inc(*V.up(*names))

            def wait_own(V):
                ve.wait_ge(*V.now())

            def modulation(s, V, m):
                n = 2 if s == 1 else 1
                ve.wait_ge(*at(f"mod{s}"))
                ps = bank_of(f"mod{s}")[:, 0:48 * n].rearrange("p (j n) -> p j n", n=n)
                tt(V, mods[s][:, :, :], ps, m["v"]["b_ada"].unsqueeze(2).to_broadcast([P, 48, n]), ALU.add, f"free:mod{s}")
                wait_own(V)
                for k, (col, g, j) in enumerate(((1, "g_mix", 0), (4, "g_ffn", 0), (1, "g_mix", n - 1))):
                    ve.scalar_tensor_tensor(amps[s][:, k, :], mod_cols(s, col, j), 1.0, m["v"][g], ALU.add, ALU.mult) \
                      .then_inc(*V.up())
                wait_own(V)

            def norm(tag, V, m, src, dst, gain, shift, chunks=DC, sq=None):
                sq = m["sq"] if sq is None else sq
                ve.wait_ge(*at(f"rt:{tag}"))
                ve.reciprocal(m["rs"], m["rt"]).then_inc(*V.up())
                wait_own(V)
                tt(V, sq[:, 0:chunks, :], src, m["rs"].unsqueeze(1).to_broadcast([P, chunks, T]), ALU.mult)
                wait_own(V)
                for c in range(chunks):
                    last = [f"h:{tag}"] if c == chunks - 1 else []
                    if shift is None:
                        ts(V, dst[:, c, :], sq[:, c, :], gain[:, c:c + 1], None, ALU.mult, None, *last)
                    else:
                        ts(V, dst[:, c, :], sq[:, c, :], gain[:, c:c + 1], shift[:, c:c + 1], ALU.mult, ALU.add, *last)

            def halves(ap):
                return ap.rearrange("p (j t) -> p j t", j=2)

            def rope(tag, V, m, raw, dst, n0, n, *names):
                ve.wait_ge(*at(f"rot:{tag}"))
                wait_own(V)
                ps = bank_of(f"rot:{tag}")[:, 0:n * T].rearrange("p (j t) -> p j t", j=n)
                cos = m["r"]["cos"].unsqueeze(1).to_broadcast([P, n, T])
                sin = m["r"]["sin"].unsqueeze(1).to_broadcast([P, n, T])
                tt(V, m["t1"][:, 0:n, :], raw[:, n0:n0 + n, :], cos, ALU.mult)
                tt(V, m["t2"][:, 0:n, :], ps, sin, ALU.mult, f"free:rot:{tag}")
                wait_own(V)
                tt(V, dst[:, n0:n0 + n, :], m["t1"][:, 0:n, :], m["t2"][:, 0:n, :], ALU.add, *names)

            def softmax_a(s, u, V, m):
                qt = u % 2
                nk = P * (qt + 1)
                c = m["sm"][:, u % 3, :]
                ps = bank_of(f"S{s}:{u}")
                ve.wait_ge(*at(f"S{s}:{u}"))
                if u >= 3:
                    wait_own(V)
                if s == 1:
                    ve.tensor_reduce(c[:, 0:1], ps, AX_X, ALU.max).then_inc(*V.up())
                    wait_own(V)
                    ts(V, c[:, 1:2], c[:, 0:1], SCALE, m["v"]["sink"][:, u // 2:u // 2 + 1], ALU.mult, ALU.max)
                    wait_own(V)
                    ts(V, c[:, 2:3], c[:, 1:2], -1.0, None, ALU.mult, None, f"max{s}:{u}")
                if s == 2:
                    ve.tensor_reduce(c[:, 0:2], ps[:, 0:2 * nk].rearrange("p (b k) -> p b k", b=2), AX_X, ALU.max) \
                      .then_inc(*V.up())
                    wait_own(V)
                    ts(V, c[:, 2:4], c[:, 0:2], -SCALE, None, ALU.mult, None, f"max{s}:{u}")
                if s == 3:
                    h = 2 * (u // 4) + u // 2 % 2
                    slope = 2.0 ** (-(h + 1)) / SCALE
                    dist = m["r"]["dist"][:, 0:P] if qt == 0 else m["r"]["dist"][:, P:3 * P]
                    if u >= 3:
                        ve.wait_ge(*at(f"exp{s}:{u - 3}"))
                    ve.scalar_tensor_tensor(m["ssb"][:, u % 3, 0:nk], dist, slope, ps[:, 0:nk], ALU.mult, ALU.add) \
                      .then_inc(*V.up(f"free:S{s}:{u}"))
                    wait_own(V)
                    ve.tensor_reduce(c[:, 0:1], m["ssb"][:, u % 3, 0:nk], AX_X, ALU.max).then_inc(*V.up())
                    wait_own(V)
                    ts(V, c[:, 2:3], c[:, 0:1], -SCALE, None, ALU.mult, None, f"max{s}:{u}")

            def softmax_b(s, u, V, m):
                nk = P * (u % 2 + 1)
                c = m["sm"][:, u % 3, :]
                p = m["probs"][:, u % 3, :]
                ve.wait_ge(*at(f"exp{s}:{u}"))
                if s == 1:
                    tt(V, c[:, 5:6], c[:, 4:5], c[:, 6:7], ALU.add)
                    wait_own(V)
                    ve.reciprocal(c[:, 7:8], c[:, 5:6]).then_inc(*V.up())
                    wait_own(V)
                    ts(V, p, p, c[:, 7:8], None, ALU.mult, None, f"P{s}:{u}")
                if s == 2:
                    h = 4 * (u // 2 % 2) + u // 4
                    ts(V, c[:, 9:11], c[:, 4:6], 1e-30, None, ALU.max, None)
                    wait_own(V)
                    ve.reciprocal(c[:, 7:9], c[:, 9:11]).then_inc(*V.up())
                    wait_own(V)
                    g = m["gl"][:, u % 2, 3 * h:3 * h + 3]
                    tt(V, c[:, 11:13], c[:, 7:9], g[:, 1:3], ALU.mult)
                    wait_own(V)
                    for b in range(2):
                        ts(V, p[:, b * nk:(b + 1) * nk], p[:, b * nk:(b + 1) * nk], c[:, 11 + b:12 + b], None,
                           ALU.mult, None, *([f"P{s}:{u}"] if b else []))
                if s == 3:
                    ve.reciprocal(c[:, 7:8], c[:, 4:5]).then_inc(*V.up())
                    wait_own(V)
                    ts(V, p[:, 0:nk], p[:, 0:nk], c[:, 7:8], None, ALU.mult, None, f"P{s}:{u}")

            def attention(s, units, V, m):
                for i in range(units + 5):
                    if i < units:
                        softmax_a(s, i, V, m)
                    if 0 <= i - 1 < units:
                        softmax_b(s, i - 1, V, m)
                    k = i - 5
                    if 0 <= k < units and k % 4 == 3:
                        ve.wait_ge(*at(f"O{s}:{k}"))
                        ve.tensor_copy(m["oT"][:, k // 4, :], bank_of(f"O{s}:{k // 4}")[:, 0:T]) \
                          .then_inc(*V.up(f"free:O{s}:{k // 4}", *([f"oT{s}"] if k == units - 1 else [])))

            def gated(s, V, m, a, b, na, nb):
                for i in range(4):
                    ve.wait_ge(*at(f"{a}:{i}"))
                    ve.wait_ge(*at(f"{na}:3"))
                    tt(V, m["merged"][:, 2 * i:2 * i + 2, :], m["siga"][:, 2 * i:2 * i + 2, :],
                       halves(bank_of(f"{a}:{i}")), ALU.mult, f"free:{a}:{i}")
                for i in range(4):
                    ve.wait_ge(*at(f"{b}:{i}"))
                    ve.wait_ge(*at(f"{nb}:3"))
                    wait_own(V)
                    tt(V, m["tmp"], m["sigp"][:, 2 * i:2 * i + 2, :], halves(bank_of(f"{b}:{i}")), ALU.mult,
                       f"free:{b}:{i}")
                    wait_own(V)
                    tt(V, m["merged"][:, 2 * i:2 * i + 2, :], m["merged"][:, 2 * i:2 * i + 2, :], m["tmp"], ALU.add,
                       *([f"merged{s}"] if i == 3 else []))

            def residual(s, tag, V, gate, n0=None):
                for i in range(4):
                    ve.wait_ge(*at(f"{tag}:{i}"))
                    ps = bank_of(f"{tag}:{i}")
                    for j in range(2):
                        c = 2 * i + j
                        names = ([f"free:{tag}:{i}"] if j else []) + ([f"x_mixed{s}"] if c == 7 else [])
                        ve.scalar_tensor_tensor(xT[:, c, :], ps[:, j * T:(j + 1) * T], gate[:, c:c + 1], xT[:, c, :],
                                                ALU.mult, ALU.add).then_inc(*V.up(*names))

            def residual_sum(s, tag, V, gate):
                for c in range(DC):
                    names = [f"x_out{s}", f"free:{tag}"] if c == 7 else []
                    ve.scalar_tensor_tensor(xT[:, c, :], acc[:, c, :], gate[:, c:c + 1], xT[:, c, :],
                                            ALU.mult, ALU.add).then_inc(*V.up(*names))

            def mix1():
                m, V = A[1], sig[1, "mix", "vector"]
                ve.wait_ge(tables_in[1], 32)
                modulation(1, V, m)
                norm("x1", V, m, xT[:, :, :], hT, amps[1][:, 0, :], mod_cols(1, 0))
                norm("ctx", V, m, m["ctxT"], m["hcT"], amps[1][:, 2, :], mod_cols(1, 0, 1))
                for tag, src, dst in (("v1x", "v1x", "v_x"), ("v1c", "v1c", "v_c")):
                    ve.wait_ge(*at(src))
                    tt(V, m[dst], bank_of(src).rearrange("p (t o) -> p t o", t=TT),
                       m["r"]["b_v"].unsqueeze(1).to_broadcast([P, TT, 256]), ALU.add, f"free:{src}", f"{tag}_sb")
                rope("k1", V, m, m["kraw"], m["kT"], 0, 2)
                for i in range(4):
                    rope(f"q1:{i}", V, m, m["qraw"], m["qT"], 2 * i, 2, *(["qT1"] if i == 3 else []))
                attention(1, 32, V, m)
                for i in range(4):
                    ve.wait_ge(*at(f"u1:{i}"))
                    tt(V, m["u"][:, :, i * 256:(i + 1) * 256], bank_of(f"u1:{i}").rearrange("p (t o) -> p t o", t=TT),
                       m["r"]["b_u"][:, i * 256:(i + 1) * 256].unsqueeze(1).to_broadcast([P, TT, 256]), ALU.add,
                       f"free:u1:{i}", *(["u1_sb"] if i == 3 else []))
                for g in range(4):
                    ve.wait_ge(*at(f"diff:{g}"))
                    ve.tensor_copy(m["diffT"][:, 2 * g:2 * g + 2, :], halves(bank_of(f"diff:{g}"))) \
                      .then_inc(*V.up(f"free:diff:{g}", f"diff_sb:{g}"))
                for g in range(4):
                    ve.wait_ge(*at(f"pooled:{g}"))
                    for j in range(2):
                        c = 2 * g + j
                        ts(V, m["poolT"][:, c, :], bank_of(f"pooled:{g}")[:, j * T:(j + 1) * T],
                           m["v"]["pool_scale"][:, c:c + 1], None, ALU.mult, None,
                           *([f"free:pooled:{g}"] if j else []), *(["poolT"] if c == 7 else []))
                gated(1, V, m, "attn_br", "pool_br", "siga1", "sigp1")
                residual(1, "out1", V, mod_cols(1, 2))

            def narrow(m):
                V = signal("narrow_vector")
                ve.wait_ge(*at("seat_of"))
                ve.tensor_copy(m["seat_of"], bank_of("seat_of")[:, 0:TT * E_N].rearrange("p (t e) -> p t e", t=TT)) \
                  .then_inc(*V.up("free:seat_of"))
                ve.memset(m["enter"][:, :, E_N, :], 0.0).then_inc(*V.up())
                ve.memset(m["leave"][0:SEATS, 0, :], 0.0).then_inc(*V.up())
                wait_own(V)
                for t in range(TT):
                    tt(V, m["enter"][:, t, 0:E_N, :], m["r"]["seat"].unsqueeze(1).to_broadcast([P, E_N, SEATS]),
                       m["seat_of"][:, t, :].unsqueeze(2).to_broadcast([P, E_N, SEATS]), ALU.is_equal,
                       *(["enter"] if t else []))
                wait_own(V)
                for i in range(4):
                    if i >= 2:
                        ve.wait_ge(*at(f"leave:{4 * i - 5}"))
                    for t in range(TT):
                        tt(V, m["gated_enter"][i % 2][:, t, :, :], m["enter"][:, t, 8 * i:8 * i + 8, :],
                           m["gate"][:, t, 8 * i:8 * i + 8].unsqueeze(2).to_broadcast([P, 8, SEATS]), ALU.mult,
                           *([f"gated_enter:{i}"] if t else []))
                bias = m["b_gu"]
                base = first_piece["moe"]
                g, l, l2, gl2, sg = [m[name][:, 0:SEATS] for name in ("g", "l", "l2", "gl2", "sg")]
                with ve.Fori(0, E_N) as e:
                    for j in range(8):
                        ps = psum[:, 4 + j % 2, :]
                        k = 5 * j
                        done = base + j + 1
                        ve.wait_ge(used.sem, e * 12 + done)
                        ve.tensor_scalar(g, ps[:, 0:SEATS], bias[:, bass.ds(e * 16 + j, 1)], 7.0, ALU.add, ALU.min) \
                          .then_inc(nar_v, 1)
                        ve.tensor_scalar(l, ps[:, SEATS:2 * SEATS], bias[:, bass.ds(e * 16 + (8 + j), 1)], 7.0,
                                         ALU.add, ALU.min).then_inc(nar_v, 1)
                        ve.wait_ge(nar_v, e * 40 + (k + 2))
                        ve.tensor_scalar(l2, l, -7.0, 1.0, ALU.max, ALU.add).then_inc(nar_v, 1)
                        ve.wait_ge(nar_v, e * 40 + (k + 3))
                        ve.tensor_tensor(gl2, g, l2, ALU.mult).then_inc(nar_v, 1)
                        ve.wait_ge(nar_v, e * 40 + (k + 4))
                        ve.wait_ge(nar_s, e * 12 + (j + 5 + (2 if j > 1 else 0)))
                        ve.tensor_tensor(m["act_e"][:, j, :], gl2, sg, ALU.mult).then_inc(nar_v, 1)
                ve.wait_ge(nar_e, E_N + 2)

            def wide(m):
                for k in range(4):
                    ve.memset(small[:, 240 + k:241 + k], 0.0).then_inc(moe_free, 1)
                ve.wait_ge(*at("gb_sb"))
                bias = m["b_gu"]
                base = first_piece["moe"]
                with ve.Fori(0, E_N) as e:
                    for j in range(8):
                        ps = psum[:, 4 + j % 4, :]
                        k = 5 * j
                        ve.wait_ge(used.sem, e * 12 + (base + j + 1))
                        ve.tensor_scalar(m["g"], ps[:, 0:T], bias[:, bass.ds(e * 16 + j, 1)], 7.0, ALU.add, ALU.min) \
                          .then_inc(moe_v, 1)
                        ve.tensor_scalar(m["l"], ps[:, T:2 * T], bias[:, bass.ds(e * 16 + (8 + j), 1)], 7.0,
                                         ALU.add, ALU.min).then_inc(moe_free, 1)
                        ve.wait_ge(moe_free, e * 8 + (4 + j + 1))
                        ve.tensor_scalar(m["l2"], m["l"], -7.0, 1.0, ALU.max, ALU.add).then_inc(moe_v, 1)
                        ve.wait_ge(moe_v, e * 40 + (k + 2))
                        ve.tensor_tensor(m["gl2"], m["g"], m["l2"], ALU.mult).then_inc(moe_v, 1)
                        ve.wait_ge(moe_v, e * 40 + (k + 3))
                        ve.tensor_tensor(m["gated"], m["gl2"], m["gb"][:, bass.ds(e, 1), :].rearrange("p a t -> p (a t)"),
                                         ALU.mult).then_inc(moe_v, 1)
                        ve.wait_ge(moe_v, e * 40 + (k + 4))
                        ve.wait_ge(moe_s, e * 8 + j + 1)
                        ve.tensor_tensor(m["act"][:, j, :], m["gated"], m["sg"], ALU.mult).then_inc(moe_v, 1)
                ve.wait_ge(moe_v, 40 * E_N)
                ve.wait_ge(used.sem, base + 12 * E_N)

            def moe():
                m, V = A[1], sig[1, "ffn", "vector"]
                norm("f1", V, m, xT[:, :, :], hT, amps[1][:, 1, :], mod_cols(1, 3))
                ve.wait_ge(*at("router"))
                logit = m["logit"]
                tt(V, logit, bank_of("router")[:, 0:TT * E_N].rearrange("p (t e) -> p t e", t=TT),
                   m["r"]["b_r"].unsqueeze(1).to_broadcast([P, TT, E_N]), ALU.add, "free:router")
                wait_own(V)
                top, idx, idf = m["top"], m["top_i"], m["top_f"]
                for t in range(TT):
                    ve.max(top[:, t, :], logit[:, t, :]).then_inc(*V.up())
                wait_own(V)
                for t in range(TT):
                    ve.max_index(idx[:, t, :], top[:, t, :], logit[:, t, :]).then_inc(*V.up())
                ts(V, m["top_n"], top[:, :, 0], -1.0, None, ALU.mult, None, "top_n")
                wait_own(V)
                ve.tensor_copy(idf, idx).then_inc(*V.up())
                ve.wait_ge(*at("top_exp"))
                ve.reciprocal(m["top_r"], m["top_s"]).then_inc(*V.up())
                wait_own(V)
                tt(V, m["top_e"], m["top_e"], m["top_r"].unsqueeze(2).to_broadcast([P, TT, 4]), ALU.mult)
                wait_own(V)
                for k in range(4):
                    for t in range(TT):
                        ts(V, m["hot"][:, t, :] if k else m["gate"][:, t, :], m["r"]["iota"], idf[:, t, k:k + 1],
                           m["top_e"][:, t, k:k + 1], ALU.is_equal, ALU.mult)
                    wait_own(V)
                    if k:
                        tt(V, m["gate"], m["gate"], m["hot"], ALU.add, *(["gates"] if k == 3 else []))
                        wait_own(V)
                ve.wait_ge(*at("gateT"))
                ps = bank_of("gateT")[0:E_N, 0:T]
                ts(V, m["selT"][0:E_N, :], ps, 0.0, None, ALU.is_gt, None)
                ve.tensor_copy(m["gateT"][0:E_N, :], ps).then_inc(*V.up("free:gateT", "gateT_sb"))
                wait_own(V)
                ve.tensor_tensor_scan(m["count"][0:E_N, :], ones[0:E_N, 0:1].to_broadcast([E_N, T]),
                                      m["selT"][0:E_N, :], 0.0, ALU.mult, ALU.add).then_inc(*V.up())
                wait_own(V)
                ts(V, m["over"][0:E_N, :], m["count"][0:E_N, T - 1:T], float(SEATS), None, ALU.is_gt, None, "over")
                tt(V, m["seatT"][0:E_N, :], m["count"][0:E_N, :], m["selT"][0:E_N, :], ALU.mult, "seatT")
                if 2 in stages:
                    modulation(2, V, A[2])
                ve.wait_ge(*at("flag"))
                ve.tensor_copy(m["flag"][0:1, :], bank_of("flag")[0:1, 0:1]).then_inc(*V.up("free:flag", "flag_set"))
                wait_own(V)
                ve.wait_ge(moe_in, 16)
                crowded = ve.value_load(m["flag"][0:1, :])
                with ve.If(crowded == 0):
                    narrow(m)
                with ve.Else():
                    wide(m)
                residual_sum(1, "moe_y", V, mod_cols(1, 5))
                norm("o1", V, m, xT[:, :, :], xT, m["v"]["g_final"], None)

            def mix2():
                m, V = A[2], sig[2, "mix", "vector"]
                ve.wait_ge(tables_in[2], 16)
                if 1 not in stages:
                    modulation(2, V, m)
                ve.memset(m["vcmp"], 0.0).then_inc(*V.up())
                ve.memset(m["pcT"], 0.0).then_inc(*V.up())
                norm("x2", V, m, xT[:, :, :], hT, amps[2][:, 0, :], mod_cols(2, 0))
                ve.wait_ge(*at("kc:0"))
                ps = bank_of("kc:0")
                ve.tensor_copy(m["kraw"][:, 0, :], ps[:, 0:T]).then_inc(*V.up())
                ve.tensor_copy(m["vcT"][:, 0, :], ps[:, T:2 * T]).then_inc(*V.up("free:kc:0", "vcT"))
                for i, v in enumerate(("v_s", "v_w")):
                    ve.wait_ge(*at(f"ks:{i}"))
                    ps = bank_of(f"ks:{i}")
                    ve.tensor_copy(m["kraw"][:, 1 + i, :], ps[:, 0:T]).then_inc(*V.up(*(["raw:k2a"] if i == 0 else ["raw:k2b"])))
                    ve.tensor_copy(m[v], ps[:, T:2 * T].rearrange("p (t o) -> p t o", t=TT)) \
                      .then_inc(*V.up(f"free:ks:{i}", f"{v}_sb"))
                rope("k2a", V, m, m["kraw"], m["kT"], 0, 2)
                rope("k2b", V, m, m["kraw"], m["kT"], 2, 1)
                wait_own(V)
                for kv, (src, pos) in enumerate(((m["kT"][:, 0, :], "pos_k"), (m["vcT"][:, 0, :], "pos_v"))):
                    win = m["win"][:, kv, :, :]
                    for half in range(2):
                        at0 = 16 * half
                        ve.tensor_copy(win[:, at0:at0 + 16, 0:CMP],
                                       src[:, at0:at0 + 16 * CMP].rearrange("p (b l) -> p l b", l=16)).then_inc(*V.up())
                    ve.tensor_copy(win[:, :, CMP], m["v"][pos]).then_inc(*V.up(*(["windows"] if kv else [])))
                for i in range(2):
                    rope(f"q2:{i}", V, m, m["qraw"], m["qT"], 2 * i, 2, *(["qT2"] if i == 1 else []))
                ve.wait_ge(*at("kcmp"))
                ve.tensor_copy(m["kcmp"][:, 0:CMP], bank_of("kcmp")[:, 0:CMP]).then_inc(*V.up("free:kcmp", "kcmp_sb"))
                ve.wait_ge(*at("vcmp"))
                ve.tensor_copy(m["vcmp"][0:CMP, :, :], bank_of("vcmp")[0:CMP, 0:P].rearrange("p (g d) -> p g d", g=2)) \
                  .then_inc(*V.up("free:vcmp"))
                ve.wait_ge(*at("cmpS"))
                cm = m["r"]["cmp_mask"].rearrange("p (t n) -> p t n", t=2)
                pc = m["pc"]
                for half in range(2):
                    src = bank_of("cmpS" if half == 0 else "cmpS1")[:, 0:256].rearrange("p (u n) -> p u n", n=16)
                    for tile in range(4):
                        u = 4 * tile + 2 * half
                        ve.scalar_tensor_tensor(pc[:, u:u + 2, 0:CMP], src[:, u:u + 2, 0:CMP], SCALE, cm[:, :, 0:CMP],
                                                ALU.mult, ALU.add) \
                          .then_inc(*V.up(*(["free:cmpS" if half == 0 else "free:cmpS1"] if tile == 3 else [])))
                wait_own(V)
                q = m["cmp_s"]
                ve.tensor_reduce(q[:, 0, :], pc[:, :, 0:CMP], AX_X, ALU.max).then_inc(*V.up())
                wait_own(V)
                ts(V, q[:, 1, :], q[:, 0, :], -1e20, None, ALU.max, None)
                wait_own(V)
                tt(V, pc[:, :, 0:CMP], pc[:, :, 0:CMP], q[:, 1, :].unsqueeze(2).to_broadcast([P, 16, CMP]),
                   ALU.subtract, "pc_raw")
                ve.wait_ge(*at("pc_exp"))
                ve.tensor_reduce(q[:, 2, :], pc[:, :, 0:CMP], AX_X, ALU.add).then_inc(*V.up())
                wait_own(V)
                ts(V, q[:, 3, :], q[:, 2, :], 1e-30, None, ALU.max, None)
                wait_own(V)
                ve.reciprocal(q[:, 4, :], q[:, 3, :]).then_inc(*V.up())
                wait_own(V)
                for u in range(16):
                    h = 4 * (u // 2 % 2) + u // 4
                    ts(V, q[:, 5, u:u + 1], q[:, 4, u:u + 1], m["gl"][:, u % 2, 3 * h:3 * h + 1], None, ALU.mult, None)
                wait_own(V)
                tt(V, pc[:, :, 0:CMP], pc[:, :, 0:CMP], q[:, 5, :].unsqueeze(2).to_broadcast([P, 16, CMP]), ALU.mult, "pc")
                for i in range(4):
                    ve.wait_ge(*at(f"pcT:{i}"))
                    ve.tensor_copy(m["pcT"][0:CMP, 4 * i:4 * i + 4, :],
                                   bank_of(f"pcT:{i}")[0:CMP, :].rearrange("p (u t) -> p u t", u=4)) \
                      .then_inc(*V.up(f"free:pcT:{i}", *(["pcT_sb"] if i == 3 else [])))
                attention(2, 16, V, m)
                lb, one_lb = small[:, 128:132], small[:, 132:136]
                tt(V, small[:, 136:140], m["v"]["lb0"], m["v"]["lb1"], ALU.subtract, "lb_diff")
                ve.wait_ge(*at("lb"))
                ts(V, one_lb, lb, -1.0, 1.0, ALU.mult, ALU.add)
                ve.wait_ge(*at("hf:sig"))
                wait_own(V)
                for h in range(4):
                    ts(V, m["fg"][:, h, :], m["kg"][:, h, :], one_lb[:, h:h + 1], lb[:, h:h + 1], ALU.mult, ALU.add,
                       *(["fg"] if h == 3 else []))
                wait_own(V)
                ts(V, m["kg"], m["fg"], -1.0, 1.0, ALU.mult, ALU.add)
                ve.wait_ge(*at("logf"))
                for h in range(4):
                    ve.tensor_tensor_scan(m["bcum"][:, h, :], m["r"]["reset"], m["eb"][:, h, :], 0.0, ALU.mult, ALU.add) \
                      .then_inc(*V.up())
                wait_own(V)
                b4 = m["bcum"].rearrange("p h (c k) -> p (h c) k", k=32)
                tt(V, m["kendT"].rearrange("p h (c k) -> p (h c) k", k=32),
                   b4[:, :, 31:32].to_broadcast([P, 32, 32]), b4, ALU.subtract, "bcum")
                ve.wait_ge(*at("eb"))
                tt(V, m["qdec"], m["qg"], m["eb"], ALU.mult)
                ve.wait_ge(*at("einv"))
                tt(V, m["kinv"], m["kg"], m["fg"], ALU.mult, "hg_ready")
                ve.wait_ge(*at("eend"))
                tt(V, m["kendT"], m["kg"], m["kendT"], ALU.mult, "kend")
                for i in range(2):
                    ve.wait_ge(*at(f"hi:{i}"))
                    ve.tensor_copy(m["hv"][:, :, i * 256:(i + 1) * 256],
                                   bank_of(f"hi:{i}").rearrange("p (t o) -> p t o", t=TT)).then_inc(*V.up(f"free:hi:{i}"))
                for t in range(TT):
                    ve.wait_ge(*at(f"kendT:{t}"))
                    ve.tensor_copy(m["kend"][:, t, :], bank_of(f"kendT:{t}")) \
                      .then_inc(*V.up(f"free:kendT:{t}", *(["kend_sb"] if t else [])))
                ve.wait_ge(*at("A"))
                tt(V, m["Asb"], bank_of("A")[:, 0:256].rearrange("p (c k) -> p c k", c=8),
                   m["r"]["hg_mask"].unsqueeze(1).to_broadcast([P, 8, 32]), ALU.mult, "free:A", "A_sb")
                ve.memset(m["S"][:, 0, :], 0.0).then_inc(*V.up())
                for c in range(7):
                    ve.wait_ge(*at(f"KV:{c}"))
                    wait_own(V)
                    for h in range(HG_H):
                        ve.scalar_tensor_tensor(m["S"][:, c + 1, h * P:(h + 1) * P], m["S"][:, c, h * P:(h + 1) * P],
                                                m["eb"][:, h, 32 * c + 31:32 * c + 32], bank_of(f"KV:{c}")[:, h * P:(h + 1) * P],
                                                ALU.mult, ALU.add) \
                          .then_inc(*V.up(*([f"free:KV:{c}"] if h == 3 else []), *([f"S:{c + 1}"] if h == 3 else [])))
                ve.wait_ge(*at("hoA"))
                ho = m["hoT"]
                for r in range(4):
                    ve.tensor_copy(ho.rearrange("p h (a c k) -> p (h a) c k", a=2, k=32)[:, :, r, :],
                                   bank_of(f"hoA:{r}")[:, 0:256].rearrange("p (g k) -> p g k", k=32)) \
                      .then_inc(*V.up(f"free:hoA:{r}"))
                wait_own(V)
                for i in range(2):
                    ve.wait_ge(*at(f"ho:{i}"))
                    ps = halves(bank_of(f"ho:{i}"))[:, :, 32:T]
                    tt(V, ho[:, 2 * i:2 * i + 2, 32:T], ho[:, 2 * i:2 * i + 2, 32:T], ps, ALU.add, f"free:ho:{i}",
                       *(["ho"] if i else []))
                for i in range(2):
                    ve.wait_ge(*at(f"hrt:{i}"))
                    wait_own(V)
                    ve.reciprocal(m["t2"], m["t1"]).then_inc(*V.up(f"hrt_read:{i}"))
                    wait_own(V)
                    tt(V, ho[:, 2 * i:2 * i + 2, :], ho[:, 2 * i:2 * i + 2, :], m["t2"], ALU.mult)
                wait_own(V)
                ve.wait_ge(*at("hg_silu"))
                ve.scalar_tensor_tensor(ho, ho, m["v"]["hg_norm"], m["hgs"], ALU.mult, ALU.mult).then_inc(*V.up("hoT"))
                gated(2, V, m, "br_a", "br_b", "siga2", "sigp2")
                residual(2, "out2", V, mod_cols(2, 2))

            def peer():
                m, V = A[2], sig[2, "ffn", "vector"]
                norm("f2", V, m, xT[:, :, :], hT, amps[2][:, 1, :], mod_cols(2, 3))
                sc, v8, i8, keep = m["sc"], m["v16"], m["i16"], m["cut"]
                for i in range(8):
                    ve.wait_ge(*at(f"ps_sb:{i}"))
                    for j in range(2):
                        for t in range(TT):
                            k = 2 * i + j
                            s = sc[:, t, k, :]
                            ve.max(v8[:, t, k, 0:8], s).then_inc(*V.up())
                            wait_own(V)
                            ve.max_index(i8[:, t, k, 0:8], v8[:, t, k, 0:8], s).then_inc(*V.up())
                            ve.match_replace(keep, v8[:, t, k, 0:8], s, SENTINEL).then_inc(*V.up())
                            wait_own(V)
                            ve.max(v8[:, t, k, 8:16], keep).then_inc(*V.up())
                            wait_own(V)
                            ve.max_index(i8[:, t, k, 8:16], v8[:, t, k, 8:16], keep).then_inc(*V.up())
                wait_own(V)
                for t in range(TT):
                    ve.tensor_copy(m["idx"][:, t, :, :].rearrange("p q (h a) -> p q h a", h=8),
                                   i8[:, t, :, :].rearrange("p (h q) a -> p q h a", q=2)) \
                      .then_inc(*V.up(*(["idx"] if t else [])))
                for t in range(TT):
                    for h in range(PE_H):
                        a = v8[:, t, 2 * h, :].unsqueeze(2).to_broadcast([P, 16, 16])
                        b = v8[:, t, 2 * h + 1, :].unsqueeze(1).to_broadcast([P, 16, 16])
                        tt(V, m["pgate"][:, t, h * 256:(h + 1) * 256].rearrange("p (a b) -> p a b", a=16), a, b, ALU.add)
                wait_own(V)
                for t in range(TT):
                    for h in range(PE_H):
                        cand = m["pgate"][:, t, h * 256:(h + 1) * 256]
                        cut = m["sel"][:, t, h * 256:(h + 1) * 256]
                        w8 = m["w8"][:, t, h, :]
                        ve.max(w8, cand).then_inc(*V.up())
                        wait_own(V)
                        ve.match_replace(cut, w8, cand, SENTINEL).then_inc(*V.up())
                        wait_own(V)
                        ve.max(m["w8b"], cut).then_inc(*V.up())
                        wait_own(V)
                        ve.match_replace(m["cut2"], m["w8b"], cut, SENTINEL).then_inc(*V.up())
                        wait_own(V)
                        ts(V, cut, m["cut2"], -1e38, None, ALU.is_le, None)
                    wait_own(V)
                    cand = m["pgate"][:, t, :].rearrange("p (h k) -> p h k", h=8)
                    tt(V, cand, cand, m["w8"][:, t, :, 0:1].to_broadcast([P, 8, 256]), ALU.subtract, f"cand:{t}")
                    ve.wait_ge(*at(f"cand_exp:{t}"))
                    picked = m["sel"][:, t, :].rearrange("p (h k) -> p h k", h=8)
                    tt(V, picked, cand, picked, ALU.mult)
                    wait_own(V)
                    ve.tensor_reduce(m["zs"][:, 0, :], picked, AX_X, ALU.add).then_inc(*V.up())
                    wait_own(V)
                    ve.reciprocal(m["zs"][:, 1, :], m["zs"][:, 0, :]).then_inc(*V.up())
                    wait_own(V)
                    for h in range(PE_H):
                        ts(V, m["pgate"][:, t, :].rearrange("p (a h b) -> p a h b", a=16, h=8)[:, :, h, :],
                           picked[:, h, :].rearrange("p (a b) -> p a b", a=16), m["zs"][:, 1, h:h + 1], None,
                           ALU.mult, None, *([f"pgate:{t}"] if h == PE_H - 1 else []))
                if 3 in stages:
                    modulation(3, V, A[3])
                ve.wait_ge(*at("idxT"))
                ve.tensor_copy(m["idxT"], bank_of("idxT").rearrange("p (q t) -> p q t", q=2)) \
                  .then_inc(*V.up("free:idxT", "idxT_sb"))
                ve.wait_ge(spilled, 16)
                for t in range(TT):
                    for i in range(4):
                        ve.wait_ge(*at(f"gT{t}:{i}"))
                        ve.tensor_copy(m["gT"][:, 4 * i:4 * i + 4, :], bank_of(f"gT{t}:{i}").rearrange("p (a k) -> p a k", a=4)) \
                          .then_inc(*V.up(f"free:gT{t}:{i}", *([f"gT_sb{t}"] if i == 3 else [])))
                    wait_own(V)

                    def onehot(q, place, at0):
                        ve.tensor_tensor(place, m["v"]["iota"].unsqueeze(1).to_broadcast([P, CHUNK, PE_N]),
                                         m["idxT"][:, q, bass.ds(at0 + t * P, CHUNK)].unsqueeze(2)
                                         .to_broadcast([P, CHUNK, PE_N]), ALU.is_equal).then_inc(tok_v[t], 1)

                    for s in range(2):
                        onehot(1, m["oh2"][s], CHUNK * s)
                        onehot(0, m["oh1"][s], CHUNK * s)
                    with ve.Fori(1, P // CHUNK // 2) as i:
                        for s in range(2):
                            ve.wait_ge(tok_e[t], i * 4 + (2 * s - 3))
                            onehot(1, m["oh2"][s], i * (2 * CHUNK) + CHUNK * s)
                            ve.wait_ge(tok_e[t], i * 4 + (2 * s - 1))
                            onehot(0, m["oh1"][s], i * (2 * CHUNK) + CHUNK * s)
                    ve.wait_ge(tok_e[t], 2 * P // CHUNK)
                    ve.wait_ge(tok_v[t], 2 * P // CHUNK)
                ve.memset(m["zero"], 0.0).then_inc(*V.up("zero"))
                ve.wait_ge(tok_s[1], 2 * P // CHUNK)
                G = m["G"]

                def u_low(s):
                    slot = (first_piece["peer"] + s) % SLOTS
                    ve.tensor_tensor(ring_parts[:, slot, 0:D], ring[:, slot, 0:D], m["u_high"][:, s % 2, :].bitcast(F32), ALU.subtract) \
                      .then_inc(blk_ul, 1)

                ve.wait_ge(*at("zeroed"))
                ve.tensor_copy(h_high[:, :, :], hT[:, :, :]).then_inc(*V.up())
                wait_own(V)
                tt(V, m["h_low"], hT[:, :, :], h_high[:, :, :].bitcast(F32), ALU.subtract, "h_parts")
                ve.wait_ge(blk_uh, 1)
                u_low(0)

                def weight(s, n):
                    ve.tensor_tensor(m["wt"][:, s % 2, :], m["ge"][:, s % 2, :],
                                     G[:, :, bass.ds(n, 1)].rearrange("p t a -> p (t a)"), ALU.mult).then_inc(blk_v, 1)

                def block(s, n, last=False):
                    if not last:
                        ve.wait_ge(blk_uh, n + 2)
                        u_low(s + 1)
                    ve.wait_ge(blk_s, n + 1)
                    ve.wait_ge(blk_a, n + 1)
                    weight(s, n)
                    wt, high, low = m["wt"][:, s % 2, :], m["wt_high"][:, s % 2, :], m["wt_low"][:, s % 2, :]
                    ve.wait_ge(blk_v, n + 1)
                    ve.tensor_copy(high, wt).then_inc(blk_w, 1)
                    ve.wait_ge(blk_w, n * 3 + 1)
                    ve.tensor_tensor(low, wt, high.bitcast(F32), ALU.subtract).then_inc(blk_w, 1)
                    slot = (first_piece["peer"] + s) % SLOTS
                    ve.wait_ge(blk_h, n + 1)
                    ve.tensor_tensor(ring_parts[:, slot, D:2 * D], ring[:, slot, D:2 * D], m["v_high"][:, s % 2, :].bitcast(F32), ALU.subtract) \
                      .then_inc(blk_w, 1)

                with ve.Fori(0, PE_N // 4 - 1) as i:
                    for s in range(4):
                        block(s, i * 4 + s)
                for s in range(4):
                    block(s, PE_N - 4 + s, s == 3)
                ve.wait_ge(blk_w, 3 * PE_N)
                ve.wait_ge(*at("peer_y"))
                ve.wait_ge(restored, 16)
                residual_sum(2, "peer_y", V, mod_cols(2, 5))
                norm("o2", V, m, xT[:, :, :], xT, m["v"]["g_final"], None)

            def mix3():
                m, V = A[3], sig[3, "mix", "vector"]
                ve.wait_ge(tables_in[3], 16)
                if 2 not in stages:
                    modulation(3, V, m)
                norm("x3", V, m, xT[:, :, :], hT, amps[3][:, 0, :], mod_cols(3, 0))
                for i in range(2):
                    ve.wait_ge(*at(f"v3:{i}"))
                    ve.tensor_copy(m["v_x"][:, :, i * 256:(i + 1) * 256],
                                   bank_of(f"v3:{i}").rearrange("p (t o) -> p t o", t=TT)) \
                      .then_inc(*V.up(f"free:v3:{i}", *(["v3_sb"] if i else [])))
                ve.memset(m["cx"][:, :, 0:2], 0.0).then_inc(*V.up())
                ve.memset(m["up"][:, :, :, 0:2].rearrange("p a b c -> p (a b) c"), 0.0).then_inc(*V.up())
                attention(3, 16, V, m)
                for i in range(2):
                    ve.wait_ge(*at(f"ucb3:{2 + i}"))
                    ve.wait_ge(*at(f"ug:{i}"))
                    tt(V, m["cx"][:, 2 * i:2 * i + 2, 2:T + 2], halves(bank_of(f"ucb3:{2 + i}")),
                       m["ug"][:, 2 * i:2 * i + 2, :], ALU.mult, f"free:ucb3:{2 + i}")
                wait_own(V)
                w = m["v"]["conv_w"]
                for c in range(4):
                    ts(V, m["cv"][:, c, :], m["cx"][:, c, 0:T], w[:, c:c + 1], m["v"]["conv_b"][:, c:c + 1], ALU.mult, ALU.add)
                for k in (1, 2):
                    wait_own(V)
                    for c in range(4):
                        ve.scalar_tensor_tensor(m["cv"][:, c, :], m["cx"][:, c, k:k + T], w[:, 4 * k + c:4 * k + c + 1],
                                                m["cv"][:, c, :], ALU.mult, ALU.add).then_inc(*V.up())
                wait_own(V)
                for i in range(2):
                    ve.wait_ge(*at(f"ucb3:{4 + i}"))
                    tt(V, m["cv"][:, 2 * i:2 * i + 2, :], halves(bank_of(f"ucb3:{4 + i}")), m["cv"][:, 2 * i:2 * i + 2, :],
                       ALU.mult, f"free:ucb3:{4 + i}", *(["cv"] if i else []))
                norm("attn3", V, m, m["oT"], m["mixed"][:, 0:4, :], m["v"]["g_attn"], None, 4, m["ug"])
                wait_own(V)
                norm("conv3", V, m, m["cv"], m["mixed"][:, 4:8, :], m["v"]["g_conv"], None, 4, m["bg"])
                residual(3, "out3", V, mod_cols(3, 2))

            def ffn3():
                m, V = A[3], sig[3, "ffn", "vector"]
                norm("f3", V, m, xT[:, :, :], hT, amps[3][:, 1, :], mod_cols(3, 3))
                fw, fb = m["v"]["f_w"], m["v"]["f_b"]
                for i in range(FFC):
                    ve.wait_ge(*at(f"up_sb:{i}"))
                    y = m["ffa"]
                    wait_own(V)
                    src = m["up"][:, i % 4, :, :]
                    for j in range(2):
                        ch = j * FFC + i
                        ts(V, y[:, j, :], src[:, j, 0:T], fw[:, ch:ch + 1], fb[:, ch:ch + 1], ALU.mult, ALU.add)
                    for k in (1, 2):
                        wait_own(V)
                        for j in range(2):
                            ch = k * 2 * FFC + j * FFC + i
                            if k == 2 and j == 0 and i >= 2:
                                ve.wait_ge(*at(f"act:{i - 2}"))
                            dst = y if k == 1 else m["ffc"][:, i % 2, :, :]
                            ve.scalar_tensor_tensor(dst[:, j, :], src[:, j, k:k + T], fw[:, ch:ch + 1], y[:, j, :],
                                                    ALU.mult, ALU.add) \
                              .then_inc(*V.up(*([f"conv:{i}"] if k == 2 and j else [])))
                    if i >= 1:
                        act(i - 1, V, m)
                act(FFC - 1, V, m)
                ve.wait_ge(*at("ffn_y"))
                residual_sum(3, "ffn_y", V, mod_cols(3, 5))
                norm("o3", V, m, xT[:, :, :], xT, m["v"]["g_final"], None)

            def act(i, V, m):
                ve.wait_ge(*at(f"silu:{i}"))
                tt(V, m["act"][:, i, :], m["ffs"][:, i % 2, :], m["ffc"][:, i % 2, 0, :], ALU.mult, f"act:{i}")

            ve.memset(ones[:, :], 1.0).then_inc(*ones_set.up("ones"))
            ve.wait_ge(x_in, 48)
            if 1 in stages:
                mix1()
                moe()
            if 2 in stages:
                mix2()
                peer()
            if 3 in stages:
                mix3()
                ffn3()

        @block.scalar
        def _(sc):
            def act(A_, out_, in_, func, *names, **kw):
                sc.activation(out_, in_, func, **kw).then_inc(*A_.up(*names))

            def modulation(s, A_, m):
                n = 2 if s == 1 else 1
                for k in range(12):
                    sc.wait_ge(*at(f"mod{s}:{k}"))
                    if k >= 2:
                        sc.wait_ge(*at(f"mod_turned{s}:{k - 2}"))
                    act(A_, m["mod_row"][k % 2][0:n, :], bank_of(f"mod{s}:{k}")[0:n, :], ACT.Copy, f"mod_row{s}:{k}",
                        f"free:mod{s}:{k}")

            def root(tag, A_, m, src, chunks, sq=None, wait=None):
                if wait:
                    sc.wait_ge(*at(wait))
                act(A_, (m["sq"] if sq is None else sq)[:, 0:chunks, :], src, ACT.Square, f"sq:{tag}")
                sc.wait_ge(*at(f"ms:{tag}"))
                act(A_, m["rt"], bank_of(f"ms:{tag}")[:, 0:T], ACT.Sqrt, f"rt:{tag}", f"free:ms:{tag}",
                    scale=1.0 / (chunks * P), bias=m["v"]["eps"])

            def evict(A_, tag, i, dst, func, bias=None, *names):
                sc.wait_ge(*at(f"{tag}:{i}"))
                ps = bank_of(f"{tag}:{i}")
                if bias is None:
                    act(A_, dst, ps.rearrange("p (j t) -> p j t", j=2), func, f"free:{tag}:{i}", *names)
                    return
                for j in range(2):
                    act(A_, dst[:, j, :], ps[:, j * T:(j + 1) * T], func, *([f"free:{tag}:{i}", *names] if j else []),
                        bias=bias[:, j:j + 1])

            def exponentials(s, u, A_, m):
                qt = u % 2
                nk = P * (qt + 1)
                c = m["sm"][:, u % 3, :]
                ps = bank_of(f"S{s}:{u}")
                sc.wait_ge(*at(f"max{s}:{u}"))
                if u >= 3:
                    sc.wait_ge(*at(f"T{s}:{u - 3}"))
                p = m["probs"][:, u % 3, :]
                if s == 1:
                    act(A_, c[:, 6:7], m["v"]["sink"][:, u // 2:u // 2 + 1], ACT.Exp, bias=c[:, 2:3])
                    act(A_, p, ps, ACT.Exp, f"free:S{s}:{u}", f"exp{s}:{u}", bias=c[:, 2:3], scale=SCALE,
                        accum_out=c[:, 4:5])
                if s == 2:
                    for b in range(2):
                        act(A_, p[:, b * nk:(b + 1) * nk], ps[:, b * nk:(b + 1) * nk], ACT.Exp,
                            *([f"free:S{s}:{u}", f"exp{s}:{u}"] if b else []), bias=c[:, 2 + b:3 + b], scale=SCALE,
                            accum_out=c[:, 4 + b:5 + b])
                if s == 3:
                    act(A_, p[:, 0:nk], m["ssb"][:, u % 3, 0:nk], ACT.Exp, f"exp{s}:{u}", bias=c[:, 2:3], scale=SCALE,
                        accum_out=c[:, 4:5])

            def attention(s, units, A_, m):
                for i in range(units + 2):
                    if i < units:
                        exponentials(s, i, A_, m)
                    k = i - 2
                    if 0 <= k < units:
                        n = P * (4 if s == 1 else (2 * (k % 2 + 1) if s == 2 else k % 2 + 1))
                        sc.wait_ge(*at(f"T{s}:{k}"))
                        if k >= 2:
                            sc.wait_ge(*at(f"O{s}:{k - 2}"))
                        act(A_, m["probsT"][:, k % 2, 0:n], bank_of(f"T{s}:{k}")[:, 0:n], ACT.Copy, f"PT{s}:{k}",
                            f"free:T{s}:{k}")

            def mix1():
                m, A_ = A[1], sig[1, "mix", "scalar"]
                root("x1", A_, m, xT[:, :, :], DC)
                modulation(1, A_, m)
                sc.wait_ge(tables_in[1], 32)
                root("ctx", A_, m, m["ctxT"], DC, wait="h:x1")
                for tag, dst in (("k1x", "kraw"), ("k1c", "kcT")):
                    sc.wait_ge(*at(tag))
                    for j in range(2):
                        act(A_, m[dst][:, j, :], bank_of(tag)[:, j * T:(j + 1) * T], ACT.Identity,
                            *([f"free:{tag}"] if j else []), *(["raw:k1"] if j and tag == "k1x" else []),
                            bias=m["v"]["b_k"][:, j:j + 1])
                for i in range(4):
                    evict(A_, "q1", i, m["qraw"][:, 2 * i:2 * i + 2, :], ACT.Identity, m["v"]["b_q"][:, 2 * i:2 * i + 2],
                          f"raw:q1:{i}")
                attention(1, 32, A_, m)
                for tag, dst in (("ga", "siga"), ("gp", "sigp")):
                    for i in range(4):
                        evict(A_, tag, i, m[dst][:, 2 * i:2 * i + 2, :], ACT.Sigmoid,
                              m["v"]["b_" + tag][:, 2 * i:2 * i + 2], f"{dst}1:{i}")

            def narrow(m):
                A_ = signal("narrow_scalar")
                for k in range(E_N // 2):
                    sc.wait_ge(*at(f"leave:{k}"))
                    act(A_, m["leave"][0:SEATS, 1 + 2 * k:3 + 2 * k, :],
                        bank_of(f"leave:{k}")[0:SEATS, :].rearrange("p (j t) -> p j t", j=2), ACT.Copy,
                        f"free:leave:{k}")

                def gathered(n, h):
                    sc.activation(m["xe"][:, n, 4 * h:4 * h + 4, :],
                                  psum[:, 6 + h, 0:4 * SEATS].rearrange("p (c k) -> p c k", c=4),
                                  ACT.Copy).then_inc(nar_s, 1)

                sc.wait_ge(nar_e, 1)
                for h in range(2):
                    gathered(0, h)
                for h in range(2):
                    sc.activation(m["y_e"][0:SEATS, h * 512:(h + 1) * 512], m["rows"][0:SEATS, 0:512], ACT.Copy,
                                  scale=0.0).then_inc(nar_s, 1)
                base = first_piece["moe"]
                with sc.Fori(0, E_N) as e:
                    for j in range(8):
                        sc.wait_ge(nar_v, e * 40 + (5 * j + 1))
                        sc.activation(m["sg"][:, 0:SEATS], m["g"][:, 0:SEATS], ACT.Sigmoid, scale=1.702) \
                          .then_inc(nar_s, 1)
                        if j == 1:
                            sc.wait_ge(nar_e, e + 2)
                            for h in range(2):
                                gathered(bass.ds((e + 1) % 2, 1), h)
                    sc.wait_ge(used.sem, e * 12 + (base + 12))
                    for h in range(2):
                        sc.activation(m["y_e"][0:SEATS, h * 512:(h + 1) * 512], psum[0:SEATS, 6 + h, :],
                                      ACT.Copy).then_inc(nar_s, 1)

            def wide(m):
                A_ = signal("wide_scalar")
                for i in range(E_N // 2):
                    evict(A_, "gb", i, m["gb"][:, 2 * i:2 * i + 2, :], ACT.Copy, None, *(["gb_sb"] if i == 15 else []))
                with sc.Fori(0, E_N) as e:
                    for j in range(8):
                        sc.wait_ge(moe_v, e * 40 + (5 * j + 1))
                        sc.activation(m["sg"], m["g"], ACT.Sigmoid, scale=1.702).then_inc(moe_s, 1)

            def moe():
                m, A_ = A[1], sig[1, "ffn", "scalar"]
                root("f1", A_, m, xT[:, :, :], DC, wait="x_mixed1")
                sc.wait_ge(*at("top_n"))
                for t in range(TT):
                    act(A_, m["top_e"][:, t, :], m["top"][:, t, 0:4], ACT.Exp, *(["top_exp"] if t else []),
                        bias=m["top_n"][:, t:t + 1], accum_out=m["top_s"][:, t:t + 1])
                if 2 in stages:
                    modulation(2, A_, m)
                for i in range(4):
                    sc.wait_ge(*at(f"x_nat:{i}"))
                    act(A_, m["x_nat"][:, i // 2, (i % 2) * 512:(i % 2 + 1) * 512], bank_of(f"x_nat:{i}"), ACT.Copy,
                        f"free:x_nat:{i}", *(["x_nat_sb"] if i == 3 else []))
                sc.wait_ge(*at("flag_set"))
                crowded = sc.value_load(m["flag"][0:1, :])
                with sc.If(crowded == 0):
                    narrow(m)
                with sc.Else():
                    wide(m)
                root("o1", A_, m, xT[:, :, :], DC, wait="x_out1")

            def mix2():
                m, A_ = A[2], sig[2, "mix", "scalar"]
                if 1 not in stages:
                    modulation(2, A_, m)
                root("x2", A_, m, xT[:, :, :], DC, wait="h:o1" if 1 in stages else None)
                for i in range(2):
                    evict(A_, "q2", i, m["qraw"][:, 2 * i:2 * i + 2, :], ACT.Copy, None, f"raw:q2:{i}")
                sc.wait_ge(*at("gl"))
                act(A_, m["gl"], bank_of("gl")[:, 0:TT * 24].rearrange("p (t k) -> p t k", t=TT), ACT.Sigmoid, "free:gl",
                    "gl_sb")
                for kv in range(2):
                    sc.wait_ge(*at(f"hid:{kv}"))
                    for g in range(2):
                        act(A_, m["hid_rows"][0:16, kv, g * P:(g + 1) * P], bank_of(f"hid:{kv}:{g}")[0:16, 0:P], ACT.Copy,
                            f"free:hid:{kv}:{g}", *([f"hid_rows:{kv}"] if g else []))
                sc.wait_ge(*at("hidT"))
                hid = bank_of("hidT")[:, 0:64].rearrange("p (i n) -> p i n", i=4)
                for i in range(4):
                    act(A_, m["hbias"][:, i, :], hid[:, i, CMP:CMP + 1], ACT.Copy)
                sc.wait_ge(*A_.now())
                for i in range(4):
                    act(A_, m["hid"][:, i, 0:CMP], hid[:, i, 0:CMP], ACT.Gelu_apprx_tanh,
                        *(["free:hidT", "hidden"] if i == 3 else []), bias=m["hbias"][:, i, :])
                sc.wait_ge(*at("pc_raw"))
                act(A_, m["pc"][:, :, 0:CMP], m["pc"][:, :, 0:CMP], ACT.Exp, "pc_exp")
                attention(2, 16, A_, m)
                for i in range(2):
                    evict(A_, "hq", i, m["qg"][:, 2 * i:2 * i + 2, :], ACT.Silu)
                for i in range(2):
                    evict(A_, "hf", i, m["kg"][:, 2 * i:2 * i + 2, :], ACT.Sigmoid, None, *(["hf:sig"] if i else []))
                sc.wait_ge(*at("lb_diff"))
                act(A_, small[:, 128:132], small[:, 136:140], ACT.Sigmoid, "lb")
                sc.wait_ge(*at("fg"))
                act(A_, m["eb"], m["fg"], ACT.Ln, "logf")
                sc.wait_ge(*at("bcum"))
                act(A_, m["eb"], m["bcum"], ACT.Exp, "eb")
                act(A_, m["fg"], m["bcum"], ACT.Exp, "einv", scale=-1.0)
                act(A_, m["kendT"], m["kendT"], ACT.Exp, "eend")
                sc.wait_ge(*at("hg_ready"))
                for i in range(2):
                    evict(A_, "hg", i, m["hgs"][:, 2 * i:2 * i + 2, :], ACT.Silu, None, *(["hg_silu"] if i else []))
                sc.wait_ge(*at("ho"))
                act(A_, m["eb"], m["hoT"], ACT.Square, "ho_sq")
                for i in range(2):
                    sc.wait_ge(*at(f"hms:{i}"))
                    if i:
                        sc.wait_ge(*at("hrt_read:0"))
                    act(A_, m["t1"], bank_of(f"hms:{i}").rearrange("p (j t) -> p j t", j=2), ACT.Sqrt, f"hrt:{i}",
                        f"free:hms:{i}", scale=1.0 / P, bias=m["v"]["eps"])
                sc.wait_ge(*at("kend"))
                for i in range(8):
                    dst = m["siga"] if i < 4 else m["sigp"]
                    k = 2 * (i % 4)
                    evict(A_, "merge", i, dst[:, k:k + 2, :], ACT.Sigmoid, None, f"sig{'a' if i < 4 else 'p'}2:{i % 4}")

            def peer():
                m, A_ = A[2], sig[2, "ffn", "scalar"]
                root("f2", A_, m, xT[:, :, :], DC, wait="x_mixed2")
                for i in range(8):
                    evict(A_, "peer_q", i, m["pqT"][:, 2 * i:2 * i + 2, :], ACT.Copy, None, f"pq_sb:{i}")
                for i in range(8):
                    sc.wait_ge(*at(f"ps:{i}"))
                    act(A_, m["sc"][:, :, 2 * i:2 * i + 2, :].rearrange("p t j k -> p j t k"),
                        bank_of(f"ps:{i}").rearrange("p (j t k) -> p j t k", j=2, t=TT), ACT.Copy, f"free:ps:{i}",
                        f"ps_sb:{i}")
                if 3 in stages:
                    modulation(3, A_, m)
                for t in range(TT):
                    sc.wait_ge(*at(f"cand:{t}"))
                    act(A_, m["pgate"][:, t, :], m["pgate"][:, t, :], ACT.Exp, f"cand_exp:{t}")
                for t in range(TT):
                    G = m["G"].rearrange("p t k -> p (t k)")

                    def copy_r(s):
                        sc.copy(m["rr"][s].rearrange("p k n -> p (k n)"), psum[:, s, :]).then_inc(tok_s[t], 1)

                    def copy_g(s, at0):
                        sc.copy(G[:, bass.ds(at0 + t * (P * PE_N), CHUNK * PE_N)], psum[:, 2 + s, :]).then_inc(tok_s[t], 1)

                    sc.wait_ge(tok_e[t], 1)
                    copy_r(0)
                    sc.wait_ge(tok_e[t], 2)
                    copy_r(1)
                    sc.wait_ge(tok_e[t], 3)
                    copy_g(0, 0)
                    with sc.Fori(1, P // CHUNK // 2) as i:
                        for s in range(2):
                            sc.wait_ge(tok_e[t], i * 4 + 2 * s)
                            copy_r(s)
                            sc.wait_ge(tok_e[t], i * 4 + (2 * s + 1))
                            copy_g(1 - s, i * (2 * CHUNK * PE_N) + (s - 1) * CHUNK * PE_N)
                    sc.wait_ge(tok_e[t], 2 * P // CHUNK)
                    copy_g(1, (P - CHUNK) * PE_N)
                    marks[f"free:G{t}"] = (f"peer_copies_{t}", 2 * P // CHUNK)

                def gelu(s):
                    sc.activation(m["ge"][:, s % 2, :], psum[:, 4 + s, 0:T], ACT.Gelu_apprx_tanh).then_inc(blk_s, 1)
                    sc.activation(m["v_high"][:, s % 2, :], ring[:, (first_piece["peer"] + s) % SLOTS, D:2 * D],
                                  ACT.Copy).then_inc(blk_h, 1)

                base = first_piece["peer"]

                def u_high(s):
                    sc.activation(m["u_high"][:, s % 2, :], ring[:, (base + s) % SLOTS, 0:D], ACT.Copy) \
                      .then_inc(blk_uh, 1)

                def landed(s):
                    return ring_full[(base + s) % SLOTS], 16 * ((base + s) // SLOTS + 1)

                sc.wait_ge(*landed(0))
                u_high(0)
                for s in range(4):
                    sc.wait_ge(*landed(s + 1))
                    if s >= 1:
                        sc.wait_ge(blk_a, s)
                    u_high(s + 1)
                    sc.wait_ge(blk_a, s + 1)
                    if s >= 2:
                        sc.wait_ge(blk_v, s - 1)
                    gelu(s)
                with sc.Fori(1, PE_N // 4 - 1) as i:
                    for s in range(4):
                        full, count = landed(s + 1)
                        sc.wait_ge(full, i * 16 + count)
                        sc.wait_ge(blk_a, i * 4 + s)
                        u_high(s + 1)
                        sc.wait_ge(blk_a, i * 4 + s + 1)
                        sc.wait_ge(blk_v, i * 4 + (s - 1))
                        gelu(s)
                for s in range(4):
                    n = PE_N - 4 + s
                    if s < 3:
                        sc.wait_ge(*landed(n + 1))
                        sc.wait_ge(blk_a, n)
                        u_high(s + 1)
                    sc.wait_ge(blk_a, n + 1)
                    sc.wait_ge(blk_v, n - 1)
                    gelu(s)
                root("o2", A_, m, xT[:, :, :], DC, wait="x_out2")

            def mix3():
                m, A_ = A[3], sig[3, "mix", "scalar"]
                if 2 not in stages:
                    modulation(3, A_, m)
                root("x3", A_, m, xT[:, :, :], DC, wait="h:o2" if 2 in stages else None)
                for i in range(4):
                    evict(A_, "qk3", i, m["qk"][:, 2 * i:2 * i + 2, :], ACT.Copy, None, *(["qk3_sb"] if i == 3 else []))
                attention(3, 16, A_, m)
                for i in range(2):
                    evict(A_, "ucb3", i, m["ug"][:, 2 * i:2 * i + 2, :], ACT.Copy, None, f"ug:{i}")
                root("attn3", A_, m, m["oT"], 4, wait="oT3")
                sc.wait_ge(*at("cv"))
                act(A_, m["sq"][:, 4:8, :], m["cv"], ACT.Square, "sq:conv3")
                sc.wait_ge(*at("h:attn3"))
                sc.wait_ge(*at("ms:conv3"))
                act(A_, m["rt"], bank_of("ms:conv3")[:, 0:T], ACT.Sqrt, "rt:conv3", "free:ms:conv3",
                    scale=1.0 / A3, bias=m["v"]["eps"])

            def ffn3():
                m, A_ = A[3], sig[3, "ffn", "scalar"]
                root("f3", A_, m, xT[:, :, :], DC, wait="x_mixed3")

                def silu(i):
                    sc.wait_ge(*at(f"conv:{i}"))
                    if i >= 2:
                        sc.wait_ge(*at(f"act:{i - 2}"))
                    act(A_, m["ffs"][:, i % 2, :], m["ffc"][:, i % 2, 1, :], ACT.Silu, f"silu:{i}")

                for i in range(FFC):
                    if i >= 4:
                        sc.wait_ge(*at(f"conv:{i - 4}"))
                    evict(A_, "up", i, m["up"][:, i % 4, :, 2:T + 2], ACT.Copy, None, f"up_sb:{i}")
                    if i >= 1:
                        silu(i - 1)
                silu(FFC - 1)
                root("o3", A_, m, xT[:, :, :], DC, wait="x_out3")

            sc.wait_ge(x_in, 48)
            for s in stages:
                src = A[s]["v"]["c"].rearrange("p (c n) -> p c n", c=DC)
                act(silu_of_c, A[s]["csil"], src, ACT.Silu, f"csil{s}")
            if 1 in stages:
                mix1()
                moe()
            if 2 in stages:
                mix2()
                peer()
            if 3 in stages:
                mix3()
                ffn3()

        @block.gpsimd
        def _(gp):
            gp.dma_start(xT[:, :, :], dram["x"]).then_inc(x_in, 16)
            gp.dma_start(vec[:, :], dram["vec"]).then_inc(x_in, 16)
            gp.dma_start(ident[:, :], dram["ident"]).then_inc(x_in, 16)
            if 1 in stages:
                m = A[1]
                gp.dma_start(m["rows"], dram["rows1"]).then_inc(tables_in[1], 16)
                gp.dma_start(m["ctxT"], dram["ctx"]).then_inc(tables_in[1], 16)
                gp.wait_ge(*at("x_mixed1"))
                gp.dma_start(m["moe_tables"], dram["moe"]).then_inc(moe_in, 16)
            if 2 in stages:
                m = A[2]
                if 1 in stages:
                    gp.wait_ge(*at("h:o1"))
                gp.dma_start(m["rows"], dram["rows2"]).then_inc(tables_in[2], 16)
                gp.wait_ge(*at("x_mixed2"))
                gp.dma_start(dram["spill"], xT[:, :, :]).then_inc(spilled, 16)
                for t in range(TT):
                    def block(s, at0):
                        gp.tensor_tensor(m["bd"][s].rearrange("p k (h a) -> p k h a", h=8),
                                         m["gT"][:, :, bass.ds(at0, CHUNK)].rearrange("p a k -> p k a").unsqueeze(2)
                                         .to_broadcast([P, CHUNK, 8, 16]),
                                         m["v"]["head_mask"].unsqueeze(1).unsqueeze(3).to_broadcast([P, CHUNK, 8, 16]),
                                         ALU.mult).then_inc(tok_p[t], 1)

                    gp.wait_ge(*at(f"gT_sb{t}"))
                    for s in range(2):
                        block(s, CHUNK * s)
                    with gp.Fori(1, P // CHUNK // 2) as i:
                        for s in range(2):
                            gp.wait_ge(tok_e[t], i * 4 + (2 * s - 3))
                            block(s, i * (2 * CHUNK) + CHUNK * s)
                gp.wait_ge(tok_p[1], P // CHUNK)
                gp.wait_ge(spilled, 16)
                gp.wait_ge(*at("peer_y"))
                gp.dma_start(xT[:, :, :], dram["spill"]).then_inc(restored, 16)
            if 3 in stages:
                m = A[3]
                if 2 in stages:
                    gp.wait_ge(*at("h:o2"))
                gp.dma_start(m["rows"], dram["rows3"]).then_inc(tables_in[3], 16)
            gp.wait_ge(*at(f"h:o{stages[-1]}"))
            gp.dma_start(dram["out"], xT[:, :, :]).then_inc(stored, 16)
            gp.wait_ge(stored, 16)
        return marks


def shapes(stages):
    _, n = piece_table(stages)
    got = {"stream": (n, P, SLOT), "x": (P, DC, T), "vec": (P, sum(V_LEN[s] for s in stages)), "ident": (P, P)}
    if 1 in stages:
        got["ctx"] = (P, DC, T)
        got["moe"] = (P, sum(k for _, k in MOE_IN))
    for s in stages:
        got[f"rows{s}"] = (P, R_LEN[s])
    return got


def program(new_core, stages):
    known = {}
    for _ in range(2):
        nc = new_core()
        dram = {n: nc.dram_tensor("in_" + n, s, F32, kind="ExternalInput").ap() for n, s in shapes(stages).items()}
        dram["spill"] = nc.dram_tensor("x_spill", (P, DC, T), F32).ap()
        dram["out"] = nc.dram_tensor("out_x", (P, DC, T), F32, kind="ExternalOutput").ap()
        known = build(nc, stages, dram, known)
    return nc


def chan(v):
    return np.ascontiguousarray(v).reshape(-1, P).T


def by_columns(w, step=256):
    k, n = w.shape
    return w.reshape(k // P, P, n // step, step).transpose(2, 1, 0, 3).reshape(n // step, P, -1)


def by_rows(w, rows=2):
    k, n = w.shape
    return w.reshape(k // (rows * P), rows, P, n).transpose(0, 2, 1, 3).reshape(k // (rows * P), P, -1)


def turned(x):
    return np.ascontiguousarray(x.T.reshape(-1, P, x.shape[0]).transpose(1, 0, 2))


def everywhere(v):
    return np.broadcast_to(np.asarray(v).reshape(1, -1), (P, np.asarray(v).size))


def rope_tables(angle, half):
    rot = np.zeros((P, P), np.float32)
    for p in range(P):
        if p % (2 * half) < half:
            rot[p + half, p] = -1.0
        else:
            rot[p - half, p] = 1.0
    return np.cos(angle).astype(np.float32), np.sin(angle).astype(np.float32), rot


def layout1(a):
    D_, W = D, {}
    w_in, b_in = a["w_in"][0], a["b_in"][0]
    order = [(2 * (t // 4) + half) * 4 + t % 4 for t in range(8) for half in range(2)]
    perm = np.concatenate([np.arange(h * HD, (h + 1) * HD) for h in order])
    cut = [0, 1024, 1280, 1536, 2560, 3584, 4608]
    parts = [slice(cut[i], cut[i + 1]) for i in range(6)]
    t = np.arange(T)
    i, j = np.arange(P)[:, None], np.arange(P)[None, :]
    pool = np.zeros((T, 4, T), np.float32)
    for g, w in enumerate((2, 4, 8, 16)):
        for k in range(T):
            lo, hi = max(k - w // 2, 0), min(k + w // 2, T)
            pool[lo:hi, g, k] = np.float32(1.0) / np.float32(hi - lo)
            pool[k, g, k] -= 1.0
    pool = pool.reshape(TT, P, 4, T).transpose(1, 0, 2, 3).reshape(1, P, -1)
    gu, dn = a["w_gu"][0], a["w_down"][0]
    gu = gu.reshape(E_N, DC, P, 2, 8, P).transpose(0, 4, 2, 1, 3, 5).reshape(E_N, 8, P, SLOT)
    dn = dn.reshape(E_N, 4, 2, P, D_).transpose(0, 1, 3, 2, 4).reshape(E_N, 4, P, SLOT)
    W["stream"] = [by_columns(a["w_ada"][0]), by_columns(w_in[:, parts[1]]), by_columns(w_in[:, parts[2]]),
                   by_columns(w_in[:, parts[0]][:, perm]), by_columns(w_in[:, parts[3]]), pool,
                   a["w_pool"][0].reshape(4, 2, P, 256).transpose(2, 0, 1, 3).reshape(1, P, -1),
                   by_columns(w_in[:, parts[4]]), by_columns(w_in[:, parts[5]]),
                   by_columns(a["w_attn_br"][0][perm]), by_columns(a["w_pool_br"][0]), by_columns(a["w_out"][0]),
                   np.concatenate([gu, dn], 1).reshape(12 * E_N, P, SLOT)]
    c2 = np.stack([chan(a["c"][0]), chan(a["c_ctx"])], 2).reshape(P, -1)
    W["vec"] = [c2, chan(a["b_ada"][0]), chan(a["norm1_g"][0]), chan(a["norm2_g"][0]), chan(b_in[parts[0]][perm]),
                chan(b_in[parts[1]]), chan(b_in[parts[4]]), chan(b_in[parts[5]]), chan(a["pool_scale"][0]),
                chan(a["final_g"]), np.full((P, 1), 1e-5, np.float32), everywhere(a["attn_sink"][0][order])]
    p = np.arange(P)
    inv = np.float32(10000.0) ** (-np.arange(16, dtype=np.float32) / np.float32(16))
    pos = np.where((p[:, None] % 64) // 32 == 0, t[None, :] // 64, t[None, :] % 64).astype(np.float32)
    cos, sin, rot = rope_tables(pos * inv[p % 16][:, None], 16)
    mask = np.concatenate([np.where(j <= i, 0, MASKED), np.where(j >= i, 0, MASKED)], 1).astype(np.float32)
    W["rows"] = [cos, sin, rot, mask, everywhere(b_in[parts[2]]), everywhere(b_in[parts[3]]),
                 everywhere(a["b_router"][0]), everywhere(np.arange(32, dtype=np.float32)),
                 everywhere(np.arange(1, SEATS + 1, dtype=np.float32)),
                 a["w_router"][0].reshape(DC, P, 32).transpose(1, 0, 2).reshape(P, -1)]
    bd = np.zeros((P, D_), np.float32)
    bd[:E_N] = a["b_down"][0]
    bgu = a["b_gu"][0].reshape(E_N * 16, P).T
    W["moe"] = np.concatenate([bgu, bd], 1)
    W["ctx"] = turned(a["ctx"][0])
    return W


def layout2(a):
    W = {}
    w_in = a["w_in_2"][0]
    names = ["q", "kc", "vc", "ks", "vs", "kw", "vw", "gl", "hq", "hf", "hi", "hg", "merge"]
    widths = [512, 128, 128, 128, 128, 128, 128, 24, 512, 512, 512, 512, 2048]
    at = dict(zip(names, np.cumsum([0] + widths[:-1])))
    col = {n: w_in[:, at[n]:at[n] + w] for n, w in zip(names, widths)}
    perm = np.concatenate([np.arange(h * HD, (h + 1) * HD) for t in range(4) for h in (t, 4 + t)])

    def both(*n):
        return by_columns(np.concatenate([col[k] for k in n], 1))

    def compress(w):
        w = w.reshape(32, HD, P).transpose(1, 0, 2)
        w = np.concatenate([w, w], 0)
        return w.reshape(P, 2, 16 * P).transpose(1, 0, 2)

    def branch(w):
        return by_columns(w, 512)

    keys = a["peer_sub_keys_2"][0].transpose(3, 1, 0, 2).reshape(1, P, -1)
    u = a["peer_u_2"][0].reshape(PE_N, PE_N, DC, P).transpose(0, 3, 2, 1).reshape(PE_N, P, D)
    v = a["peer_v_2"][0].reshape(PE_N, PE_N, D)
    W["stream"] = [by_columns(a["w_ada_2"][0]), both("kc", "vc"), both("ks", "vs"), both("kw", "vw"),
                   by_columns(col["q"][:, perm]), compress(a["w_ck1_2"][0]), compress(a["w_cv1_2"][0]),
                   both("hq"), both("hf"), both("hi"), both("hg"), both("merge"),
                   branch(a["w_branch_2"][0, 0][perm]), branch(a["w_branch_2"][0, 1]), by_columns(a["w_out_2"][0]),
                   by_columns(a["w_peer_q_2"][0]), keys, np.concatenate([u, v], 2)]

    def pos(w):
        w = w.T
        return np.concatenate([w, w], 0)

    head_mask = np.zeros((P, PE_H), np.float32)
    head_mask[np.arange(P), np.arange(P) // 16] = 1.0
    lb = a["hgrn_lb_logits_2"]
    W["vec"] = [chan(a["c_2"][0]), chan(a["b_ada_2"][0]), chan(a["g_mix_2"][0]), chan(a["g_ffn_2"][0]),
                chan(a["g_final_2"]), np.full((P, 1), 1e-6, np.float32), chan(lb[0]), chan(lb[1]),
                chan(a["hgrn_out_norm_2"][0]), pos(a["cmp_pos_k_2"][0]), pos(a["cmp_pos_v_2"][0]),
                everywhere(np.arange(PE_N, dtype=np.float32)), head_mask]
    p, t = np.arange(P), np.arange(T)
    inv = np.float32(10000.0) ** (-np.arange(32, dtype=np.float32) / np.float32(32))
    cos, sin, rot = rope_tables(t.astype(np.float32)[None, :] * inv[p % 32][:, None], 32)
    i, j = np.arange(P)[:, None], np.arange(P)[None, :]
    end = np.arange(16) * 16 + 31
    cmp_mask = np.where(end[None, None, :] <= (i[:, :, None] + P * np.arange(2)[None, :, None]), 0, MASKED)
    reset = np.broadcast_to((t % HG_C != 0).astype(np.float32)[None, :], (P, T))
    hg_mask = np.arange(32)[None, :] >= (p % 32)[:, None]
    w_gl = col["gl"].reshape(DC, P, 24).transpose(1, 0, 2).reshape(P, -1)
    W["rows"] = [cos, sin, rot, np.where(j <= i, 0, MASKED).astype(np.float32),
                 cmp_mask.astype(np.float32).reshape(P, -1), reset, hg_mask.astype(np.float32), w_gl,
                 a["w_ck2_2"][0], a["w_cv2_2"][0]]
    return W


def layout3(a):
    W = {}
    w_in = a["w_in_3"][0]
    up = a["w_up_3"][0].reshape(DC, P, 2, FFC, P).transpose(3, 1, 0, 2, 4).reshape(FFC, P, SLOT)
    W["stream"] = [by_columns(a["w_ada_3"][0]), by_columns(w_in[:, 0:1024]), by_columns(w_in[:, 1024:1536]),
                   by_columns(w_in[:, 1536:3072]), by_columns(a["w_out_3"][0]), up, by_rows(a["w_down_3"][0])]

    def taps(w):
        return np.concatenate([chan(w[k]) for k in range(3)], 1)

    W["vec"] = [chan(a["c_3"][0]), chan(a["b_ada_3"][0]), chan(a["g_mix_3"][0]), chan(a["g_ffn_3"][0]),
                chan(a["g_final_3"]), np.full((P, 1), 1e-6, np.float32), taps(a["conv_w_3"][0]),
                chan(a["conv_b_3"][0]), chan(a["g_attn_out_3"][0]), chan(a["g_conv_out_3"][0]),
                taps(a["ffn_conv_w_3"][0]), chan(a["ffn_conv_b_3"][0])]
    i, j = np.arange(P)[:, None], np.arange(T)[None, :]
    first = np.where(j[:, :P] <= i, j[:, :P] - i, MASKED)
    second = np.where(j <= i + P, j - i - P, MASKED)
    W["rows"] = [first.astype(np.float32), second.astype(np.float32)]
    return W


def arrays(a, stages):
    W = {s: {1: layout1, 2: layout2, 3: layout3}[s](a) for s in stages}
    got = {"in_stream": np.concatenate(ahead({s: W[s]["stream"] for s in stages}, stages), 0),
           "in_x": turned(a["x"][0]), "in_vec": np.concatenate([v for s in stages for v in W[s]["vec"]], 1),
           "in_ident": np.eye(P, dtype=np.float32)}
    if 1 in stages:
        got["in_ctx"], got["in_moe"] = W[1]["ctx"], W[1]["moe"]
    for s in stages:
        got[f"in_rows{s}"] = np.concatenate(W[s]["rows"], 1)
    return {k: np.ascontiguousarray(v) for k, v in got.items()}


STAGES = (1, 2, 3)


def kernel(**inputs):
    from concourse import bacc
    from concourse.bass_utils import run_bass_kernel_spmd

    nc = program(lambda: bacc.Bacc("TRN2", target_bir_lowering=False, num_devices=1), STAGES)
    r = run_bass_kernel_spmd(nc, [arrays(inputs, STAGES)], core_ids=[0])
    out = r.results[0]["out_x"]
    return np.ascontiguousarray(out.transpose(2, 1, 0).reshape(1, T, D))
```
